# Optimizing a Trainium2 kernel written in Bass

```python
import math
import jax, jax.numpy as jnp
from jax import lax
import numpy as np

'''Hybrid decoder block: parallel Mamba-2 SSD and differential-attention branches
merged by per-channel sigmoid gates (Griffin-style), then a PEER product-key expert
channel mixer. All sub-layers are pre-RMSNorm, adaLN-modulated by a per-sequence
conditioning vector c, and merged into the residual stream with plain adds.

Inputs:  x (BATCH, SEQ, D_MODEL) f32, c (BATCH, D_MODEL) f32,
         positions (BATCH, SEQ) int32, plus learned parameters (leading DEPTH axis).
Output:  (BATCH, SEQ, D_MODEL) after the final RMSNorm.
'''

D_MODEL = 1024
BATCH = 1
SEQ = 1024
DEPTH = 1

SSD_EXPAND = 2
D_INNER = SSD_EXPAND * D_MODEL
SSD_HEAD_DIM = 64
SSD_HEADS = D_INNER // SSD_HEAD_DIM
SSD_GROUPS = 8
SSD_STATE = 128
CONV_K = 4
CONV_CH = D_INNER + 2 * SSD_GROUPS * SSD_STATE
CHUNK = 128
ATTN_HEADS = 8
ATTN_HEAD_DIM = D_MODEL // (2 * ATTN_HEADS)
ATTN_QK = ATTN_HEADS * 2 * ATTN_HEAD_DIM
ATTN_V = ATTN_HEADS * 2 * ATTN_HEAD_DIM
Q_BLOCK = 128
NUM_BUCKETS = 32
MAX_DISTANCE = 128
PEER_HEADS = 8
N_KEYS = 128
N_EXPERTS = N_KEYS * N_KEYS
PEER_DK = 128
PEER_TOPK = 16
TOKEN_BLOCK = 128
OFF_Z = 0
OFF_XBC = OFF_Z + D_INNER
OFF_DT = OFF_XBC + CONV_CH
OFF_Q = OFF_DT + SSD_HEADS
OFF_K = OFF_Q + ATTN_QK
OFF_V = OFF_K + ATTN_QK
OFF_GS = OFF_V + ATTN_V
OFF_GA = OFF_GS + D_MODEL
IN_COLS = OFF_GA + D_MODEL
EPS = 1e-6

kernel_name = 'hybrid_ssd_diffattn_peer_block'

def _rms(x):
    xf = x.astype(jnp.float32)
    return xf * lax.rsqrt(jnp.mean(xf * xf, axis=-1, keepdims=True) + EPS)

def rmsnorm(x, w):
    return (_rms(x) * w.astype(jnp.float32)).astype(x.dtype)

def t5_bucket(rel):
    n = jnp.maximum(-rel, 0)
    max_exact = NUM_BUCKETS // 2
    nf = jnp.maximum(n, 1).astype(jnp.float32)
    large = max_exact + (jnp.log(nf / max_exact) / math.log(MAX_DISTANCE / max_exact)
                         * (NUM_BUCKETS - max_exact)).astype(jnp.int32)
    large = jnp.minimum(large, NUM_BUCKETS - 1)
    return jnp.where(n < max_exact, n, large)

def causal_dwconv(u, w, bias):
    ch = u.shape[-1]
    y = lax.conv_general_dilated(u, w[:, None, :], window_strides=(1,),
                                 padding=[(CONV_K - 1, 0)],
                                 dimension_numbers=('NWC', 'WIO', 'NWC'),
                                 feature_group_count=ch)
    return y + bias

def ssd_scan(xh, dt, a, bm, cm):
    b, s, h, p = xh.shape
    g, n = bm.shape[2], bm.shape[3]
    r = h // g
    nc = s // CHUNK
    f32 = jnp.float32
    x = xh.reshape(b, nc, CHUNK, g, r, p).astype(f32)
    dtc = dt.reshape(b, nc, CHUNK, g, r)
    bc = bm.reshape(b, nc, CHUNK, g, n).astype(f32)
    cc = cm.reshape(b, nc, CHUNK, g, n).astype(f32)
    a_cum = jnp.cumsum(dtc * a.reshape(g, r), axis=2)
    causal = jnp.tril(jnp.ones((CHUNK, CHUNK), dtype=bool))
    seg = a_cum[:, :, :, None] - a_cum[:, :, None, :]
    decay = jnp.exp(jnp.where(causal[:, :, None, None], seg, -jnp.inf))
    cb = jnp.einsum('bclgn,bcsgn->bclsg', cc, bc)
    wts = cb[..., None] * decay * dtc[:, :, None]
    y_diag = jnp.einsum('bclsgr,bcsgrp->bclgrp', wts, x)
    to_end = jnp.exp(a_cum[:, :, -1:] - a_cum) * dtc
    states = jnp.einsum('bclgn,bclgr,bclgrp->bcgrpn', bc, to_end, x)
    chunk_decay = jnp.exp(a_cum[:, :, -1])

    def step(carry, inp):
        st, dec = inp
        return carry * dec[..., None, None] + st, carry

    init = jnp.zeros((b, g, r, p, n), f32)
    _, prev = lax.scan(step, init, (jnp.moveaxis(states, 1, 0), jnp.moveaxis(chunk_decay, 1, 0)))
    prev = jnp.moveaxis(prev, 0, 1)
    y_off = jnp.einsum('bclgn,bcgrpn,bclgr->bclgrp', cc, prev, jnp.exp(a_cum))
    return (y_diag + y_off).reshape(b, s, h, p).astype(xh.dtype)

def diff_attention(q, k, v, positions, bias_table, lam):
    b, s, h, _, d = q.shape
    nblk = s // Q_BLOCK
    qb = jnp.moveaxis(q.reshape(b, nblk, Q_BLOCK, h, 2, d), 1, 0)
    pb = jnp.moveaxis(positions.reshape(b, nblk, Q_BLOCK), 1, 0)
    kidx = jnp.arange(s)
    scale = d ** -0.5

    def block(args):
        qi, pi, bi = args
        qidx = bi * Q_BLOCK + jnp.arange(Q_BLOCK)
        logits = jnp.einsum('bqhid,bkhid->bhiqk', qi, k).astype(jnp.float32) * scale
        rel = positions[:, None, :] - pi[:, :, None]
        bias = bias_table[t5_bucket(rel)].astype(jnp.float32)
        logits = logits + jnp.transpose(bias, (0, 3, 1, 2))[:, :, None]
        mask = kidx[None, :] <= qidx[:, None]
        logits = jnp.where(mask, logits, -jnp.inf)
        pr = jax.nn.softmax(logits, axis=-1)
        attn = pr[:, :, 0] - lam * pr[:, :, 1]
        return jnp.einsum('bhqk,bkhv->bqhv', attn.astype(v.dtype), v)

    out = lax.map(block, (qb, pb, jnp.arange(nblk)))
    return jnp.moveaxis(out, 0, 1).reshape(b, s, h, -1)

def peer(xn, wq, key1, key2, u, v):
    b, s, dm = xn.shape
    toks = xn.reshape(-1, TOKEN_BLOCK, dm)
    half = PEER_DK // 2

    def block(xt):
        q = (xt @ wq).reshape(TOKEN_BLOCK, PEER_HEADS, 2, half).astype(jnp.float32)
        s1 = jnp.einsum('thd,hkd->thk', q[:, :, 0], key1.astype(jnp.float32))
        s2 = jnp.einsum('thd,hkd->thk', q[:, :, 1], key2.astype(jnp.float32))
        v1, i1 = lax.top_k(s1, PEER_TOPK)
        v2, i2 = lax.top_k(s2, PEER_TOPK)
        comb = (v1[..., :, None] + v2[..., None, :]).reshape(TOKEN_BLOCK, PEER_HEADS, PEER_TOPK * PEER_TOPK)
        sc, pos = lax.top_k(comb, PEER_TOPK)
        e1 = jnp.take_along_axis(i1, pos // PEER_TOPK, axis=-1)
        e2 = jnp.take_along_axis(i2, pos % PEER_TOPK, axis=-1)
        experts = e1 * N_KEYS + e2
        gate = jax.nn.softmax(sc, axis=-1)
        ue = u[experts]
        act = jax.nn.gelu(jnp.einsum('thkd,td->thk', ue, xt).astype(jnp.float32), approximate=False) * gate
        return jnp.einsum('thk,thkd->td', act.astype(xt.dtype), v[experts])

    return lax.map(block, toks).reshape(b, s, dm)

def setup_inputs(seed: int = 0) -> dict:
    key = jax.random.key(seed)
    ks = jax.random.split(key, 32)
    L = DEPTH
    f32 = jnp.float32

    def nrm(k, shape, std):
        return jax.random.normal(k, shape, f32) * std

    x = nrm(ks[0], (BATCH, SEQ, D_MODEL), 1.0)
    c = nrm(ks[1], (BATCH, D_MODEL), 1.0)
    positions = (jax.random.randint(ks[2], (BATCH, 1), 0, 1024, dtype=jnp.int32)
                 + jnp.arange(SEQ, dtype=jnp.int32)[None, :])
    ada_w = nrm(ks[3], (L, D_MODEL, 6 * D_MODEL), 0.02)
    ada_b = nrm(ks[4], (L, 6 * D_MODEL), 0.01)
    norm1_w = 1.0 + nrm(ks[5], (L, D_MODEL), 0.02)
    norm2_w = 1.0 + nrm(ks[6], (L, D_MODEL), 0.02)
    final_norm_w = 1.0 + nrm(ks[7], (D_MODEL,), 0.02)
    w_in = nrm(ks[8], (L, D_MODEL, IN_COLS), D_MODEL ** -0.5)
    conv_w = nrm(ks[9], (L, CONV_K, CONV_CH), CONV_K ** -0.5)
    conv_b = nrm(ks[10], (L, CONV_CH), 0.02)
    dt0 = jnp.exp(jax.random.uniform(ks[11], (L, SSD_HEADS), f32, math.log(1e-3), math.log(1e-1)))
    dt_bias = dt0 + jnp.log(-jnp.expm1(-dt0))
    a_log = jnp.log(jax.random.uniform(ks[12], (L, SSD_HEADS), f32, 1.0, 16.0))
    d_skip = 1.0 + nrm(ks[13], (L, SSD_HEADS), 0.02)
    ssd_norm_w = 1.0 + nrm(ks[14], (L, D_INNER), 0.02)
    w_ssd_o = nrm(ks[15], (L, D_INNER, D_MODEL), D_INNER ** -0.5)
    lambda_q1 = nrm(ks[16], (L, ATTN_HEAD_DIM), 0.1)
    lambda_k1 = nrm(ks[17], (L, ATTN_HEAD_DIM), 0.1)
    lambda_q2 = nrm(ks[18], (L, ATTN_HEAD_DIM), 0.1)
    lambda_k2 = nrm(ks[19], (L, ATTN_HEAD_DIM), 0.1)
    attn_norm_w = 1.0 + nrm(ks[20], (L, 2 * ATTN_HEAD_DIM), 0.02)
    w_attn_o = nrm(ks[21], (L, ATTN_V, D_MODEL), ATTN_V ** -0.5)
    rel_bias = nrm(ks[22], (NUM_BUCKETS, ATTN_HEADS), 0.5)
    w_out = nrm(ks[23], (L, D_MODEL, D_MODEL), D_MODEL ** -0.5)
    peer_wq = nrm(ks[24], (L, D_MODEL, PEER_HEADS * PEER_DK), D_MODEL ** -0.5)
    peer_key1 = nrm(ks[25], (L, PEER_HEADS, N_KEYS, PEER_DK // 2), (PEER_DK // 2) ** -0.5)
    peer_key2 = nrm(ks[26], (L, PEER_HEADS, N_KEYS, PEER_DK // 2), (PEER_DK // 2) ** -0.5)
    peer_u = nrm(ks[27], (L, N_EXPERTS, D_MODEL), D_MODEL ** -0.5)
    peer_v = nrm(ks[28], (L, N_EXPERTS, D_MODEL), 0.3)
    return {'x': x, 'c': c, 'positions': positions, 'ada_w': ada_w, 'ada_b': ada_b,
            'norm1_w': norm1_w, 'norm2_w': norm2_w, 'final_norm_w': final_norm_w,
            'w_in': w_in, 'conv_w': conv_w, 'conv_b': conv_b, 'dt_bias': dt_bias,
            'a_log': a_log, 'd_skip': d_skip, 'ssd_norm_w': ssd_norm_w, 'w_ssd_o': w_ssd_o,
            'lambda_q1': lambda_q1, 'lambda_k1': lambda_k1, 'lambda_q2': lambda_q2,
            'lambda_k2': lambda_k2, 'attn_norm_w': attn_norm_w, 'w_attn_o': w_attn_o,
            'rel_bias': rel_bias, 'w_out': w_out, 'peer_wq': peer_wq,
            'peer_key1': peer_key1, 'peer_key2': peer_key2, 'peer_u': peer_u, 'peer_v': peer_v}

def reference(x, c, positions, ada_w, ada_b, norm1_w, norm2_w, final_norm_w,
              w_in, conv_w, conv_b, dt_bias, a_log, d_skip, ssd_norm_w, w_ssd_o,
              lambda_q1, lambda_k1, lambda_q2, lambda_k2, attn_norm_w, w_attn_o,
              rel_bias, w_out, peer_wq, peer_key1, peer_key2, peer_u, peer_v):
    b, s, _ = x.shape
    f32 = jnp.float32
    h = x
    for l in range(DEPTH):
        lambda_init = 0.8 - 0.6 * math.exp(-0.3 * l)
        ada = jax.nn.silu(c) @ ada_w[l] + ada_b[l]
        sh1, sc1, g1, sh2, sc2, g2 = [m[:, None, :] for m in jnp.split(ada, 6, axis=-1)]

        n1 = rmsnorm(h, norm1_w[l]) * (1.0 + sc1) + sh1
        proj = n1 @ w_in[l]

        z = proj[..., OFF_Z:OFF_XBC]
        xbc = jax.nn.silu(causal_dwconv(proj[..., OFF_XBC:OFF_DT], conv_w[l], conv_b[l]))
        xs = xbc[..., :D_INNER].reshape(b, s, SSD_HEADS, SSD_HEAD_DIM)
        bm = xbc[..., D_INNER:D_INNER + SSD_GROUPS * SSD_STATE].reshape(b, s, SSD_GROUPS, SSD_STATE)
        cm = xbc[..., D_INNER + SSD_GROUPS * SSD_STATE:].reshape(b, s, SSD_GROUPS, SSD_STATE)
        dt = jax.nn.softplus(proj[..., OFF_DT:OFF_Q].astype(f32) + dt_bias[l].astype(f32))
        a = -jnp.exp(a_log[l].astype(f32))
        y = ssd_scan(xs, dt, a, bm, cm) + d_skip[l][:, None] * xs
        yz = (y.reshape(b, s, D_INNER) * jax.nn.silu(z)).reshape(b, s, SSD_GROUPS, D_INNER // SSD_GROUPS)
        y_ssd = (_rms(yz).reshape(b, s, D_INNER) * ssd_norm_w[l]).astype(x.dtype)
        y_ssd = y_ssd @ w_ssd_o[l]

        q = proj[..., OFF_Q:OFF_K].reshape(b, s, ATTN_HEADS, 2, ATTN_HEAD_DIM)
        k = proj[..., OFF_K:OFF_V].reshape(b, s, ATTN_HEADS, 2, ATTN_HEAD_DIM)
        v = proj[..., OFF_V:OFF_GS].reshape(b, s, ATTN_HEADS, 2 * ATTN_HEAD_DIM)
        lam = (jnp.exp(jnp.sum(lambda_q1[l].astype(f32) * lambda_k1[l].astype(f32)))
               - jnp.exp(jnp.sum(lambda_q2[l].astype(f32) * lambda_k2[l].astype(f32)))
               + lambda_init)
        att = diff_attention(q, k, v, positions, rel_bias, lam)
        att = rmsnorm(att, attn_norm_w[l]) * (1.0 - lambda_init)
        y_att = att.reshape(b, s, ATTN_V) @ w_attn_o[l]

        gate_s = jax.nn.sigmoid(proj[..., OFF_GS:OFF_GA])
        gate_a = jax.nn.sigmoid(proj[..., OFF_GA:IN_COLS])
        mix = (gate_s * y_ssd + gate_a * y_att) @ w_out[l]
        h = h + g1 * mix

        n2 = rmsnorm(h, norm2_w[l]) * (1.0 + sc2) + sh2
        h = h + g2 * peer(n2, peer_wq[l], peer_key1[l], peer_key2[l], peer_u[l], peer_v[l])
    return rmsnorm(h, final_norm_w)


_drawn_inputs = setup_inputs


def setup_inputs(seed=0):
    import zlib

    import numpy as np

    out = dict(_drawn_inputs(seed))
    spreads = {}
    factors = {'ada_b': 4.434,
     'norm1_w': 6.187,
     'norm2_w': 37.103,
     'final_norm_w': 25.587,
     'conv_b': 22.998,
     'd_skip': 200.0,
     'ssd_norm_w': 82.455,
     'lambda_q1': 3.47,
     'lambda_q2': 4.495,
     'lambda_k2': 3.665,
     'attn_norm_w': 106.765}
    for name, (base, spread) in spreads.items():
        noise = np.random.default_rng([zlib.crc32(name.encode()), seed]).standard_normal(out[name].shape)
        drawn = base * np.exp(spread * noise) if base else spread * noise
        out[name] = __import__('jax').numpy.asarray(drawn.astype(out[name].dtype))
    for name, factor in factors.items():
        out[name] = (out[name] * factor).astype(out[name].dtype)
    return out
```

```python
import math
from contextlib import ExitStack

import numpy as np

import concourse.bass as bass
from concourse import mybir

F32 = mybir.dt.float32
I32 = mybir.dt.int32
U32 = mybir.dt.uint32
BF16 = mybir.dt.bfloat16
ALU = mybir.AluOpType
ACT = mybir.ActivationFunctionType
AX = mybir.AxisListType

P = 128
S = 1024
D = 1024
TT = S // P
KD = D // P
HALF = 512
DI = 2048
SH = 32
G = 8
HPG = SH // G
HD = DI // SH
GW = DI // G
CONV_TILES = 32
AH = 8
NB = 32
PH = 8
NK = 128
TOPK = 16
EPS = 1e-6
HEAD_SCALE = 64 ** -0.5
LAMBDA_INIT = 0.8 - 0.6 * math.exp(-0.3 * 0)
FINFO_MIN = -3.0e38


class Steps:

    def __init__(self, eng, sem, base=0):
        self.eng, self.sem, self.base, self.n = eng, sem, base, 0

    def of(self, ins):
        ins.then_inc(self.sem, 1)
        self.n += 1

    def wait(self):
        self.eng.wait_ge(self.sem, self.base + self.n)


class Space:

    def __init__(self, nc, stack, stage):
        self.nc, self.stack, self.stage = nc, stack, stage
        self.sems = []
        stack.callback(self.clear)

    def clear(self):
        if self.sems:
            self.nc.clear_and_free_semaphores(self.sems)
            self.nc.all_engine_barrier()

    def sb(self, name, shape, dt=F32):
        return self.stack.enter_context(self.nc.sbuf_tensor(f"{self.stage}_{name}", shape, dt))

    def ps(self, name, shape, dt=F32):
        return self.stack.enter_context(self.nc.psum_tensor(f"{self.stage}_{name}", shape, dt))

    def sem(self, name):
        self.sems.append(self.nc.alloc_semaphore(f"{self.stage}_{name}"))
        return self.sems[-1]


def stage_modulation(nc, d):
    with ExitStack() as stack:
        sp = Space(nc, stack, "mod")
        cT = sp.sb("cT", [P, KD])
        silu_c = sp.sb("silu_c", [P, KD])
        w = [sp.sb(f"w{s}", [P, KD, HALF]) for s in range(2)]
        ada_b = sp.sb("ada_b", [1, 6 * D])
        norm_w = sp.sb("norm_w", [1, 2 * D])
        rows = sp.sb("rows", [1, 6 * D])
        acc = [sp.ps(f"acc{s}", [1, HALF]) for s in range(2)]
        small_in = sp.sem("small_in")
        w_in = [sp.sem(f"w_in{s}") for s in range(2)]
        silu_done = sp.sem("silu_done")
        w_used = [sp.sem(f"w_used{s}") for s in range(2)]
        acc_out = [sp.sem(f"acc_out{s}") for s in range(2)]
        dve_step = sp.sem("dve_step")
        rows_out = sp.sem("rows_out")

        with nc.Block() as block:
            @block.sync
            def _(sync):
                sync.dma_start(cT[:], d["cT"]).then_inc(small_in, 16)
                sync.dma_start(ada_b[:], d["ada_b"]).then_inc(small_in, 16)
                sync.dma_start(norm_w[:, 0:D], d["norm1_w"]).then_inc(small_in, 16)
                sync.dma_start(norm_w[:, D:2 * D], d["norm2_w"]).then_inc(small_in, 16)
                for s in range(2):
                    sync.sem_inc(w_used[s], 1)
                with sync.Fori(0, 6) as i:
                    for s in range(2):
                        sync.wait_ge(w_used[s], i + 1)
                        sync.dma_start(w[s][:], d["ada_w"].rearrange("(k p) n -> p k n", p=P)[
                            :, :, bass.ds(i * D + s * HALF, HALF)]).then_inc(w_in[s], 16)
                sync.wait_ge(dve_step, 4)
                sync.wait_ge(acc_out[0], 7)
                sync.wait_ge(acc_out[1], 7)
                sync.dma_start(d["rows"].rearrange("v n -> (v n)").rearrange("(a n) -> a n", a=1),
                               rows[:]).then_inc(rows_out, 16)
                sync.wait_ge(rows_out, 16)

            @block.scalar
            def _(act):
                act.wait_ge(small_in, 64)
                act.activation(silu_c[:], cT[:], ACT.Silu).then_inc(silu_done, 1)

            @block.tensor
            def _(pe):
                pe.wait_ge(silu_done, 1)
                with pe.Fori(0, 6) as i:
                    for s in range(2):
                        pe.wait_ge(w_in[s], i * 16 + 16)
                        pe.wait_ge(acc_out[s], i + 1)
                        for k in range(KD):
                            mm = pe.matmul(acc[s][:], silu_c[:, k:k + 1], w[s][:, k, :], start=(k == 0), stop=(k == KD - 1))
                        mm.then_inc(w_used[s], 1)

            @block.vector
            def _(dve):
                dve.wait_ge(small_in, 64)
                for s in range(2):
                    dve.sem_inc(acc_out[s], 1)
                with dve.Fori(0, 6) as i:
                    for s in range(2):
                        dve.wait_ge(w_used[s], i + 2)
                        part = bass.ds(i * D + s * HALF, HALF)
                        dve.tensor_tensor(rows[:, part], acc[s][:], ada_b[:, part], ALU.add).then_inc(acc_out[s], 1)
                dve.wait_ge(acc_out[0], 7)
                dve.wait_ge(acc_out[1], 7)
                for n, v in enumerate((1, 4)):
                    row = rows[:, v * D:(v + 1) * D]
                    dve.tensor_scalar(row, row, 1.0, math.sqrt(D), ALU.add, ALU.mult).then_inc(dve_step, 1)
                    dve.wait_ge(dve_step, 2 * n + 1)
                    dve.tensor_tensor(row, row, norm_w[:, n * D:(n + 1) * D], ALU.mult).then_inc(dve_step, 1)


def stage_project(nc, d):
    with ExitStack() as stack:
        sp = Space(nc, stack, "proj")
        n1T = sp.sb("n1T", [P, KD, S])
        norm_rows_to_transposed(nc, sp, d, n1T)
        project_channel_major(nc, d, n1T)
        project_token_major(nc, d, n1T)


def norm_rows_to_transposed(nc, outer, d, n1T):
    with ExitStack() as stack:
        sp = Space(nc, stack, "n1")
        ident = sp.sb("ident", [P, P])
        scale_row = sp.sb("scale_row", [P, D])
        shift_row = sp.sb("shift_row", [P, D])
        x = [sp.sb(f"x{s}", [P, D]) for s in range(2)]
        n1 = [sp.sb(f"n1{s}", [P, D]) for s in range(2)]
        squares = sp.sb("squares", [P, D])
        eps = sp.sb("eps", [P, 1])
        ss = [sp.sb(f"ss{s}", [P, 1]) for s in range(2)]
        rstd = [sp.sb(f"rstd{s}", [P, 1]) for s in range(2)]
        turned = [sp.ps(f"turned{s}", [P, KD, P]) for s in range(2)]
        const_in = sp.sem("const_in")
        x_in = [sp.sem(f"x_in{s}") for s in range(2)]
        ss_done = [sp.sem(f"ss_done{s}") for s in range(2)]
        dve_step = sp.sem("dve_step")
        n1_ready = [sp.sem(f"n1_ready{s}") for s in range(2)]
        turned_ready = [sp.sem(f"turned_ready{s}") for s in range(2)]
        turned_out = [sp.sem(f"turned_out{s}") for s in range(2)]
        with nc.Block() as block:
            @block.sync
            def _(sync):
                sync.dma_start(ident[:], d["ident"]).then_inc(const_in, 16)
                sync.dma_start(eps[:], d["eps"][0].rearrange("(p a) -> p a", a=1)).then_inc(const_in, 16)
                sync.dma_start(scale_row[:], d["rows"][1].partition_broadcast(P)).then_inc(const_in, 16)
                sync.dma_start(shift_row[:], d["rows"][0].partition_broadcast(P)).then_inc(const_in, 16)
                for s in range(2):
                    sync.sem_inc(n1_ready[s], 1)
                with sync.Fori(0, TT // 2) as i:
                    for s in range(2):
                        sync.wait_ge(n1_ready[s], i + 1)
                        sync.dma_start(x[s][:], d["x"][bass.ds((2 * i + s) * P, P), :]).then_inc(x_in[s], 16)

            @block.scalar
            def _(act):
                act.wait_ge(const_in, 64)
                for s in range(2):
                    act.sem_inc(turned_out[s], 1)
                with act.Fori(0, TT // 2) as i:
                    for s in range(2):
                        act.wait_ge(x_in[s], i * 16 + 16)
                        act.wait_ge(n1_ready[s], i + 1)
                        act.activation(squares[:], x[s][:], ACT.Square, accum_out=ss[s][:]).then_inc(ss_done[s], 1)
                        act.wait_ge(ss_done[s], 2 * i + 1)
                        act.activation(ss[s][:], ss[s][:], ACT.Sqrt, bias=eps[:]).then_inc(ss_done[s], 1)
                    for s in range(2):
                        act.wait_ge(turned_ready[s], i + 1)
                        act.activation(n1T[:, :, bass.ds((2 * i + s) * P, P)], turned[s][:], ACT.Copy).then_inc(turned_out[s], 1)

            @block.vector
            def _(dve):
                dve.wait_ge(const_in, 64)
                with dve.Fori(0, TT // 2) as i:
                    for s in range(2):
                        st = Steps(dve, dve_step, i * 4 + 2 * s)
                        dve.wait_ge(ss_done[s], 2 * i + 2)
                        st.of(dve.reciprocal(rstd[s][:], ss[s][:]))
                        dve.wait_ge(turned_out[s], i + 1)
                        st.wait()
                        st.of(dve.scalar_tensor_tensor(n1[s][:], x[s][:], rstd[s][:], scale_row[:], ALU.mult, ALU.mult))
                        st.wait()
                        dve.tensor_tensor(n1[s][:], n1[s][:], shift_row[:], ALU.add).then_inc(n1_ready[s], 1)

            @block.tensor
            def _(pe):
                pe.wait_ge(const_in, 64)
                with pe.Fori(0, TT // 2) as i:
                    for s in range(2):
                        pe.wait_ge(n1_ready[s], i + 2)
                        pe.wait_ge(turned_out[s], i + 1)
                        for k in range(KD):
                            mm = pe.transpose(turned[s][:, k, :], n1[s][:, k * P:(k + 1) * P], ident[:])
                        mm.then_inc(turned_ready[s], 1)


def project_channel_major(nc, d, n1T):
    QK = 2 * AH
    with ExitStack() as stack:
        sp = Space(nc, stack, "pc")
        w = [sp.sb(f"w{s}", [P, KD, P]) for s in range(2)]
        conv_w = sp.sb("conv_w", [P, CONV_TILES, 5])
        u = [sp.sb(f"u{s}", [P, S + 3]) for s in range(2)]
        y = [sp.sb(f"y{s}", [P, S]) for s in range(2)]
        out = [sp.sb(f"out{s}", [P, S]) for s in range(2)]
        acc = [sp.ps(f"acc{s}", [P, S]) for s in range(2)]
        conv_in = sp.sem("conv_in")
        w_in = [sp.sem(f"w_in{s}") for s in range(2)]
        acc_ready = [sp.sem(f"acc_ready{s}") for s in range(2)]
        acc_out = [sp.sem(f"acc_out{s}") for s in range(2)]
        padded = sp.sem("padded")
        dve_step = sp.sem("dve_step")
        y_ready = [sp.sem(f"y_ready{s}") for s in range(2)]
        out_ready = [sp.sem(f"out_ready{s}") for s in range(2)]
        stored = [sp.sem(f"stored{s}") for s in range(2)]
        NQ, NC = QK // 2, CONV_TILES // 2
        with nc.Block() as block:
            @block.gpsimd
            def _(pool):
                pool.dma_start(conv_w[:], d["conv_w"]).then_inc(conv_in, 16)
                with pool.Fori(0, NQ + NC) as i:
                    for s in range(2):
                        pool.wait_ge(acc_ready[s], i + 1)
                        pool.dma_start(w[s][:], d["w_ch"][2 * i + s]).then_inc(w_in[s], 16)

            @block.sync
            def _(sync):
                for s in range(2):
                    sync.sem_inc(stored[s], 16)
                with sync.Fori(0, NQ) as i:
                    for s in range(2):
                        sync.wait_ge(acc_out[s], i + 2)
                        sync.dma_start(d["qkT"][2 * i + s], out[s][:]).then_inc(stored[s], 16)
                with sync.Fori(0, NC) as i:
                    for s in range(2):
                        sync.wait_ge(out_ready[s], i + 2)
                        sync.dma_start(d["xbcT"][2 * i + s], out[s][:]).then_inc(stored[s], 16)
                for s in range(2):
                    sync.wait_ge(stored[s], 16 * (1 + NQ + NC))

            @block.tensor
            def _(pe):
                for s in range(2):
                    pe.sem_inc(acc_ready[s], 1)
                with pe.Fori(0, NQ + NC) as i:
                    for s in range(2):
                        pe.wait_ge(w_in[s], i * 16 + 16)
                        pe.wait_ge(acc_out[s], i + 1)
                        for h in range(2):
                            for k in range(KD):
                                mm = pe.matmul(acc[s][:, h * HALF:(h + 1) * HALF], w[s][:, k, :],
                                               n1T[:, k, h * HALF:(h + 1) * HALF], start=(k == 0), stop=(k == KD - 1))
                        mm.then_inc(acc_ready[s], 1)

            @block.scalar
            def _(act):
                for s in range(2):
                    act.sem_inc(acc_out[s], 1)
                for first, scale in ((0, HEAD_SCALE), (NQ // 2, 1.0)):
                    with act.Fori(first, first + NQ // 2) as i:
                        for s in range(2):
                            act.wait_ge(acc_ready[s], i + 2)
                            act.wait_ge(stored[s], i * 16 + 16)
                            act.activation(out[s][:], acc[s][:], ACT.Copy, scale=scale).then_inc(acc_out[s], 1)
                act.wait_ge(padded, 2)
                for s in range(2):
                    act.wait_ge(acc_ready[s], NQ + 2)
                    act.activation(u[s][:, 3:S + 3], acc[s][:], ACT.Copy).then_inc(acc_out[s], 1)
                with act.Fori(0, NC - 1) as i:
                    for s in range(2):
                        act.wait_ge(y_ready[s], i + 1)
                        act.wait_ge(acc_ready[s], i + NQ + 3)
                        act.activation(u[s][:, 3:S + 3], acc[s][:], ACT.Copy).then_inc(acc_out[s], 1)
                        act.wait_ge(stored[s], i * 16 + NQ * 16 + 16)
                        act.activation(out[s][:], y[s][:], ACT.Silu).then_inc(out_ready[s], 1)
                for s in range(2):
                    act.wait_ge(y_ready[s], NC)
                    act.wait_ge(stored[s], (NC - 1 + NQ + 1) * 16)
                    act.activation(out[s][:], y[s][:], ACT.Silu).then_inc(out_ready[s], 1)

            @block.vector
            def _(dve):
                for s in range(2):
                    dve.sem_inc(out_ready[s], 1)
                for s in range(2):
                    dve.memset(u[s][:, 0:3], 0.0).then_inc(padded, 1)
                dve.wait_ge(conv_in, 16)
                dve.wait_ge(padded, 2)
                with dve.Fori(0, NC) as i:
                    for s in range(2):
                        st = Steps(dve, dve_step, i * 6 + 3 * s)
                        cw = conv_w[:, bass.ds(2 * i + s, 1), :].rearrange("p a b -> p (a b)")
                        dve.wait_ge(acc_out[s], i + NQ + 2)
                        dve.wait_ge(out_ready[s], i + 1)
                        st.of(dve.tensor_scalar(y[s][:], u[s][:, 3:S + 3], cw[:, 3:4], cw[:, 4:5], ALU.mult, ALU.add))
                        for j in range(3):
                            st.wait()
                            tap = dve.scalar_tensor_tensor(y[s][:], u[s][:, j:S + j], cw[:, j:j + 1], y[s][:], ALU.mult, ALU.add)
                            if j < 2:
                                st.of(tap)
                        tap.then_inc(y_ready[s], 1)


def project_token_major(nc, d, n1T):
    with ExitStack() as stack:
        sp = Space(nc, stack, "pt")
        NBUF = 4
        w = [sp.sb(f"w{s}", [P, KD, HALF]) for s in range(2)]
        w_dt = sp.sb("w_dt", [P, KD, SH])
        dt_bias = sp.sb("dt_bias", [P, SH])
        out = [sp.sb(f"out{s}", [P, HALF]) for s in range(NBUF)]
        raw = sp.sb("raw", [P, TT, SH])
        mag = sp.sb("mag", [P, TT, SH])
        dt = sp.sb("dt", [P, TT, SH])
        acc = [sp.ps(f"acc{s}", [P, HALF]) for s in range(NBUF)]
        acc_dt = sp.ps("acc_dt", [P, TT, SH])
        small_in = sp.sem("small_in")
        w_in = [sp.sem(f"w_in{s}") for s in range(2)]
        acc_ready = [sp.sem(f"acc_ready{s}") for s in range(NBUF)]
        out_ready = [sp.sem(f"out_ready{s}") for s in range(NBUF)]
        stored = [sp.sem(f"stored{s}") for s in range(NBUF)]
        dt_ready = sp.sem("dt_ready")
        dt_step = sp.sem("dt_step")
        mag_step = sp.sem("mag_step")
        dt_stored = sp.sem("dt_stored")
        PARTS = [("z", 2, ACT.Silu), ("v", 1, ACT.Copy), ("gate", 2, ACT.Sigmoid)]
        TURNS = sum(n for _, n, _ in PARTS)
        USES = 2 * TT // NBUF
        with nc.Block() as block:
            @block.gpsimd
            def _(pool):
                pool.dma_start(w_dt[:], d["w_dt"].rearrange("(k p) n -> p k n", p=P)).then_inc(small_in, 16)
                pool.dma_start(dt_bias[:], d["dt_bias"].partition_broadcast(P)).then_inc(small_in, 16)
                w_tok = d["w_tok"].rearrange("(k p) n -> p k n", p=P)
                for s in range(2):
                    pool.dma_start(w[s][:], w_tok[:, :, s * HALF:(s + 1) * HALF]).then_inc(w_in[s], 16)
                with pool.Fori(0, TURNS - 1) as i:
                    for s in range(2):
                        pool.wait_ge(acc_ready[(s * TT + TT - 1) % NBUF], i * USES + (s + 1) * TT // NBUF)
                        pool.dma_start(w[s][:], w_tok[:, :, bass.ds((2 * i + 2 + s) * HALF, HALF)]).then_inc(w_in[s], 16)
                pool.wait_ge(dt_step, 3)
                pool.dma_start(d["dt"].rearrange("t p n -> p t n"), dt[:]).then_inc(dt_stored, 16)
                pool.wait_ge(dt_stored, 16)

            @block.tensor
            def _(pe):
                pe.wait_ge(small_in, 32)
                for t in range(TT):
                    for k in range(KD):
                        mm = pe.matmul(acc_dt[:, t, :], n1T[:, k, t * P:(t + 1) * P], w_dt[:, k, :],
                                       start=(k == 0), stop=(k == KD - 1))
                mm.then_inc(dt_ready, 1)
                with pe.Fori(0, TURNS) as i:
                    for s in range(2):
                        pe.wait_ge(w_in[s], i * 16 + 16)
                        for t in range(TT):
                            n = s * TT + t
                            b = n % NBUF
                            pe.wait_ge(out_ready[b], i * USES + n // NBUF + 1)
                            for k in range(KD):
                                mm = pe.matmul(acc[b][:], n1T[:, k, t * P:(t + 1) * P], w[s][:, k, :],
                                               start=(k == 0), stop=(k == KD - 1))
                            mm.then_inc(acc_ready[b], 1)

            @block.scalar
            def _(act):
                for b in range(NBUF):
                    act.sem_inc(out_ready[b], 1)
                first = 0
                for name, turns, func in PARTS:
                    with act.Fori(first, first + turns) as i:
                        for n in range(2 * TT):
                            b = n % NBUF
                            act.wait_ge(acc_ready[b], i * USES + n // NBUF + 1)
                            act.wait_ge(stored[b], (i * USES + n // NBUF + 1) * 16)
                            act.activation(out[b][:], acc[b][:], func).then_inc(out_ready[b], 1)
                    first += turns
                act.wait_ge(dt_step, 1)
                act.activation(mag[:], raw[:], ACT.Abs).then_inc(mag_step, 1)
                act.wait_ge(mag_step, 1)
                act.activation(mag[:], mag[:], ACT.Exp, scale=-1.0).then_inc(mag_step, 1)
                act.wait_ge(mag_step, 2)
                act.activation(mag[:], mag[:], ACT.Ln, bias=1.0).then_inc(mag_step, 1)

            @block.sync
            def _(sync):
                for b in range(NBUF):
                    sync.sem_inc(stored[b], 16)
                first = 0
                for name, turns, func in PARTS:
                    with sync.Fori(first, first + turns) as i:
                        for n in range(2 * TT):
                            b = n % NBUF
                            sync.wait_ge(out_ready[b], i * USES + n // NBUF + 2)
                            sync.dma_start(d[name][n % TT, :, bass.ds((2 * (i - first) + n // TT) * HALF, HALF)],
                                           out[b][:]).then_inc(stored[b], 16)
                    first += turns
                for b in range(NBUF):
                    sync.wait_ge(stored[b], (TURNS * USES + 1) * 16)

            @block.vector
            def _(dve):
                dve.wait_ge(small_in, 32)
                dve.wait_ge(dt_ready, 1)
                dve.tensor_tensor(raw[:], acc_dt[:], dt_bias[:].unsqueeze(1).to_broadcast([P, TT, SH]), ALU.add).then_inc(dt_step, 1)
                dve.wait_ge(mag_step, 1)
                dve.tensor_scalar(raw[:], raw[:], 0.0, None, ALU.max).then_inc(dt_step, 1)
                dve.wait_ge(dt_step, 2)
                dve.wait_ge(mag_step, 3)
                dve.tensor_tensor(dt[:], raw[:], mag[:], ALU.add).then_inc(dt_step, 1)


def bucket_starts(max_distance=128):
    exact = NB // 2
    return [b if b <= exact else math.ceil(exact * (max_distance / exact) ** ((b - exact) / (NB - exact)))
            for b in range(NB)]


def stage_rel_bias(nc, d):
    QG = 4
    QB = 16
    NJ = QB // QG
    with ExitStack() as stack:
        sp = Space(nc, stack, "rb")
        pos_k_int = sp.sb("pos_k_int", [P, S], I32)
        pos_q_int = sp.sb("pos_q_int", [P, S // QG], I32)
        pos_k = sp.sb("pos_k", [P, S])
        limit = sp.sb("limit", [P, S // QG])
        first = sp.sb("first", [P, 1])
        table = sp.sb("table", [P, AH])
        before = sp.sb("before", [P, AH])
        diffs = sp.sb("diffs", [P, NJ, P])
        steps = [sp.sb(f"steps{s}", [P, NJ, S]) for s in range(2)]
        out = [sp.sb(f"out{s}", [P, S]) for s in range(2)]
        acc = [sp.ps(f"acc{s}", [P, S]) for s in range(2)]
        zeroed = sp.sem("zeroed")
        small_in = sp.sem("small_in")
        dve_step = sp.sem("dve_step")
        steps_ready = [sp.sem(f"steps_ready{s}") for s in range(2)]
        acc_ready = [sp.sem(f"acc_ready{s}") for s in range(2)]
        out_ready = [sp.sem(f"out_ready{s}") for s in range(2)]
        stored = [sp.sem(f"stored{s}") for s in range(2)]
        N = P // QB // 2
        with nc.Block() as block:
            @block.sync
            def _(sync):
                sync.dma_start(pos_k_int[:], d["pos"].partition_broadcast(P)).then_inc(small_in, 16)
                sync.dma_start(first[:], d["first"].rearrange("(p a) -> p a", a=1)).then_inc(small_in, 16)
                sync.wait_ge(zeroed, 2)
                for i in range(QG):
                    sync.dma_start(pos_q_int[i * NB:(i + 1) * NB, :], d["pos_q"][i].partition_broadcast(NB)).then_inc(small_in, 16)
                    sync.dma_start(table[i * NB:(i + 1) * NB, :], d["rel_bias"]).then_inc(small_in, 16)
                    sync.dma_start(before[i * NB + 1:(i + 1) * NB, :], d["rel_bias"][0:NB - 1, :]).then_inc(small_in, 16)
                for s in range(2):
                    sync.sem_inc(stored[s], 16)
                for qt in range(TT):
                    with sync.Fori(qt * N, qt * N + N) as i:
                        for s in range(2):
                            sync.wait_ge(out_ready[s], i + 2)
                            sync.dma_start(d["bias"].rearrange("q h k -> (q h) k")[bass.ds((2 * i + s) * P, P), 0:(qt + 1) * P],
                                           out[s][:, 0:(qt + 1) * P]).then_inc(stored[s], 16)
                for s in range(2):
                    sync.wait_ge(stored[s], (TT * N + 1) * 16)

            @block.vector
            def _(dve):
                dve.memset(before[:], 0.0).then_inc(zeroed, 1)
                dve.memset(diffs[:], 0.0).then_inc(zeroed, 1)
                st = Steps(dve, dve_step)
                dve.wait_ge(zeroed, 2)
                dve.wait_ge(small_in, 16 * (2 + 3 * QG))
                st.of(dve.tensor_tensor(table[:], table[:], before[:], ALU.subtract))
                st.of(dve.tensor_copy(pos_k[:], pos_k_int[:]))
                st.of(dve.tensor_copy(limit[:], pos_q_int[:]))
                st.wait()
                st.of(dve.tensor_scalar(limit[:], limit[:], first[:], None, ALU.subtract))
                for j in range(NJ):
                    for i in range(QG):
                        col = (j * QG + i) * AH
                        st.of(dve.tensor_copy(diffs[i * NB:(i + 1) * NB, j, col:col + AH], table[i * NB:(i + 1) * NB, :]))
                st.wait()
                for s in range(2):
                    dve.sem_inc(acc_ready[s], 1)
                for qt in range(TT):
                    ext = (qt + 1) * P
                    with dve.Fori(qt * N, qt * N + N) as i:
                        for s in range(2):
                            dve.wait_ge(acc_ready[s], i + 1)
                            for j in range(NJ):
                                ins = dve.tensor_scalar(steps[s][:, j, 0:ext], pos_k[:, 0:ext],
                                                        limit[:, bass.ds((2 * i + s) * NJ + j, 1)], None, ALU.is_le)
                            ins.then_inc(steps_ready[s], 1)

            @block.tensor
            def _(pe):
                for qt in range(TT):
                    ext = (qt + 1) * P
                    with pe.Fori(qt * N, qt * N + N) as i:
                        for s in range(2):
                            pe.wait_ge(steps_ready[s], i + 1)
                            pe.wait_ge(out_ready[s], i + 1)
                            for c in range(0, ext, HALF):
                                e = min(c + HALF, ext)
                                for j in range(NJ):
                                    mm = pe.matmul(acc[s][:, c:e], diffs[:, j, :], steps[s][:, j, c:e],
                                                   start=(j == 0), stop=(j == NJ - 1))
                            mm.then_inc(acc_ready[s], 1)

            @block.scalar
            def _(act):
                for s in range(2):
                    act.sem_inc(out_ready[s], 1)
                for qt in range(TT):
                    ext = (qt + 1) * P
                    with act.Fori(qt * N, qt * N + N) as i:
                        for s in range(2):
                            act.wait_ge(acc_ready[s], i + 2)
                            act.wait_ge(stored[s], i * 16 + 16)
                            act.activation(out[s][:, 0:ext], acc[s][:, 0:ext], ACT.Copy).then_inc(out_ready[s], 1)


def stage_attention(nc, d):
    with ExitStack() as stack:
        sp = Space(nc, stack, "at")
        ident = sp.sb("ident", [P, P])
        causal = sp.sb("causal", [P, P])
        ident_b = sp.sb("ident_b", [P, P], BF16)
        causal_b = sp.sb("causal_b", [P, P], BF16)
        lam_in = sp.sb("lam_in", [P, 4, 64])
        lam_prod = sp.sb("lam_prod", [P, 64])
        lam_sum = sp.sb("lam_sum", [P, 2])
        neg_lam = sp.sb("neg_lam", [P, 1])
        norm_w = sp.sb("norm_w", [P, 1])
        q = [sp.sb(f"q{s}", [P, S]) for s in range(2)]
        k = [sp.sb(f"k{s}", [P, S]) for s in range(2)]
        v = [sp.sb(f"v{s}", [P, TT, P]) for s in range(2)]
        bias = [sp.sb(f"bias{b}", [P, S]) for b in range(2)]
        soft = [[sp.sb(f"soft{b}{i}", [P, S]) for i in range(2)] for b in range(2)]
        top = [sp.sb(f"top{b}", [P, 2]) for b in range(2)]
        neg_top = [sp.sb(f"neg_top{b}", [P, 2]) for b in range(2)]
        total = [sp.sb(f"total{b}", [P, 2]) for b in range(2)]
        share = [sp.sb(f"share{b}", [P, 2]) for b in range(2)]
        diff = [sp.sb(f"diff{b}", [P, S]) for b in range(2)]
        diffT = [sp.sb(f"diffT{b}", [P, S]) for b in range(2)]
        squares = sp.sb("squares", [P, P])
        eps = sp.sb("eps", [P, 1])
        wait_here = sp.sb("wait_here", [1, 4])
        ss = sp.sb("ss", [P, TT])
        rstd = sp.sb("rstd", [P, TT])
        heads_out = sp.sb("heads_out", [P, TT, P])
        outT = [sp.sb(f"outT{s}", [P, S]) for s in range(2)]
        logit_ps = [sp.ps(f"logit_ps{i}", [P, S]) for i in range(2)]
        turn_ps = sp.ps("turn_ps", [P, S])
        av_ps = sp.ps("av_ps", [P, HALF])
        const_in = sp.sem("const_in")
        prep = sp.sem("prep")
        lam_exp = sp.sem("lam_exp")
        qkv_in = [sp.sem(f"qkv_in{s}") for s in range(2)]
        bias_in = [sp.sem(f"bias_in{b}") for b in range(2)]
        logits_mm = [sp.sem(f"logits_mm{i}") for i in range(2)]
        logits_ready = [sp.sem(f"logits_ready{i}") for i in range(2)]
        top_ready = [sp.sem(f"top_ready{i}") for i in range(2)]
        exp_done = [sp.sem(f"exp_done{i}") for i in range(2)]
        dve_step = sp.sem("dve_step")
        diff_ready = sp.sem("diff_ready")
        turned = sp.sem("turned")
        diffT_ready = sp.sem("diffT_ready")
        av_ready = sp.sem("av_ready")
        ss_ready = sp.sem("ss_ready")
        root_ready = sp.sem("root_ready")
        av_taken = sp.sem("av_taken")
        normed_ready = sp.sem("normed_ready")
        outT_mm = sp.sem("outT_mm")
        outT_ready = sp.sem("outT_ready")
        stored = [sp.sem(f"stored{s}") for s in range(2)]
        TURNS = AH // 2
        PAR = TT // 2

        def pipeline(stages):
            for n in range(TT + len(stages) - 1):
                for m, stage in enumerate(stages):
                    if stage is not None and 0 <= n - m < TT:
                        stage(n - m)

        with nc.Block() as block:
            @block.sync
            def _(sync):
                sync.dma_start(ident[:], d["ident"]).then_inc(const_in, 16)
                sync.dma_start(causal[:], d["causal"]).then_inc(const_in, 16)
                sync.dma_start(norm_w[:], d["attn_norm_w"].rearrange("(p a) -> p a", a=1)).then_inc(const_in, 16)
                sync.dma_start(eps[:], d["eps"][2].rearrange("(p a) -> p a", a=1)).then_inc(const_in, 16)
                for n in range(4):
                    sync.dma_start(lam_in[:, n, :], d["lambdas"][n].partition_broadcast(P)).then_inc(const_in, 16)
                for s in range(2):
                    sync.sem_inc(stored[s], 16)
                with sync.Fori(0, TURNS) as i:
                    for s in range(2):
                        h = 2 * i + s
                        for qt in range(TT):
                            b, ext = qt % 2, (qt + 1) * P
                            sync.wait_ge(logits_ready[1], h * TT + max(qt, 1))
                            sync.dma_start(bias[b][:, 0:ext], d["bias"][qt * P:(qt + 1) * P, bass.ds(h, 1), 0:ext].rearrange(
                                "q a k -> q (a k)")).then_inc(bias_in[b], 16)

            @block.gpsimd
            def _(pool):
                def load_head(h, s):
                    pool.dma_start(q[s][:], d["qkT"][h]).then_inc(qkv_in[s], 16)
                    pool.dma_start(k[s][:], d["qkT"][h + AH]).then_inc(qkv_in[s], 16)
                    pool.dma_start(v[s][:], d["v"][:, :, bass.ds(h * P, P)].rearrange("t p n -> p t n")).then_inc(qkv_in[s], 16)

                for s in range(2):
                    load_head(s, s)
                with pool.Fori(0, TURNS - 1) as i:
                    for s in range(2):
                        pool.wait_ge(av_ready, (2 * i + s) * TT + TT)
                        load_head(2 * i + s + 2, s)

            @block.tensor
            def _(pe):
                pe.wait_ge(prep, 3)
                with pe.Fori(0, TURNS) as i:
                    for s in range(2):
                        h = 2 * i + s

                        def logits(n):
                            if n == 0:
                                pe.wait_ge(qkv_in[s], i * 48 + 48)
                            for half in range(2):
                                pe.wait_ge(logits_ready[half], h * TT + n + 1)
                                rows = slice(half * 64, half * 64 + 64)
                                ext = (n + 1) * P
                                for c in range(0, ext, HALF):
                                    e = min(c + HALF, ext)
                                    last = e == ext
                                    mm = pe.matmul(logit_ps[half][:, c:e], q[s][rows, n * P:ext], k[s][rows, c:e],
                                                   start=True, stop=not last)
                                mm = pe.matmul(logit_ps[half][:, ext - P:ext], ident_b[:], causal_b[:], start=False, stop=True)
                                mm.then_inc(logits_mm[half], 1)

                        def turn(n):
                            pe.wait_ge(diff_ready, h * TT + n + 1)
                            pe.wait_ge(diffT_ready, h * TT + n + 1)
                            if n == 0:
                                pe.wait_ge(outT_ready, h + 1)
                            for t in range(n + 1):
                                mm = pe.transpose(turn_ps[:, t * P:(t + 1) * P], diff[n % 2][:, t * P:(t + 1) * P], ident[:])
                            mm.then_inc(turned, 1)

                        def times_v(n):
                            pe.wait_ge(diffT_ready, h * TT + n + 2)
                            pe.wait_ge(av_taken, h * TT + n + 1)
                            for t in range(n + 1):
                                mm = pe.matmul(av_ps[:, 0:P], diffT[n % 2][:, t * P:(t + 1) * P], v[s][:, t, :],
                                               start=(t == 0), stop=(t == n))
                            mm.then_inc(av_ready, 1)

                        pipeline([logits, turn, times_v])
                        pe.wait_ge(normed_ready, h + 1)
                        for t in range(TT):
                            mm = pe.transpose(turn_ps[:, t * P:(t + 1) * P], heads_out[:, t, :], ident[:])
                        mm.then_inc(outT_mm, 1)

            @block.vector
            def _(dve):
                dve.wait_ge(const_in, 16 * 8)
                st = Steps(dve, dve_step)
                dve.tensor_copy(ident_b[:], ident[:]).then_inc(prep, 1)
                dve.tensor_copy(causal_b[:], causal[:]).then_inc(prep, 1)
                for n in range(2):
                    st.of(dve.tensor_tensor(lam_prod[:], lam_in[:, 2 * n, :], lam_in[:, 2 * n + 1, :], ALU.mult))
                    st.wait()
                    st.of(dve.reduce_sum(lam_sum[:, n:n + 1], lam_prod[:], AX.X))
                    st.wait()
                st.of(dve.tensor_scalar(norm_w[:], norm_w[:], (1.0 - LAMBDA_INIT) * math.sqrt(P), None, ALU.mult))
                dve.wait_ge(lam_exp, 1)
                st.of(dve.tensor_tensor(neg_lam[:], lam_sum[:, 1:2], lam_sum[:, 0:1], ALU.subtract))
                st.wait()
                dve.tensor_scalar(neg_lam[:], neg_lam[:], LAMBDA_INIT, None, ALU.subtract).then_inc(prep, 1)
                dve.wait_ge(prep, 3)
                for half in range(2):
                    dve.sem_inc(logits_ready[half], 1)
                dve.sem_inc(av_taken, 1)
                base, PER_HEAD = st.n, 3 * TT + 1
                with dve.Fori(0, TURNS) as i:
                    for s in range(2):
                        h = 2 * i + s
                        own = Steps(dve, dve_step, h * PER_HEAD + base)

                        def logits(n):
                            b, ext = n % 2, (n + 1) * P
                            dve.wait_ge(bias_in[b], h * PAR * 16 + (n // 2 + 1) * 16)
                            for half in range(2):
                                dve.wait_ge(logits_mm[half], h * TT + n + 1)
                                dve.memset(wait_here[:, 2 * b + half:2 * b + half + 1], 0.0)
                                dve.tensor_tensor_reduce(soft[b][half][:, 0:ext], logit_ps[half][:, 0:ext], bias[b][:, 0:ext],
                                                         1.0, FINFO_MIN, ALU.add, ALU.max, top[b][:, half:half + 1]
                                                         ).then_inc(logits_ready[half], 1)
                            for half in range(2):
                                dve.wait_ge(logits_ready[half], h * TT + n + 2)
                                dve.tensor_scalar(neg_top[b][:, half:half + 1], top[b][:, half:half + 1], -1.0, None,
                                                  ALU.mult).then_inc(top_ready[half], 1)

                        def difference(n):
                            b, ext = n % 2, (n + 1) * P
                            for half in range(2):
                                dve.wait_ge(exp_done[half], h * TT + n + 1)
                            own.of(dve.reciprocal(share[b][:], total[b][:]))
                            own.wait()
                            own.of(dve.tensor_scalar(share[b][:, 1:2], share[b][:, 1:2], neg_lam[:], None, ALU.mult))
                            own.wait()
                            own.of(dve.tensor_scalar(diff[b][:, 0:ext], soft[b][1][:, 0:ext], share[b][:, 1:2], None, ALU.mult))
                            own.wait()
                            dve.scalar_tensor_tensor(diff[b][:, 0:ext], soft[b][0][:, 0:ext], share[b][:, 0:1],
                                                     diff[b][:, 0:ext], ALU.mult, ALU.add).then_inc(diff_ready, 1)

                        def take_av(n):
                            dve.wait_ge(ss_ready, h * TT + n + 1)
                            if n == 0:
                                dve.wait_ge(outT_ready, h + 1)
                            dve.tensor_copy(heads_out[:, n, :], av_ps[:, 0:P]).then_inc(av_taken, 1)

                        pipeline([logits, difference, take_av])
                        dve.wait_ge(root_ready, h + 1)
                        own.of(dve.reciprocal(rstd[:], ss[:]))
                        own.wait()
                        dve.wait_ge(av_taken, h * TT + TT + 1)
                        dve.tensor_tensor(heads_out[:], heads_out[:], rstd[:].unsqueeze(2).to_broadcast([P, TT, P]),
                                          ALU.mult).then_inc(normed_ready, 1)
                        assert own.n == PER_HEAD

            @block.scalar
            def _(act):
                act.wait_ge(dve_step, 4)
                act.activation(lam_sum[:], lam_sum[:], ACT.Exp).then_inc(lam_exp, 1)
                act.wait_ge(prep, 3)
                act.sem_inc(diffT_ready, 1)
                act.sem_inc(outT_ready, 1)
                with act.Fori(0, TURNS) as i:
                    for s in range(2):
                        h = 2 * i + s

                        def exponentials(n):
                            b, ext = n % 2, (n + 1) * P
                            for half in range(2):
                                act.wait_ge(top_ready[half], h * TT + n + 1)
                                act.activation(soft[b][half][:, 0:ext], soft[b][half][:, 0:ext], ACT.Exp,
                                               bias=neg_top[b][:, half:half + 1],
                                               accum_out=total[b][:, half:half + 1]).then_inc(exp_done[half], 1)

                        def take_turned(n):
                            act.wait_ge(turned, h * TT + n + 1)
                            act.activation(diffT[n % 2][:, 0:(n + 1) * P], turn_ps[:, 0:(n + 1) * P], ACT.Copy).then_inc(diffT_ready, 1)

                        def sum_squares(n):
                            act.wait_ge(av_ready, h * TT + n + 1)
                            act.activation(squares[:], av_ps[:, 0:P], ACT.Square, accum_out=ss[:, n:n + 1]).then_inc(ss_ready, 1)

                        pipeline([exponentials, take_turned, sum_squares])
                        act.wait_ge(ss_ready, h * TT + TT)
                        act.activation(ss[:], ss[:], ACT.Sqrt, bias=eps[:]).then_inc(root_ready, 1)
                        act.wait_ge(stored[s], i * 16 + 16)
                        act.wait_ge(outT_mm, h + 1)
                        act.activation(outT[s][:], turn_ps[:], ACT.Copy, scale=norm_w[:]).then_inc(outT_ready, 1)
                        act.wait_ge(outT_ready, h + 2)
                        act.dma_start(d["attT"][h], outT[s][:]).then_inc(stored[s], 16)
                for s in range(2):
                    act.wait_ge(stored[s], (TURNS + 1) * 16)


def stage_ssd(nc, d):
    OUTS = 4
    TURNS_PER_GROUP = TT + OUTS
    with ExitStack() as stack:
        sp = Space(nc, stack, "ssd")
        ident = sp.sb("ident", [P, P])
        upto = sp.sb("upto", [P, P])
        after = sp.sb("after", [P, P])
        ones = sp.sb("ones", [P, P])
        eps = sp.sb("eps", [P, 1])
        norm_w = sp.sb("norm_w", [P, DI // P])
        skip = sp.sb("skip", [P, SH])
        a_row = sp.sb("a_row", [P, SH])
        dt = sp.sb("dt", [P, TT, SH])
        da = sp.sb("da", [P, TT, SH])
        from_start = sp.sb("from_start", [P, TT, SH])
        to_end = sp.sb("to_end", [P, TT, SH])
        whole = sp.sb("whole", [P, TT, SH])
        bT = [sp.sb(f"bT{s}", [P, S]) for s in range(2)]
        cT = [sp.sb(f"cT{s}", [P, S]) for s in range(2)]
        xT = [sp.sb(f"xT{s}", [P, 2, S]) for s in range(2)]
        z = [sp.sb(f"z{s}", [P, TT, GW]) for s in range(2)]
        rows = [sp.sb(f"rows{b}", [P, HALF]) for b in range(2)]
        spread = [sp.sb(f"spread{b}", [P, HPG, P]) for b in range(2)]
        x_dt = [sp.sb(f"x_dt{b}", [P, HPG, HD]) for b in range(2)]
        x_end = [sp.sb(f"x_end{b}", [P, HPG, HD]) for b in range(2)]
        x_skip = [sp.sb(f"x_skip{b}", [P, HPG, HD]) for b in range(2)]
        decay = [sp.sb(f"decay{b}", [P, HPG, P]) for b in range(2)]
        cb = sp.sb("cb", [P, P])
        weights = [sp.sb(f"weights{b}", [P, HPG, P]) for b in range(2)]
        state = sp.sb("state", [P, HPG, HD])
        scaled = sp.sb("scaled", [P, HPG, HD])
        y = sp.sb("y", [P, HPG, HD])
        yz = sp.sb("yz", [P, TT, GW])
        squares = sp.sb("squares", [P, GW])
        ss = sp.sb("ss", [P, TT])
        rstd = sp.sb("rstd", [P, TT])
        ynT = [sp.sb(f"ynT{s}", [P, 2, S]) for s in range(2)]
        turn_ps = [sp.ps(f"turn_ps{b}", [P, HALF]) for b in range(2)]
        seg_ps = [sp.ps(f"seg_ps{b}", [P, HPG, P]) for b in range(2)]
        y_ps = [sp.ps(f"y_ps{b}", [P, 2, HPG, HD]) for b in range(2)]
        st_ps = sp.ps("st_ps", [P, HPG, HD])
        sums_ps = sp.ps("sums_ps", [P, TT, SH])

        const_in = sp.sem("const_in")
        prep = sp.sem("prep")
        a_exp = sp.sem("a_exp")
        sums_mm = sp.sem("sums_mm")
        sums_exp = sp.sem("sums_exp")
        group_in = [sp.sem(f"group_in{s}") for s in range(2)]
        turn_mm = sp.sem("turn_mm")
        turn_taken = sp.sem("turn_taken")
        spread_ready = sp.sem("spread_ready")
        seg_mm = sp.sem("seg_mm")
        decay_ready = sp.sem("decay_ready")
        x_ready = sp.sem("x_ready")
        weights_ready = sp.sem("weights_ready")
        y_mm = sp.sem("y_mm")
        state_ready = sp.sem("state_ready")
        y_taken = sp.sem("y_taken")
        dve_step = sp.sem("dve_step")
        ss_ready = sp.sem("ss_ready")
        root_ready = sp.sem("root_ready")
        normed_ready = sp.sem("normed_ready")
        stored = [sp.sem(f"stored{s}") for s in range(2)]
        TURNS = G // 2
        CONSTS = 8

        def heads(t, c, g):
            return t[:, c, bass.ds(g * HPG, HPG)]

        def pipeline(stages):
            for n in range(TT + len(stages) - 1):
                for m, stage in enumerate(stages):
                    if stage is not None and 0 <= n - m < TT:
                        stage(n - m)

        with nc.Block() as block:
            @block.sync
            def _(sync):
                sync.dma_start(ident[:], d["ident"]).then_inc(const_in, 16)
                sync.dma_start(upto[:], d["upto"]).then_inc(const_in, 16)
                sync.dma_start(after[:], d["after"]).then_inc(const_in, 16)
                sync.dma_start(eps[:], d["eps"][1].rearrange("(p a) -> p a", a=1)).then_inc(const_in, 16)
                sync.dma_start(norm_w[:], d["ssd_norm_w"]).then_inc(const_in, 16)
                sync.dma_start(skip[:], d["d_skip"].partition_broadcast(P)).then_inc(const_in, 16)
                sync.dma_start(a_row[:], d["a_log"].partition_broadcast(P)).then_inc(const_in, 16)
                sync.dma_start(dt[:], d["dt"].rearrange("t p n -> p t n")).then_inc(const_in, 16)

                def load_group(g, s):
                    sync.dma_start(bT[s][:], d["xbcT"][DI // P + g]).then_inc(group_in[s], 16)
                    sync.dma_start(cT[s][:], d["xbcT"][DI // P + G + g]).then_inc(group_in[s], 16)
                    sync.dma_start(xT[s][:], d["xbcT"][bass.ds(2 * g, 2)].rearrange("a p n -> p a n")).then_inc(group_in[s], 16)
                    sync.dma_start(z[s][:], d["z"][:, :, bass.ds(g * GW, GW)].rearrange("t p n -> p t n")).then_inc(group_in[s], 16)

                for s in range(2):
                    load_group(s, s)
                with sync.Fori(0, TURNS - 1) as i:
                    for s in range(2):
                        sync.wait_ge(y_taken, (2 * i + s) * TT + TT + 2)
                        load_group(2 * i + s + 2, s)

            @block.gpsimd
            def _(pool):
                pool.wait_ge(prep, 5)
                with pool.Fori(0, TURNS) as i:
                    for s in range(2):
                        g = 2 * i + s

                        def spread_da(c):
                            u = g * TT + c
                            pool.wait_ge(seg_mm, u + 1)
                            pool.tensor_tensor(spread[c % 2][:], after[:].unsqueeze(1).to_broadcast([P, HPG, P]),
                                               heads(da, c, g).unsqueeze(2).to_broadcast([P, HPG, P]), ALU.mult).then_inc(spread_ready, 1)

                        def scale_x(c):
                            u, b = g * TT + c, c % 2
                            pool.wait_ge(turn_taken, g * TURNS_PER_GROUP + c + 3)
                            pool.wait_ge(y_taken, u + 1)
                            x = rows[b][:, 0:GW].rearrange("p (r e) -> p r e", r=HPG)
                            for out, factor in ((x_dt[b], heads(dt, c, g)), (x_end[b], heads(to_end, c, g)),
                                                (x_skip[b], skip[:, bass.ds(g * HPG, HPG)])):
                                pool.tensor_tensor(out[:], x, factor.unsqueeze(2).to_broadcast([P, HPG, HD]),
                                                   ALU.mult).then_inc(x_ready, 1)

                        pipeline([spread_da, scale_x])

            @block.tensor
            def _(pe):
                pe.wait_ge(const_in, 16 * CONSTS)
                pe.wait_ge(prep, 3)
                for n, left in enumerate((upto, after, ones)):
                    if n:
                        pe.wait_ge(sums_exp, n)
                    pe.matmul(sums_ps[:], left[:], da[:], start=True, stop=True).then_inc(sums_mm, 1)
                pe.sem_inc(seg_mm, 2)
                with pe.Fori(0, TURNS) as i:
                    for s in range(2):
                        g = 2 * i + s

                        def turn_and_segments(c):
                            u, b = g * TT + c, c % 2
                            cols = slice(c * P, (c + 1) * P)
                            if c == 0:
                                pe.wait_ge(group_in[s], i * 64 + 64)
                            pe.wait_ge(turn_taken, g * TURNS_PER_GROUP + c + 1)
                            pe.transpose(turn_ps[b][:, 0:P], xT[s][:, 0, cols], ident[:])
                            pe.transpose(turn_ps[b][:, P:2 * P], xT[s][:, 1, cols], ident[:])
                            pe.transpose(turn_ps[b][:, 2 * P:3 * P], bT[s][:, cols], ident[:])
                            pe.matmul(turn_ps[b][:, 3 * P:4 * P], bT[s][:, cols], cT[s][:, cols],
                                      start=True, stop=True).then_inc(turn_mm, 1)
                            pe.wait_ge(spread_ready, u + 1)
                            pe.wait_ge(decay_ready, u + 1)
                            for r in range(HPG):
                                mm = pe.matmul(seg_ps[b][:, r, :], spread[b][:, r, :], upto[:], start=True, stop=True)
                            mm.then_inc(seg_mm, 1)

                        def outputs(c):
                            u, b = g * TT + c, c % 2
                            pe.wait_ge(weights_ready, u + 3)
                            pe.wait_ge(x_ready, 3 * u + 3)
                            pe.wait_ge(y_taken, u + 1)
                            for r in range(HPG):
                                mm = pe.matmul(y_ps[b][:, 0, r, :], weights[b][:, r, :], x_dt[b][:, r, :], start=True, stop=True)
                            if c > 0:
                                pe.wait_ge(state_ready, g * (TT - 1) + c)
                                mm = pe.matmul(y_ps[b][:, 1, :, :], cT[s][:, c * P:(c + 1) * P], state[:], start=True, stop=True)
                            if c < TT - 1:
                                mm = pe.matmul(st_ps[:], rows[b][:, 2 * P:3 * P], x_end[b][:], start=True, stop=True)
                            mm.then_inc(y_mm, 1)

                        pipeline([turn_and_segments, outputs])
                        pe.wait_ge(normed_ready, g + 1)
                        for o in range(OUTS):
                            pe.wait_ge(turn_taken, g * TURNS_PER_GROUP + TT + o + 1)
                            for t in range(4):
                                tok = 4 * (o % 2) + t
                                mm = pe.transpose(turn_ps[o % 2][:, t * P:(t + 1) * P], yz[:, tok, (o // 2) * P:(o // 2 + 1) * P], ident[:])
                            mm.then_inc(turn_mm, 1)

            @block.vector
            def _(dve):
                dve.memset(ones[:], 1.0).then_inc(prep, 1)
                dve.wait_ge(const_in, 16 * CONSTS)
                dve.wait_ge(a_exp, 1)
                dve.tensor_scalar(a_row[:], a_row[:], -1.0, None, ALU.mult).then_inc(prep, 1)
                dve.wait_ge(prep, 2)
                dve.tensor_tensor(da[:], dt[:], a_row[:].unsqueeze(1).to_broadcast([P, TT, SH]), ALU.mult).then_inc(prep, 1)
                dve.wait_ge(sums_exp, 2)
                dve.tensor_tensor(to_end[:], to_end[:], dt[:], ALU.mult).then_inc(prep, 1)
                dve.wait_ge(sums_exp, 3)
                dve.tensor_scalar(norm_w[:], norm_w[:], math.sqrt(GW), None, ALU.mult).then_inc(prep, 1)
                dve.sem_inc(weights_ready, 2)
                dve.sem_inc(y_taken, 2)
                PER_GROUP = 37
                with dve.Fori(0, TURNS) as i:
                    for s in range(2):
                        g = 2 * i + s
                        own = Steps(dve, dve_step, g * PER_GROUP)

                        def weigh(c):
                            u, b = g * TT + c, c % 2
                            dve.wait_ge(turn_taken, g * TURNS_PER_GROUP + c + 3)
                            dve.wait_ge(weights_ready, u + 2)
                            own.of(dve.tensor_tensor(cb[:], rows[b][:, 3 * P:4 * P], upto[:], ALU.mult))
                            own.wait()
                            dve.wait_ge(decay_ready, u + 3)
                            dve.tensor_tensor(weights[b][:], decay[b][:], cb[:].unsqueeze(1).to_broadcast([P, HPG, P]),
                                              ALU.mult).then_inc(weights_ready, 1)

                        def finish(c):
                            u, b = g * TT + c, c % 2
                            dve.wait_ge(y_mm, u + 1)
                            dve.wait_ge(y_taken, u + 2)
                            if c == 0:
                                dve.tensor_copy(state[:], st_ps[:]).then_inc(state_ready, 1)
                            elif c < TT - 1:
                                own.of(dve.tensor_tensor(state[:], state[:], heads(whole, c, g).unsqueeze(2).to_broadcast(
                                    [P, HPG, HD]), ALU.mult))
                                own.wait()
                                dve.tensor_tensor(state[:], state[:], st_ps[:], ALU.add).then_inc(state_ready, 1)
                            dve.wait_ge(x_ready, 3 * u + 3)
                            if c == 0:
                                own.of(dve.tensor_tensor(y[:], y_ps[b][:, 0, :, :], x_skip[b][:], ALU.add))
                                dve.wait_ge(turn_taken, g * TURNS_PER_GROUP + 2)
                            else:
                                own.of(dve.tensor_tensor(scaled[:], y_ps[b][:, 1, :, :], heads(from_start, c, g).unsqueeze(2).to_broadcast(
                                    [P, HPG, HD]), ALU.mult))
                                own.wait()
                                own.of(dve.tensor_tensor(y[:], y_ps[b][:, 0, :, :], scaled[:], ALU.add))
                                own.wait()
                                own.of(dve.tensor_tensor(y[:], y[:], x_skip[b][:], ALU.add))
                            own.wait()
                            dve.tensor_tensor(yz[:, c, :], y[:].rearrange("p r e -> p (r e)"), z[s][:, c, :], ALU.mult).then_inc(y_taken, 1)

                        def weigh_first(c):
                            if c == 0:
                                dve.wait_ge(group_in[s], i * 64 + 64)
                            weigh(c)

                        pipeline([weigh_first, finish])
                        dve.wait_ge(root_ready, g + 1)
                        own.of(dve.reciprocal(rstd[:], ss[:]))
                        own.wait()
                        dve.tensor_tensor(yz[:], yz[:], rstd[:].unsqueeze(2).to_broadcast([P, TT, GW]), ALU.mult).then_inc(normed_ready, 1)
                        assert own.n == PER_GROUP
                        dve.wait_ge(stored[s], i * 16 + 16)
                        for o in range(OUTS):
                            dve.wait_ge(turn_mm, g * TURNS_PER_GROUP + TT + o + 1)
                            dve.tensor_scalar(ynT[s][:, o // 2, (o % 2) * HALF:(o % 2 + 1) * HALF], turn_ps[o % 2][:],
                                              norm_w[:, bass.ds(2 * g + o // 2, 1)], None, ALU.mult).then_inc(turn_taken, 1)

            @block.scalar
            def _(act):
                act.wait_ge(const_in, 16 * CONSTS)
                act.activation(a_row[:], a_row[:], ACT.Exp).then_inc(a_exp, 1)
                for n, out in enumerate((from_start, to_end, whole)):
                    act.wait_ge(sums_mm, n + 1)
                    act.activation(out[:], sums_ps[:], ACT.Exp).then_inc(sums_exp, 1)
                act.wait_ge(prep, 5)
                act.sem_inc(turn_taken, 2)
                act.sem_inc(decay_ready, 2)
                for s in range(2):
                    act.sem_inc(stored[s], 16)
                with act.Fori(0, TURNS) as i:
                    for s in range(2):
                        g = 2 * i + s

                        def take_and_decay(c):
                            u, b = g * TT + c, c % 2
                            act.wait_ge(turn_mm, g * TURNS_PER_GROUP + c + 1)
                            act.wait_ge(y_taken, u + 1)
                            act.activation(rows[b][:], turn_ps[b][:], ACT.Copy).then_inc(turn_taken, 1)
                            act.wait_ge(seg_mm, u + 3)
                            act.wait_ge(weights_ready, u + 1)
                            act.activation(decay[b][:], seg_ps[b][:], ACT.Exp).then_inc(decay_ready, 1)

                        def sum_squares(c):
                            act.wait_ge(y_taken, g * TT + c + 3)
                            act.activation(squares[:], yz[:, c, :], ACT.Square, accum_out=ss[:, c:c + 1]).then_inc(ss_ready, 1)
                            act.wait_ge(ss_ready, g * TT + c + 1)

                        pipeline([take_and_decay, None, sum_squares])
                        act.activation(ss[:], ss[:], ACT.Sqrt, bias=eps[:]).then_inc(root_ready, 1)
                        act.wait_ge(turn_taken, g * TURNS_PER_GROUP + TURNS_PER_GROUP + 2)
                        act.dma_start(d["ynT"][bass.ds(2 * g, 2)].rearrange("a p n -> p a n"), ynT[s][:]).then_inc(stored[s], 16)
                for s in range(2):
                    act.wait_ge(stored[s], (TURNS + 1) * 16)


def stage_merge(nc, d):
    with ExitStack() as stack:
        sp = Space(nc, stack, "mg")
        KS, KA = DI // P, D // P
        ident = sp.sb("ident", [P, P])
        eps = sp.sb("eps", [P, 1])
        g1 = sp.sb("g1", [P, D])
        scale2 = sp.sb("scale2", [P, D])
        shift2 = sp.sb("shift2", [P, D])
        w_ssd = sp.sb("w_ssd", [P, KS, D])
        w_att = sp.sb("w_att", [P, KA, D])
        w_out = sp.sb("w_out", [P, KD, D])
        ynT = sp.sb("ynT", [P, KS, P])
        attT = sp.sb("attT", [P, KA, P])
        gates = sp.sb("gates", [P, 2 * D])
        x = sp.sb("x", [P, D])
        mix = sp.sb("mix", [P, D])
        other = sp.sb("other", [P, D])
        mixT = sp.sb("mixT", [P, KD, P])
        n2 = sp.sb("n2", [P, D])
        ss = sp.sb("ss", [P, 1])
        rstd = sp.sb("rstd", [P, 1])
        n2T = sp.sb("n2T", [P, KD, P])
        ssd_ps = sp.ps("ssd_ps", [P, D])
        att_ps = sp.ps("att_ps", [P, D])
        turn_ps = sp.ps("turn_ps", [P, KD, P])
        out_ps = sp.ps("out_ps", [P, D])
        w_in = sp.sem("w_in")
        w_later = sp.sem("w_later")
        branches_in = sp.sem("branches_in")
        rows_in = sp.sem("rows_in")
        branches_mm = sp.sem("branches_mm")
        dve_step = sp.sem("dve_step")
        mix_ready = sp.sem("mix_ready")
        turned = sp.sem("turned")
        turned_out = sp.sem("turned_out")
        out_mm = sp.sem("out_mm")
        h_ready = sp.sem("h_ready")
        ss_step = sp.sem("ss_step")
        n2_ready = sp.sem("n2_ready")
        stored = sp.sem("stored")
        with nc.Block() as block:
            @block.sync
            def _(sync):
                sync.dma_start(ident[:], d["ident"]).then_inc(w_in, 16)
                sync.dma_start(eps[:], d["eps"][0].rearrange("(p a) -> p a", a=1)).then_inc(w_in, 16)
                for row, n in ((g1, 2), (scale2, 4), (shift2, 3)):
                    sync.dma_start(row[:], d["rows"][n].partition_broadcast(P)).then_inc(w_in, 16)
                sync.dma_start(w_ssd[:], d["w_ssd_o"].rearrange("(k p) n -> p k n", p=P)).then_inc(w_in, 16)
                sync.dma_start(w_att[:], d["w_attn_o"].rearrange("(k p) n -> p k n", p=P)).then_inc(w_in, 16)
                sync.dma_start(w_out[:], d["w_out"].rearrange("(k p) n -> p k n", p=P)).then_inc(w_later, 16)
                sync.sem_inc(stored, 48)
                with sync.Fori(0, TT) as t:
                    sync.wait_ge(h_ready, t + 1)
                    sync.dma_start(d["h"][t], x[:]).then_inc(stored, 16)
                    sync.wait_ge(n2_ready, t + 1)
                    sync.wait_ge(turned_out, 2 * t + 3)
                    sync.dma_start(d["n2T"][:, :, bass.ds(t * P, P)].rearrange("k p n -> p k n"), n2T[:]).then_inc(stored, 32)
                sync.wait_ge(stored, 48 * (TT + 1))

            @block.gpsimd
            def _(pool):
                def load_branches(t):
                    pool.dma_start(ynT[:], d["ynT"][:, :, bass.ds(t * P, P)].rearrange("k p n -> p k n")).then_inc(branches_in, 16)
                    pool.dma_start(attT[:], d["attT"][:, :, bass.ds(t * P, P)].rearrange("k p n -> p k n")).then_inc(branches_in, 16)

                load_branches(0)
                pool.dma_start(gates[:], d["gate"][0]).then_inc(rows_in, 16)
                pool.dma_start(x[:], d["x"][0:P, :]).then_inc(rows_in, 16)
                with pool.Fori(1, TT) as t:
                    pool.wait_ge(branches_mm, t)
                    load_branches(t)
                    pool.wait_ge(mix_ready, t)
                    pool.dma_start(gates[:], d["gate"][t]).then_inc(rows_in, 16)
                    pool.wait_ge(n2_ready, t)
                    pool.wait_ge(stored, t * 48 + 48)
                    pool.dma_start(x[:], d["x"][bass.ds(t * P, P), :]).then_inc(rows_in, 16)

            @block.tensor
            def _(pe):
                pe.wait_ge(w_in, 7 * 16)
                with pe.Fori(0, TT) as t:
                    pe.wait_ge(branches_in, t * 32 + 32)
                    for ps, w, y, n in ((ssd_ps, w_ssd, ynT, KS), (att_ps, w_att, attT, KA)):
                        for c in range(2):
                            for k in range(n):
                                mm = pe.matmul(ps[:, c * HALF:(c + 1) * HALF], y[:, k, :], w[:, k, c * HALF:(c + 1) * HALF],
                                               start=(k == 0), stop=(k == n - 1))
                    mm.then_inc(branches_mm, 1)
                    pe.wait_ge(mix_ready, t + 1)
                    for k in range(KD):
                        mm = pe.transpose(turn_ps[:, k, :], mix[:, k * P:(k + 1) * P], ident[:])
                    mm.then_inc(turned, 1)
                    pe.wait_ge(turned_out, 2 * t + 2)
                    pe.wait_ge(w_later, 16)
                    for c in range(2):
                        for k in range(KD):
                            mm = pe.matmul(out_ps[:, c * HALF:(c + 1) * HALF], mixT[:, k, :], w_out[:, k, c * HALF:(c + 1) * HALF],
                                           start=(k == 0), stop=(k == KD - 1))
                    mm.then_inc(out_mm, 1)
                    pe.wait_ge(n2_ready, t + 1)
                    for k in range(KD):
                        mm = pe.transpose(turn_ps[:, k, :], n2[:, k * P:(k + 1) * P], ident[:])
                    mm.then_inc(turned, 1)

            @block.vector
            def _(dve):
                dve.wait_ge(w_in, 7 * 16)
                with dve.Fori(0, TT) as t:
                    own = Steps(dve, dve_step, t * 5)
                    dve.wait_ge(branches_mm, t + 1)
                    dve.wait_ge(rows_in, t * 32 + 32)
                    dve.wait_ge(turned_out, 2 * t + 1)
                    own.of(dve.tensor_tensor(mix[:], ssd_ps[:], gates[:, 0:D], ALU.mult))
                    own.of(dve.tensor_tensor(other[:], att_ps[:], gates[:, D:2 * D], ALU.mult))
                    own.wait()
                    dve.tensor_tensor(mix[:], mix[:], other[:], ALU.add).then_inc(mix_ready, 1)
                    dve.wait_ge(out_mm, t + 1)
                    own.of(dve.tensor_tensor(mix[:], out_ps[:], g1[:], ALU.mult))
                    own.wait()
                    dve.tensor_tensor(x[:], x[:], mix[:], ALU.add).then_inc(h_ready, 1)
                    dve.wait_ge(ss_step, 2 * t + 2)
                    own.of(dve.reciprocal(rstd[:], ss[:]))
                    own.wait()
                    own.of(dve.scalar_tensor_tensor(n2[:], x[:], rstd[:], scale2[:], ALU.mult, ALU.mult))
                    own.wait()
                    dve.tensor_tensor(n2[:], n2[:], shift2[:], ALU.add).then_inc(n2_ready, 1)

            @block.scalar
            def _(act):
                act.wait_ge(w_in, 7 * 16)
                act.sem_inc(turned_out, 1)
                with act.Fori(0, TT) as t:
                    act.wait_ge(turned, 2 * t + 1)
                    act.activation(mixT[:], turn_ps[:], ACT.Copy).then_inc(turned_out, 1)
                    act.wait_ge(h_ready, t + 1)
                    act.activation(other[:], x[:], ACT.Square, accum_out=ss[:]).then_inc(ss_step, 1)
                    act.wait_ge(ss_step, 2 * t + 1)
                    act.activation(ss[:], ss[:], ACT.Sqrt, bias=eps[:]).then_inc(ss_step, 1)
                    act.wait_ge(turned, 2 * t + 2)
                    act.wait_ge(stored, t * 48 + 48)
                    act.activation(n2T[:], turn_ps[:], ACT.Copy).then_inc(turned_out, 1)


PAIR_ROWS = [(0, 1, 16), (1, 2, 8), (2, 3, 5), (3, 4, 4), (4, 5, 3), (5, 8, 2), (8, 16, 1)]
PAIRS = sum((a1 - a0) * nb for a0, a1, nb in PAIR_ROWS)


def stage_peer_topk(nc, d):
    with ExitStack() as stack:
        sp = Space(nc, stack, "tk")
        ident = sp.sb("ident", [P, P])
        pair_iota = sp.sb("pair_iota", [P, PAIRS])
        n2T = sp.sb("n2T", [P, KD, S])
        wq = [sp.sb(f"wq{s}", [P, KD, P]) for s in range(2)]
        keys = [sp.sb(f"keys{s}", [P, 2 * NK]) for s in range(2)]
        qT = [sp.sb(f"qT{s}", [P, S]) for s in range(2)]
        score = [sp.sb(f"score{s}", [P, TT, 2, NK]) for s in range(2)]
        top = [sp.sb(f"top{s}", [P, TT, 2, TOPK]) for s in range(2)]
        index = [sp.sb(f"index{s}", [P, TT, 2, TOPK], U32) for s in range(2)]
        indexf = [sp.sb(f"indexf{s}", [P, TT, 2, TOPK]) for s in range(2)]
        pair = [sp.sb(f"pair{s}", [P, TT, PAIRS]) for s in range(2)]
        pair_id = [sp.sb(f"pair_id{s}", [P, TT, PAIRS]) for s in range(2)]
        best = [sp.sb(f"best{s}", [P, TT, TOPK]) for s in range(2)]
        place = [sp.sb(f"place{s}", [P, TT, TOPK], U32) for s in range(2)]
        placef = [sp.sb(f"placef{s}", [P, TT, TOPK]) for s in range(2)]
        waits = sp.sb("waits", [1, 10])
        hot = sp.sb("hot", [P, TT * TOPK, PAIRS])
        expert = [sp.sb(f"expert{s}", [P, TT, TOPK], I32) for s in range(2)]
        total = [sp.sb(f"total{s}", [P, TT]) for s in range(2)]
        chosen = sp.sb("chosen", [P, 3, TT, PH, TOPK])
        chosenT = sp.sb("chosenT", [P, 3, S])
        split = [sp.sb(f"split{s}", [P, TT, TOPK], I32) for s in range(2)]
        q_ps = sp.ps("q_ps", [P, S])
        score_ps = sp.ps("score_ps", [P, TT, 2 * NK])
        turn_ps = [sp.ps(f"turn_ps{b}", [P, HALF]) for b in range(2)]
        const_in = sp.sem("const_in")
        keys_zero = sp.sem("keys_zero")
        w_in = [sp.sem(f"w_in{s}") for s in range(2)]
        q_mm = sp.sem("q_mm")
        q_ready = sp.sem("q_ready")
        score_mm = sp.sem("score_mm")
        score_ready = sp.sem("score_ready")
        dve_step = sp.sem("dve_step")
        place_ready = sp.sem("place_ready")
        hot_made = sp.sem("hot_made")
        hot_ready = sp.sem("hot_ready")
        gate_exp = sp.sem("gate_exp")
        head_done = sp.sem("head_done")
        turn_mm = sp.sem("turn_mm")
        turned = sp.sem("turned")
        stored = sp.sem("stored")
        TURNS = PH // 2
        with nc.Block() as block:
            @block.sync
            def _(sync):
                sync.dma_start(n2T[:], d["n2T"].rearrange("k p n -> p k n")).then_inc(const_in, 16)
                sync.dma_start(ident[:], d["ident"]).then_inc(const_in, 16)
                sync.dma_start(pair_iota[:], d["iota"][0:PAIRS].partition_broadcast(P)).then_inc(const_in, 16)

                def load_head(h, s):
                    sync.dma_start(wq[s][:], d["w_pq"][h]).then_inc(w_in[s], 16)
                    sync.dma_start(keys[s][0:64, 0:NK], d["key1T"][h]).then_inc(w_in[s], 16)
                    sync.dma_start(keys[s][64:P, NK:2 * NK], d["key2T"][h]).then_inc(w_in[s], 16)

                sync.wait_ge(keys_zero, 2)
                for s in range(2):
                    load_head(s, s)
                with sync.Fori(0, TURNS - 1) as i:
                    for s in range(2):
                        sync.wait_ge(score_mm, 2 * i + s + 1)
                        load_head(2 * i + s + 2, s)
                sync.wait_ge(turned, 6)
                sync.dma_start(d["chosenT"].rearrange("a p n -> p a n"), chosenT[:]).then_inc(stored, 16)
                sync.wait_ge(stored, 16)

            @block.tensor
            def _(pe):
                pe.wait_ge(const_in, 48)
                with pe.Fori(0, TURNS) as i:
                    for s in range(2):
                        h = 2 * i + s
                        pe.wait_ge(w_in[s], i * 48 + 48)
                        pe.wait_ge(q_ready, h + 1)
                        for c in range(2):
                            for k in range(KD):
                                mm = pe.matmul(q_ps[:, c * HALF:(c + 1) * HALF], wq[s][:, k, :], n2T[:, k, c * HALF:(c + 1) * HALF],
                                               start=(k == 0), stop=(k == KD - 1))
                        mm.then_inc(q_mm, 1)
                        pe.wait_ge(q_ready, h + 2)
                        pe.wait_ge(score_ready, h + 1)
                        for t in range(TT):
                            mm = pe.matmul(score_ps[:, t, :], qT[s][:, t * P:(t + 1) * P], keys[s][:], start=True, stop=True)
                        mm.then_inc(score_mm, 1)
                pe.wait_ge(head_done, PH)
                for n in range(6):
                    if n >= 2:
                        pe.wait_ge(turned, n - 1)
                    for t in range(4):
                        tt = 4 * (n % 2) + t
                        mm = pe.transpose(turn_ps[n % 2][:, t * P:(t + 1) * P],
                                          chosen[:, n // 2, tt, :, :].rearrange("p h k -> p (h k)"), ident[:])
                    mm.then_inc(turn_mm, 1)

            @block.scalar
            def _(act):
                act.sem_inc(q_ready, 1)
                act.sem_inc(score_ready, 1)
                with act.Fori(0, TURNS) as i:
                    for s in range(2):
                        h = 2 * i + s
                        act.wait_ge(q_mm, h + 1)
                        act.activation(qT[s][:], q_ps[:], ACT.Copy).then_inc(q_ready, 1)
                        act.wait_ge(score_mm, h + 1)
                        act.wait_ge(place_ready, h + 1)
                        act.activation(score[s][:], score_ps[:].rearrange("p t (a n) -> p t a n", a=2), ACT.Copy).then_inc(score_ready, 1)
                        act.wait_ge(place_ready, h + 3)
                        act.activation(best[s][:], best[s][:], ACT.Exp).then_inc(gate_exp, 1)
                for n in range(6):
                    act.wait_ge(turn_mm, n + 1)
                    act.activation(chosenT[:, n // 2, (n % 2) * HALF:(n % 2 + 1) * HALF], turn_ps[n % 2][:], ACT.Copy).then_inc(turned, 1)

            @block.gpsimd
            def _(pool):
                pool.wait_ge(const_in, 48)
                with pool.Fori(0, TURNS) as i:
                    for s in range(2):
                        h = 2 * i + s
                        pool.wait_ge(hot_made, h + 1)
                        hot4 = hot[:].rearrange("p (t k) n -> p t k n", t=TT)
                        pool.tensor_tensor(hot4, hot4, pair_id[s][:].unsqueeze(2).to_broadcast([P, TT, TOPK, PAIRS]), ALU.mult).then_inc(hot_ready, 1)

            @block.vector
            def _(dve):
                for s in range(2):
                    dve.memset(keys[s][:], 0.0).then_inc(keys_zero, 1)
                dve.sem_inc(place_ready, 2)

                def two_rounds(own, lists, cell):
                    def passes(make):
                        nonlocal cell
                        own.of(dve.memset(waits[:, cell:cell + 1], 0.0))
                        cell += 1
                        for values, out, place in lists:
                            own.of(make(values, out, place))
                        own.wait()

                    for lo in (0, 8):
                        if lo:
                            passes(lambda values, out, place: dve.match_replace(values, out[:, 0:8], values, FINFO_MIN))
                        passes(lambda values, out, place: dve.max(out[:, lo:lo + 8], values))
                        passes(lambda values, out, place: dve.max_index(place[:, lo:lo + 8], out[:, lo:lo + 8], values))

                def select(i, s, own):
                    h = 2 * i + s
                    dve.wait_ge(score_ready, h + 2)
                    two_rounds(own, [(score[s][:, t, a, :], top[s][:, t, a, :], index[s][:, t, a, :])
                                     for t in range(TT) for a in range(2)], 0)
                    own.of(dve.tensor_copy(indexf[s][:], index[s][:]))
                    own.wait()
                    own.of(dve.tensor_scalar(indexf[s][:, :, 0, :], indexf[s][:, :, 0, :], float(NK), None, ALU.mult))
                    own.wait()
                    for out, src in ((pair[s], top[s]), (pair_id[s], indexf[s])):
                        at = 0
                        for a0, a1, nb in PAIR_ROWS:
                            na = a1 - a0
                            own.of(dve.tensor_tensor(out[:, :, at:at + na * nb].rearrange("p t (a b) -> p t a b", a=na),
                                                     src[:, :, 0, a0:a1].unsqueeze(3).to_broadcast([P, TT, na, nb]),
                                                     src[:, :, 1, 0:nb].unsqueeze(2).to_broadcast([P, TT, na, nb]), ALU.add))
                            at += na * nb
                    own.wait()
                    two_rounds(own, [(pair[s][:, t, :], best[s][:, t, :], place[s][:, t, :]) for t in range(TT)], 5)
                    own.of(dve.tensor_copy(placef[s][:], place[s][:]))
                    own.of(dve.tensor_copy(total[s][:], best[s][:, :, 0:1].rearrange("p t a -> p (t a)")))
                    own.wait()
                    dve.tensor_tensor(best[s][:], best[s][:], total[s][:].unsqueeze(2).to_broadcast([P, TT, TOPK]),
                                      ALU.subtract).then_inc(place_ready, 1)
                    dve.tensor_tensor(hot[:], placef[s][:].rearrange("p t k -> p (t k)").unsqueeze(2).to_broadcast([P, TT * TOPK, PAIRS]),
                                      pair_iota[:].unsqueeze(1).to_broadcast([P, TT * TOPK, PAIRS]), ALU.is_equal).then_inc(hot_made, 1)

                def collect(i, s, own):
                    h = 2 * i + s
                    dve.wait_ge(gate_exp, h + 1)
                    own.of(dve.reduce_sum(total[s][:], best[s][:], AX.X))
                    own.wait()
                    own.of(dve.reciprocal(total[s][:], total[s][:]))
                    own.wait()
                    own.of(dve.tensor_tensor(chosen[:, 2, :, bass.ds(h, 1), :].rearrange("p t a k -> p t (a k)"), best[s][:],
                                             total[s][:].unsqueeze(2).to_broadcast([P, TT, TOPK]), ALU.mult))
                    dve.wait_ge(hot_ready, h + 1)
                    own.of(dve.reduce_sum(placef[s][:].rearrange("p t k -> p (t k)"), hot[:], AX.X))
                    own.wait()
                    own.of(dve.tensor_copy(expert[s][:], placef[s][:]))
                    own.wait()
                    own.of(dve.tensor_scalar(split[s][:], expert[s][:], 7, None, ALU.arith_shift_right))
                    own.of(dve.tensor_scalar(expert[s][:], expert[s][:], NK - 1, None, ALU.bitwise_and))
                    own.wait()
                    own.of(dve.tensor_copy(chosen[:, 0, :, bass.ds(h, 1), :].rearrange("p t a k -> p t (a k)"), split[s][:]))
                    own.of(dve.tensor_copy(chosen[:, 1, :, bass.ds(h, 1), :].rearrange("p t a k -> p t (a k)"), expert[s][:]))
                    own.wait()
                    dve.sem_inc(head_done, 1)

                PER_HEAD = 5 * 2 * TT + 2 + 2 * len(PAIR_ROWS) + 5 * TT + 2 + 9 + 10
                with dve.Fori(0, TURNS) as i:
                    for s in range(2):
                        own = Steps(dve, dve_step, (2 * i + s) * PER_HEAD)
                        select(i, s, own)
                        collect(i, s, own)
                        assert own.n == PER_HEAD, own.n


def stage_peer_gates(nc, d):
    TOK = 4
    UN = 2
    NBANK = 4
    INNER = P // (TOK * NBANK)
    with ExitStack() as stack:
        sp = Space(nc, stack, "gt")
        chosenT = sp.sb("chosenT", [P, 3, S])
        iota = sp.sb("iota", [P, NK])
        row_hot = [sp.sb(f"row_hot{b}", [P, TOK, NK]) for b in range(NBANK)]
        col_hot = [sp.sb(f"col_hot{b}", [P, TOK, NK]) for b in range(NBANK)]
        gates = [sp.sb(f"gates{s}", [P, NK, P]) for s in range(2)]
        gate_ps = [sp.ps(f"gate_ps{b}", [P, TOK, NK]) for b in range(NBANK)]
        const_in = sp.sem("const_in")
        hot_ready = [sp.sem(f"hot_ready{b}") for b in range(NBANK)]
        gates_mm = [sp.sem(f"gates_mm{b}") for b in range(NBANK)]
        gates_taken = [sp.sem(f"gates_taken{b}") for b in range(NBANK)]
        stored = [sp.sem(f"stored{s}") for s in range(2)]
        TURNS = TT // 2
        with nc.Block() as block:
            @block.sync
            def _(sync):
                sync.dma_start(chosenT[:], d["chosenT"].rearrange("a p n -> p a n")).then_inc(const_in, 16)
                sync.dma_start(iota[:], d["iota"].partition_broadcast(P)).then_inc(const_in, 16)
                for s in range(2):
                    sync.sem_inc(stored[s], 16)
                with sync.Fori(0, TURNS) as i:
                    for s in range(2):
                        for b in range(NBANK):
                            sync.wait_ge(gates_taken[b], (2 * i + s) * INNER + INNER + 1)
                        sync.dma_start(d["gates"][:, :, bass.ds((2 * i + s) * P, P)], gates[s][:]).then_inc(stored[s], 16)
                for s in range(2):
                    sync.wait_ge(stored[s], (TURNS + 1) * 16)

            @block.vector
            def _(dve):
                dve.wait_ge(const_in, 32)
                for b in range(NBANK):
                    dve.sem_inc(gates_mm[b], 1)
                with dve.Fori(0, TT * INNER) as j:
                    for b in range(NBANK):
                        dve.wait_ge(gates_mm[b], j + 1)
                        for t in range(TOK):
                            tok = bass.ds(j * TOK * NBANK + b * TOK + t, 1)
                            dve.tensor_scalar(row_hot[b][:, t, :], iota[:], chosenT[:, 0, tok], None, ALU.is_equal)
                            ins = dve.tensor_scalar(col_hot[b][:, t, :], iota[:], chosenT[:, 1, tok], chosenT[:, 2, tok],
                                                    ALU.is_equal, ALU.mult)
                        ins.then_inc(hot_ready[b], 1)

            @block.tensor
            def _(pe):
                with pe.Fori(0, TT * INNER) as j:
                    for b in range(NBANK):
                        pe.wait_ge(hot_ready[b], j + 1)
                        pe.wait_ge(gates_taken[b], j + 1)
                        for t in range(TOK):
                            mm = pe.matmul(gate_ps[b][:, t, :], row_hot[b][:, t, :], col_hot[b][:, t, :], start=True, stop=True)
                        mm.then_inc(gates_mm[b], 1)

            @block.scalar
            def _(act):
                for b in range(NBANK):
                    act.sem_inc(gates_taken[b], 1)
                with act.Fori(0, TURNS) as i:
                    for s in range(2):
                        act.wait_ge(stored[s], i * 16 + 16)
                        with act.Fori(0, INNER) as j:
                            for b in range(NBANK):
                                act.wait_ge(gates_mm[b], (2 * i + s) * INNER + j + 2)
                                act.activation(gates[s][:, :, bass.ds(j * TOK * NBANK + b * TOK, TOK)],
                                               gate_ps[b][:].rearrange("p t n -> p n t"), ACT.Copy).then_inc(gates_taken[b], 1)


def stage_peer_mix(nc, d):
    NJ = 4
    TURNS = NK // NJ
    with ExitStack() as stack:
        outer = Space(nc, stack, "px")
        acc = outer.sb("acc", [P, TT, D])
        peer_experts(nc, d, acc, NJ, TURNS)
        peer_finish(nc, d, acc)


def peer_experts(nc, d, acc, NJ, TURNS):
    with ExitStack() as stack:
        sp = Space(nc, stack, "pe")
        n2T = sp.sb("n2T", [P, KD, S])
        uT = [sp.sb(f"uT{j}", [P, KD, P]) for j in range(NJ)]
        gate = [sp.sb(f"gate{j}", [P, S]) for j in range(NJ)]
        v = [sp.sb(f"v{j}", [P, D]) for j in range(NJ)]
        hidden = [sp.sb(f"hidden{b}", [P, S]) for b in range(2)]
        weight = [sp.sb(f"weight{j}", [P, S]) for j in range(NJ)]
        hid_ps = [sp.ps(f"hid_ps{b}", [P, S]) for b in range(2)]
        NOUT = 4
        out_ps = [sp.ps(f"out_ps{b}", [P, HALF]) for b in range(NOUT)]
        n2_in = sp.sem("n2_in")
        zeroed = sp.sem("zeroed")
        u_in = [sp.sem(f"u_in{j}") for j in range(NJ)]
        gate_in = [sp.sem(f"gate_in{j}") for j in range(NJ)]
        v_in = [sp.sem(f"v_in{j}") for j in range(NJ)]
        hid_mm = [sp.sem(f"hid_mm{j}") for j in range(NJ)]
        gelu_done = [sp.sem(f"gelu_done{j}") for j in range(NJ)]
        weight_ready = [sp.sem(f"weight_ready{j}") for j in range(NJ)]
        out_mm = [sp.sem(f"out_mm{b}") for b in range(NOUT)]
        out_taken = [sp.sem(f"out_taken{b}") for b in range(NOUT)]
        TILES = 2 * TT
        USES = TILES // NOUT
        LAST = (TILES - 1) % NOUT
        with nc.Block() as block:
            @block.sync
            def _(sync):
                sync.dma_start(n2T[:], d["n2T"].rearrange("k p n -> p k n")).then_inc(n2_in, 16)

                def load_first(i):
                    for j in range(NJ):
                        e = i * NJ + j
                        if not isinstance(i, int):
                            sync.wait_ge(hid_mm[j], i)
                        sync.dma_start(uT[j][:], d["uT"][e]).then_inc(u_in[j], 16)
                        if not isinstance(i, int):
                            sync.wait_ge(weight_ready[j], i + 1)
                        sync.dma_start(gate[j][:], d["gates"][:, bass.ds(e, 1), :].rearrange("p a n -> p (a n)")).then_inc(gate_in[j], 16)

                def load_v(i):
                    if not isinstance(i, int):
                        sync.wait_ge(out_mm[LAST], i * USES)
                    for j in range(NJ):
                        sync.dma_start(v[j][:], d["v_experts"][:, bass.ds(i * NJ + j, 1), :].rearrange("p a n -> p (a n)")).then_inc(v_in[j], 16)

                load_first(0)
                load_v(0)
                with sync.Fori(1, TURNS) as i:
                    load_first(i)
                    load_v(i)

            @block.tensor
            def _(pe):
                pe.wait_ge(n2_in, 16)
                with pe.Fori(0, TURNS) as i:
                    for j in range(NJ):
                        pe.wait_ge(u_in[j], i * 16 + 16)
                        pe.wait_ge(gelu_done[(j - 2) % NJ], i + 1 + (j >= 2))
                        for c in range(2):
                            for k in range(KD):
                                mm = pe.matmul(hid_ps[j % 2][:, c * HALF:(c + 1) * HALF], uT[j][:, k, :],
                                               n2T[:, k, c * HALF:(c + 1) * HALF], start=(k == 0), stop=(k == KD - 1))
                        mm.then_inc(hid_mm[j], 1)
                    for b0 in range(0, TILES, NOUT):
                        for js in (range(NJ - 1), range(NJ - 1, NJ)):
                            for b in range(NOUT):
                                t, c = divmod(b0 + b, 2)
                                if js[0] == 0:
                                    pe.wait_ge(out_taken[b], i * USES + b0 // NOUT + 1)
                                for j in js:
                                    if b0 == 0 and b == 0:
                                        pe.wait_ge(weight_ready[j], i + 2)
                                        pe.wait_ge(v_in[j], i * 16 + 16)
                                    mm = pe.matmul(out_ps[b][:], weight[j][:, t * P:(t + 1) * P], v[j][:, c * HALF:(c + 1) * HALF],
                                                   start=(j == 0), stop=(j == NJ - 1))
                                if js[-1] == NJ - 1:
                                    mm.then_inc(out_mm[b], 1)

            @block.scalar
            def _(act):
                for j in range(NJ):
                    act.sem_inc(gelu_done[j], 1)
                with act.Fori(0, TURNS) as i:
                    for j in range(NJ):
                        act.wait_ge(hid_mm[j], i + 1)
                        act.wait_ge(weight_ready[(j - 2) % NJ], i + 1 + (j >= 2))
                        act.activation(hidden[j % 2][:], hid_ps[j % 2][:], ACT.Gelu).then_inc(gelu_done[j], 1)

            @block.vector
            def _(dve):
                dve.memset(acc[:], 0.0).then_inc(zeroed, 1)
                dve.wait_ge(zeroed, 1)
                for j in range(NJ):
                    dve.sem_inc(weight_ready[j], 1)
                for b in range(NOUT):
                    dve.sem_inc(out_taken[b], 1)
                with dve.Fori(0, TURNS) as i:
                    for j in range(NJ):
                        dve.wait_ge(gelu_done[j], i + 2)
                        dve.wait_ge(gate_in[j], i * 16 + 16)
                        dve.wait_ge(out_taken[LAST], i * USES + 1)
                        dve.tensor_tensor(weight[j][:], hidden[j % 2][:], gate[j][:], ALU.mult).then_inc(weight_ready[j], 1)
                    for n in range(TILES):
                        t, c = divmod(n, 2)
                        b = n % NOUT
                        dve.wait_ge(out_mm[b], i * USES + n // NOUT + 1)
                        part = acc[:, t, c * HALF:(c + 1) * HALF]
                        dve.tensor_tensor(part, part, out_ps[b][:], ALU.add).then_inc(out_taken[b], 1)


def peer_finish(nc, d, acc):
    with ExitStack() as stack:
        sp = Space(nc, stack, "fin")
        g2 = sp.sb("g2", [P, D])
        norm_w = sp.sb("norm_w", [P, D])
        eps = sp.sb("eps", [P, 1])
        h = sp.sb("h", [P, TT, D])
        squares = sp.sb("squares", [P, D])
        ss = sp.sb("ss", [P, TT])
        rstd = sp.sb("rstd", [P, TT])
        const_in = sp.sem("const_in")
        h_in = sp.sem("h_in")
        dve_step = sp.sem("dve_step")
        h_ready = sp.sem("h_ready")
        ss_ready = sp.sem("ss_ready")
        root_ready = sp.sem("root_ready")
        out_ready = sp.sem("out_ready")
        stored = sp.sem("stored")
        with nc.Block() as block:
            @block.sync
            def _(sync):
                sync.dma_start(g2[:], d["rows"][5].partition_broadcast(P)).then_inc(const_in, 16)
                sync.dma_start(norm_w[:], d["final_norm_w"].partition_broadcast(P)).then_inc(const_in, 16)
                sync.dma_start(eps[:], d["eps"][0].rearrange("(p a) -> p a", a=1)).then_inc(const_in, 16)
                sync.dma_start(h[:], d["h"].rearrange("t p n -> p t n")).then_inc(const_in, 16)
                for t in range(TT):
                    sync.wait_ge(out_ready, t + 1)
                    sync.dma_start(d["out"][t * P:(t + 1) * P, :], h[:, t, :]).then_inc(stored, 16)
                sync.wait_ge(stored, 16 * TT)

            @block.vector
            def _(dve):
                dve.wait_ge(const_in, 64)
                st = Steps(dve, dve_step)
                st.of(dve.tensor_scalar(norm_w[:], norm_w[:], math.sqrt(D), None, ALU.mult))
                for t in range(TT):
                    st.of(dve.tensor_tensor(acc[:, t, :], acc[:, t, :], g2[:], ALU.mult))
                    st.wait()
                    dve.tensor_tensor(h[:, t, :], h[:, t, :], acc[:, t, :], ALU.add).then_inc(h_ready, 1)
                dve.wait_ge(root_ready, 1)
                st.of(dve.reciprocal(rstd[:], ss[:]))
                st.wait()
                for t in range(TT):
                    dve.scalar_tensor_tensor(h[:, t, :], h[:, t, :], rstd[:, t:t + 1], norm_w[:], ALU.mult, ALU.mult).then_inc(out_ready, 1)

            @block.scalar
            def _(act):
                act.wait_ge(const_in, 64)
                for t in range(TT):
                    act.wait_ge(h_ready, t + 1)
                    act.activation(squares[:], h[:, t, :], ACT.Square, accum_out=ss[:, t:t + 1]).then_inc(ss_ready, 1)
                    act.wait_ge(ss_ready, t + 1)
                act.activation(ss[:], ss[:], ACT.Sqrt, bias=eps[:]).then_inc(root_ready, 1)


OFF_XBC, OFF_DT = DI, DI + CONV_TILES * P
OFF_Q = OFF_DT + SH
OFF_V = OFF_Q + 2 * D
OFF_END = OFF_V + D + 2 * D


def layouts(a):
    c = np.ascontiguousarray
    w_in = a["w_in"][0]
    ch = np.concatenate([w_in[:, OFF_Q:OFF_V], w_in[:, OFF_XBC:OFF_DT]], axis=1)
    conv = np.concatenate([a["conv_w"][0], a["conv_b"]], axis=0)
    out = {
        "x": a["x"][0], "cT": c(a["c"].reshape(KD, P).T), "ada_w": a["ada_w"][0], "ada_b": a["ada_b"],
        "norm1_w": a["norm1_w"], "norm2_w": a["norm2_w"],
        "w_ch": c(ch.reshape(KD, P, -1, P).transpose(2, 1, 0, 3)),
        "conv_w": c(conv.reshape(5, CONV_TILES, P).transpose(2, 1, 0)),
        "w_tok": c(np.concatenate([w_in[:, :DI], w_in[:, OFF_V:OFF_END]], axis=1)),
        "w_dt": c(w_in[:, OFF_DT:OFF_Q]), "dt_bias": a["dt_bias"][0],
        "ident": np.eye(P, dtype=np.float32),
        "eps": np.tile(np.array([[D], [GW], [P]], np.float32) * np.float32(EPS), (1, P)),
    }
    b, n = np.arange(NB), np.arange(P)
    out |= {
        "pos": a["positions"][0], "pos_q": c(a["positions"][0].reshape(-1, 4).T), "rel_bias": a["rel_bias"],
        "first": np.tile(np.where(b == 0, -2.0 ** 30, bucket_starts()).astype(np.float32), 4),
        "causal": np.where(n[None, :] <= n[:, None], 0, -1e30).astype(np.float32),
        "attn_norm_w": a["attn_norm_w"][0],
        "w_pq": c(a["peer_wq"][0].reshape(KD, P, PH, P).transpose(2, 1, 0, 3)),
        "key1T": c(a["peer_key1"][0].transpose(0, 2, 1)), "key2T": c(a["peer_key2"][0].transpose(0, 2, 1)),
        "iota": np.arange(NK, dtype=np.float32),
        "uT": c(a["peer_u"][0].reshape(NK, NK, KD, P).transpose(1, 3, 2, 0)),
        "v_experts": a["peer_v"][0].reshape(NK, NK, D), "final_norm_w": a["final_norm_w"],
        "w_ssd_o": a["w_ssd_o"][0], "w_attn_o": a["w_attn_o"][0], "w_out": a["w_out"][0],
        "upto": (n[:, None] <= n[None, :]).astype(np.float32), "after": (n[:, None] > n[None, :]).astype(np.float32),
        "ssd_norm_w": c(a["ssd_norm_w"][0].reshape(-1, P).T), "d_skip": a["d_skip"][0], "a_log": a["a_log"][0],
        "lambdas": np.stack([a["lambda_q1"][0], a["lambda_k1"][0], a["lambda_q2"][0], a["lambda_k2"][0]]),
    }
    return out


_SCRATCH = {
    "rows": (6, D), "qkT": (2 * AH, P, S), "xbcT": (CONV_TILES, P, S), "z": (TT, P, DI), "v": (TT, P, D),
    "gate": (TT, P, 2 * D), "dt": (TT, P, SH), "bias": (S, AH, S), "ynT": (DI // P, P, S), "attT": (KD, P, S),
    "h": (TT, P, D), "n2T": (KD, P, S), "chosenT": (3, P, S), "gates": (NK, NK, S),
}


def hybrid_block(nc, d):
    stage_modulation(nc, d)
    stage_rel_bias(nc, d)
    stage_project(nc, d)
    stage_ssd(nc, d)
    stage_attention(nc, d)
    stage_merge(nc, d)
    stage_peer_topk(nc, d)
    stage_peer_gates(nc, d)
    stage_peer_mix(nc, d)


def kernel(**inputs):
    import concourse.bacc as _bacc
    from concourse.bass_utils import run_bass_kernel_spmd as _run

    nc = _bacc.Bacc("TRN2", target_bir_lowering=False, num_devices=1)
    arrays, d = {}, {}
    for name, a in layouts({k: np.asarray(v) for k, v in inputs.items()}).items():
        a = np.ascontiguousarray(a)
        arrays[f"in_{name}"] = a
        d[name] = nc.dram_tensor(f"in_{name}", a.shape, mybir.dt.from_np(a.dtype), kind="ExternalInput").ap()
    for name, shape in _SCRATCH.items():
        d[name] = nc.dram_tensor(f"scratch_{name}", shape, F32, kind="Internal").ap()
    out = nc.dram_tensor("out_0", (S, D), F32, kind="ExternalOutput").ap()
    d["out"] = out
    hybrid_block(nc, d)
    r = _run(nc, [arrays], core_ids=[0])
    return r.results[0]["out_0"].reshape(1, S, D)
```

```python
import math
from contextlib import ExitStack

import numpy as np

import concourse.bass as bass
from concourse import mybir

F32 = mybir.dt.float32
F32R = mybir.dt.float32r
I32 = mybir.dt.int32
U32 = mybir.dt.uint32
BF16 = mybir.dt.bfloat16
ALU = mybir.AluOpType
ACT = mybir.ActivationFunctionType
AX = mybir.AxisListType

P = 128
S = 1024
D = 1024
TT = S // P
KD = D // P
HALF = 512
DI = 2048
SH = 32
G = 8
HPG = SH // G
HD = DI // SH
GW = DI // G
CONV_TILES = 32
AH = 8
NB = 32
PH = 8
NK = 128
TOPK = 16
EPS = 1e-6
HEAD_SCALE = 64 ** -0.5
LAMBDA_INIT = 0.8 - 0.6 * math.exp(-0.3 * 0)
FINFO_MIN = -3.0e38


PARTS = ((0, 0), (0, 1), (1, 0))


class Steps:

    def __init__(self, eng, sem, base=0):
        self.eng, self.sem, self.base, self.n = eng, sem, base, 0

    def of(self, ins):
        ins.then_inc(self.sem, 1)
        self.n += 1

    def wait(self):
        self.eng.wait_ge(self.sem, self.base + self.n)


class Space:

    def __init__(self, nc, stack, stage):
        self.nc, self.stack, self.stage = nc, stack, stage
        self.sems = []
        stack.callback(self.clear)

    def clear(self):
        if self.sems:
            self.nc.clear_and_free_semaphores(self.sems)
            self.nc.all_engine_barrier()

    def sb(self, name, shape, dt=F32):
        return self.stack.enter_context(self.nc.sbuf_tensor(f"{self.stage}_{name}", shape, dt))

    def ps(self, name, shape, dt=F32):
        return self.stack.enter_context(self.nc.psum_tensor(f"{self.stage}_{name}", shape, dt))

    def sem(self, name):
        self.sems.append(self.nc.alloc_semaphore(f"{self.stage}_{name}"))
        return self.sems[-1]


def bucket_starts(max_distance=128):
    exact = NB // 2
    return [b if b <= exact else math.ceil(exact * (max_distance / exact) ** ((b - exact) / (NB - exact)))
            for b in range(NB)]


def stage_modulation_and_bias(nc, d):
    QG = 4
    QB = 16
    NJ = QB // QG
    NBUF = 4
    N = P // QB // NBUF
    ROWS = 6
    with ExitStack() as stack:
        sp = Space(nc, stack, "mr")
        cT = sp.sb("cT", [P, KD])
        silu_c = sp.sb("silu_c", [P, KD])
        w = [sp.sb(f"w{s}", [P, KD, HALF]) for s in range(2)]
        ada_b = sp.sb("ada_b", [1, ROWS * D])
        norm_w = sp.sb("norm_w", [1, 2 * D])
        rows = sp.sb("rows", [1, ROWS * D])
        row_ps = [sp.ps(f"row_ps{s}", [1, HALF]) for s in range(2)]
        c_in = sp.sem("c_in")
        row_consts_in = sp.sem("row_consts_in")
        w_in = [sp.sem(f"w_in{s}") for s in range(2)]
        silu_done = sp.sem("silu_done")
        row_mm = [sp.sem(f"row_mm{s}") for s in range(2)]
        row_taken = [sp.sem(f"row_taken{s}") for s in range(2)]
        scale_step = sp.sem("scale_step")
        rows_out = sp.sem("rows_out")

        pos_k_int = sp.sb("pos_k_int", [P, S], I32)
        pos_q_int = sp.sb("pos_q_int", [P, S // QG], I32)
        pos_k = sp.sb("pos_k", [P, S])
        limit = sp.sb("limit", [P, S // QG])
        first = sp.sb("first", [P, 1])
        table = sp.sb("table", [P, AH])
        before = sp.sb("before", [P, AH])
        diffs_raw = sp.sb("diffs_raw", [P, NJ, P])
        diffs = [sp.sb(f"diffs_{part}", [P, NJ, P], F32R) for part in ("hi", "lo")]
        steps = [sp.sb(f"steps{s}", [P, NJ, S], F32R) for s in range(NBUF)]
        out = [sp.sb(f"out{s}", [P, S]) for s in range(2)]
        acc = [sp.ps(f"acc{s}", [P, S]) for s in range(2)]
        zeroed = sp.sem("zeroed")
        small_in = sp.sem("small_in")
        dve_step = sp.sem("dve_step")
        diffs_ready = sp.sem("diffs_ready")
        steps_ready = [sp.sem(f"steps_ready{b}") for b in range(NBUF)]
        acc_ready = [sp.sem(f"acc_ready{b}") for b in range(NBUF)]
        out_ready = [sp.sem(f"out_ready{s}") for s in range(2)]
        stored = [sp.sem(f"stored{s}") for s in range(2)]

        def query_tiles(eng, turn, chunk=None):
            for n, qt in enumerate(reversed(range(TT))):
                if chunk is not None and n < ROWS:
                    chunk(n)
                with eng.Fori(n * N, n * N + N) as i:
                    turn(i, i + (qt - n) * N, qt)

        with nc.Block() as block:
            @block.sync
            def _(sync):
                sync.dma_start(pos_k_int[:], d["pos"].partition_broadcast(P)).then_inc(small_in, 16)
                sync.dma_start(first[:], d["first"].rearrange("(p a) -> p a", a=1)).then_inc(small_in, 16)
                sync.wait_ge(zeroed, 2)
                for i in range(QG):
                    sync.dma_start(pos_q_int[i * NB:(i + 1) * NB, :], d["pos_q"][i].partition_broadcast(NB)).then_inc(small_in, 16)
                    sync.dma_start(table[i * NB:(i + 1) * NB, :], d["rel_bias"]).then_inc(small_in, 16)
                    sync.dma_start(before[i * NB + 1:(i + 1) * NB, :], d["rel_bias"][0:NB - 1, :]).then_inc(small_in, 16)
                for s in range(2):
                    sync.sem_inc(stored[s], 16)

                def turn(i, g, qt):
                    for b in range(NBUF):
                        s = b % 2
                        sync.wait_ge(out_ready[s], 2 * i + b // 2 + 2)
                        sync.dma_start(d["bias"].rearrange("q h k -> (q h) k")[bass.ds((NBUF * g + b) * P, P), 0:(qt + 1) * P],
                                       out[s][:, 0:(qt + 1) * P]).then_inc(stored[s], 16)

                query_tiles(sync, turn)
                sync.wait_ge(scale_step, 4)
                for s in range(2):
                    sync.wait_ge(row_taken[s], ROWS)
                sync.dma_start(d["rows"].rearrange("v n -> (v n)").rearrange("(a n) -> a n", a=1),
                               rows[:]).then_inc(rows_out, 16)
                sync.wait_ge(rows_out, 16)
                for s in range(2):
                    sync.wait_ge(stored[s], (TT * N * NBUF // 2 + 1) * 16)

            @block.gpsimd
            def _(pool):
                ada_w = d["ada_w"].rearrange("(k p) n -> p k n", p=P)
                pool.dma_start(cT[:], d["cT"]).then_inc(c_in, 16)
                for n in range(ROWS):
                    for s in range(2):
                        if n > 0:
                            pool.wait_ge(row_mm[s], n)
                        pool.dma_start(w[s][:], ada_w[:, :, (2 * n + s) * HALF:(2 * n + s + 1) * HALF]).then_inc(w_in[s], 16)
                    if n == 0:
                        pool.dma_start(ada_b[:], d["ada_b"]).then_inc(row_consts_in, 16)
                        pool.dma_start(norm_w[:, 0:D], d["norm1_w"]).then_inc(row_consts_in, 16)
                        pool.dma_start(norm_w[:, D:2 * D], d["norm2_w"]).then_inc(row_consts_in, 16)

            @block.vector
            def _(dve):
                dve.memset(before[:], 0.0).then_inc(zeroed, 1)
                dve.memset(diffs_raw[:], 0.0).then_inc(zeroed, 1)
                st = Steps(dve, dve_step)
                dve.wait_ge(zeroed, 2)
                dve.wait_ge(small_in, 16 * (2 + 3 * QG))
                st.of(dve.tensor_tensor(table[:], table[:], before[:], ALU.subtract))
                st.of(dve.tensor_copy(pos_k[:], pos_k_int[:]))
                st.of(dve.tensor_copy(limit[:], pos_q_int[:]))
                st.wait()
                st.of(dve.tensor_scalar(limit[:], limit[:], first[:], None, ALU.subtract))
                for j in range(NJ):
                    for i in range(QG):
                        col = (j * QG + i) * AH
                        st.of(dve.tensor_copy(diffs_raw[i * NB:(i + 1) * NB, j, col:col + AH], table[i * NB:(i + 1) * NB, :]))
                st.wait()
                st.of(dve.tensor_copy(diffs[0][:], diffs_raw[:]))
                st.wait()
                dve.tensor_tensor(diffs[1][:], diffs_raw[:], diffs[0][:].bitcast(F32), ALU.subtract).then_inc(diffs_ready, 1)
                for b in range(NBUF):
                    dve.sem_inc(acc_ready[b], 1)

                def turn(i, g, qt):
                    ext = (qt + 1) * P
                    for b in range(NBUF):
                        dve.wait_ge(acc_ready[b], i + 1)
                        for j in range(NJ):
                            ins = dve.tensor_scalar(steps[b][:, j, 0:ext], pos_k[:, 0:ext],
                                                    limit[:, bass.ds((NBUF * g + b) * NJ + j, 1)], None, ALU.is_le)
                        ins.then_inc(steps_ready[b], 1)

                def take_row(n):
                    for s in range(2):
                        part = slice((2 * n + s) * HALF, (2 * n + s + 1) * HALF)
                        dve.wait_ge(row_mm[s], n + 1)
                        dve.tensor_tensor(rows[:, part], row_ps[s][:], ada_b[:, part], ALU.add).then_inc(row_taken[s], 1)

                def chunk(n):
                    if n == 0:
                        dve.wait_ge(row_consts_in, 48)
                    else:
                        take_row(n - 1)

                query_tiles(dve, turn, chunk)
                take_row(ROWS - 1)
                for s in range(2):
                    dve.wait_ge(row_taken[s], ROWS)
                for n, v in enumerate((1, 4)):
                    row = rows[:, v * D:(v + 1) * D]
                    dve.tensor_scalar(row, row, 1.0, math.sqrt(D), ALU.add, ALU.mult).then_inc(scale_step, 1)
                    dve.wait_ge(scale_step, 2 * n + 1)
                    dve.tensor_tensor(row, row, norm_w[:, n * D:(n + 1) * D], ALU.mult).then_inc(scale_step, 1)

            @block.tensor
            def _(pe):
                def turn(i, g, qt):
                    ext = (qt + 1) * P
                    if qt == TT - 1:
                        pe.wait_ge(diffs_ready, 1)
                    for b in range(NBUF):
                        s = b % 2
                        pe.wait_ge(steps_ready[b], i + 1)
                        pe.wait_ge(out_ready[s], 2 * i + b // 2 + 1)
                        for c in range(0, ext, HALF):
                            e = min(c + HALF, ext)
                            for j in range(NJ):
                                for part in range(2):
                                    mm = pe.matmul(acc[s][:, c:e], diffs[part][:, j, :], steps[b][:, j, c:e],
                                                   start=(j == 0 and part == 0), stop=(j == NJ - 1 and part == 1))
                        mm.then_inc(acc_ready[b], 1)

                def chunk(n):
                    if n == 0:
                        pe.wait_ge(silu_done, 1)
                    for s in range(2):
                        pe.wait_ge(w_in[s], n * 16 + 16)
                        if n > 0:
                            pe.wait_ge(row_taken[s], n)
                        for k in range(KD):
                            mm = pe.matmul(row_ps[s][:], silu_c[:, k:k + 1], w[s][:, k, :], start=(k == 0), stop=(k == KD - 1))
                        mm.then_inc(row_mm[s], 1)

                query_tiles(pe, turn, chunk)

            @block.scalar
            def _(act):
                act.wait_ge(c_in, 16)
                act.activation(silu_c[:], cT[:], ACT.Silu).then_inc(silu_done, 1)
                for s in range(2):
                    act.sem_inc(out_ready[s], 1)

                def turn(i, g, qt):
                    for b in range(NBUF):
                        s = b % 2
                        act.wait_ge(acc_ready[b], i + 2)
                        act.wait_ge(stored[s], (2 * i + b // 2 + 1) * 16)
                        act.activation(out[s][:, 0:(qt + 1) * P], acc[s][:, 0:(qt + 1) * P], ACT.Copy).then_inc(out_ready[s], 1)

                query_tiles(act, turn)


def stage_project(nc, d):
    with ExitStack() as stack:
        sp = Space(nc, stack, "proj")
        n1T = [sp.sb(f"n1T_{part}", [P, KD, S], F32R) for part in ("hi", "lo")]
        w_ch = [sp.sb(f"w_ch{s}", [P, KD, P]) for s in range(2)]
        w_tok = [sp.sb(f"w_tok{s}", [P, KD, HALF]) for s in range(2)]
        w_dt = sp.sb("w_dt", [P, KD, SH])
        norm_rows_to_transposed(nc, d, n1T, w_ch)
        project_channel_major(nc, d, n1T, w_ch, w_tok, w_dt)
        project_token_major(nc, d, n1T, w_tok, w_dt)


def norm_rows_to_transposed(nc, d, n1T, w_ch):
    with ExitStack() as stack:
        sp = Space(nc, stack, "n1")
        ident = sp.sb("ident", [P, P])
        scale_row = sp.sb("scale_row", [P, D])
        shift_row = sp.sb("shift_row", [P, D])
        x = [sp.sb(f"x{t}", [P, D]) for t in range(TT)]
        squares = sp.sb("squares", [P, D])
        eps = sp.sb("eps", [P, 1])
        ss = sp.sb("ss", [P, TT])
        rstd = sp.sb("rstd", [P, TT])
        turned = [sp.ps(f"turned{s}", [P, KD, P]) for s in range(2)]
        const_in = sp.sem("const_in")
        eps_in = sp.sem("eps_in")
        w_in = sp.sem("w_in")
        x_in = [sp.sem(f"x_in{t}") for t in range(TT)]
        ss_done = sp.sem("ss_done")
        root_done = sp.sem("root_done")
        rstd_done = sp.sem("rstd_done")
        scaled = sp.sem("scaled")
        n1_ready = sp.sem("n1_ready")
        turned_ready = sp.sem("turned_ready")
        turned_hi = sp.sem("turned_hi")
        turned_out = sp.sem("turned_out")
        with nc.Block() as block:
            @block.sync
            def _(sync):
                for t in range(TT):
                    sync.dma_start(x[t][:], d["x"][t * P:(t + 1) * P, :]).then_inc(x_in[t], 16)
                    if t == 0:
                        sync.dma_start(eps[:], d["eps"][0].rearrange("(p a) -> p a", a=1)).then_inc(eps_in, 16)
                sync.dma_start(scale_row[:], d["rows"][1].partition_broadcast(P)).then_inc(const_in, 16)
                sync.dma_start(shift_row[:], d["rows"][0].partition_broadcast(P)).then_inc(const_in, 16)
                sync.dma_start(ident[:], d["ident"]).then_inc(const_in, 16)
                for s in range(2):
                    sync.dma_start(w_ch[s][:], d["w_ch"][s]).then_inc(w_in, 16)
                sync.wait_ge(w_in, 32)

            @block.scalar
            def _(act):
                act.wait_ge(eps_in, 16)
                for t in range(TT):
                    act.wait_ge(x_in[t], 16)
                    act.activation(squares[:], x[t][:], ACT.Square, accum_out=ss[:, t:t + 1]).then_inc(ss_done, 1)
                    act.wait_ge(ss_done, t + 1)
                act.activation(ss[:], ss[:], ACT.Sqrt, bias=eps[:]).then_inc(root_done, 1)
                for t in range(TT):
                    act.wait_ge(turned_ready, t + 1)
                    act.activation(n1T[0][:, :, t * P:(t + 1) * P], turned[t % 2][:], ACT.Copy).then_inc(turned_hi, 1)

            @block.vector
            def _(dve):
                dve.wait_ge(const_in, 48)
                dve.wait_ge(root_done, 1)
                dve.reciprocal(rstd[:], ss[:]).then_inc(rstd_done, 1)
                dve.wait_ge(rstd_done, 1)

                def low(t):
                    cols = slice(t * P, (t + 1) * P)
                    dve.wait_ge(turned_hi, t + 1)
                    dve.tensor_tensor(n1T[1][:, :, cols], turned[t % 2][:], n1T[0][:, :, cols].bitcast(F32),
                                      ALU.subtract).then_inc(turned_out, 1)

                for t in range(TT):
                    dve.scalar_tensor_tensor(x[t][:], x[t][:], rstd[:, t:t + 1], scale_row[:], ALU.mult, ALU.mult).then_inc(scaled, 1)
                    if t >= 2:
                        low(t - 2)
                for t in (TT - 2, TT - 1):
                    low(t)

            @block.gpsimd
            def _(pool):
                pool.wait_ge(const_in, 48)
                for t in range(TT):
                    pool.wait_ge(scaled, t + 1)
                    pool.tensor_tensor(x[t][:], x[t][:], shift_row[:], ALU.add).then_inc(n1_ready, 1)

            @block.tensor
            def _(pe):
                pe.wait_ge(const_in, 48)
                for t in range(TT):
                    pe.wait_ge(n1_ready, t + 1)
                    if t >= 2:
                        pe.wait_ge(turned_out, t - 1)
                    for k in range(KD):
                        mm = pe.transpose(turned[t % 2][:, k, :], x[t][:, k * P:(k + 1) * P], ident[:])
                    mm.then_inc(turned_ready, 1)


def project_channel_major(nc, d, n1T, w_raw, w_tok, w_dt):
    with ExitStack() as stack:
        sp = Space(nc, stack, "pc")
        w = [[sp.sb(f"w{s}_{part}", [P, KD, P], F32R) for part in ("hi", "lo")] for s in range(2)]
        conv_w = sp.sb("conv_w", [P, CONV_TILES, 5])
        u = [sp.sb(f"u{s}", [P, S + 3]) for s in range(2)]
        y = [sp.sb(f"y{s}", [P, S]) for s in range(2)]
        out = [sp.sb(f"out{s}", [P, S]) for s in range(2)]
        acc = [sp.ps(f"acc{s}", [P, S]) for s in range(2)]
        conv_in = sp.sem("conv_in")
        later_in = sp.sem("later_in")
        w_in = [sp.sem(f"w_in{s}") for s in range(2)]
        w_hi = [sp.sem(f"w_hi{s}") for s in range(2)]
        w_lo = [sp.sem(f"w_lo{s}") for s in range(2)]
        acc_ready = [sp.sem(f"acc_ready{s}") for s in range(2)]
        acc_out = [sp.sem(f"acc_out{s}") for s in range(2)]
        padded = sp.sem("padded")
        dve_step = sp.sem("dve_step")
        y_ready = [sp.sem(f"y_ready{s}") for s in range(2)]
        out_ready = [sp.sem(f"out_ready{s}") for s in range(2)]
        stored = [sp.sem(f"stored{s}") for s in range(2)]
        DIRECT = [("qkT", 0, AH // 2, ACT.Copy, HEAD_SCALE), ("qkT", AH, AH // 2, ACT.Copy, 1.0),
                  ("gateT", 0, KD, ACT.Sigmoid, 1.0)]
        NQ, NC = sum(x[2] for x in DIRECT), CONV_TILES // 2
        N = NQ + NC
        with nc.Block() as block:
            @block.gpsimd
            def _(pool):
                pool.dma_start(conv_w[:], d["conv_w"]).then_inc(conv_in, 16)
                with pool.Fori(1, N) as i:
                    for s in range(2):
                        pool.wait_ge(w_lo[s], i)
                        pool.dma_start(w_raw[s][:], d["w_ch"][2 * i + s]).then_inc(w_in[s], 16)
                pool.dma_start(w_dt[:], d["w_dt"].rearrange("(k p) n -> p k n", p=P)).then_inc(later_in, 16)
                for s in range(2):
                    pool.dma_start(w_tok[s][:], d["w_tok"].rearrange("(k p) n -> p k n", p=P)[:, :, s * HALF:(s + 1) * HALF]).then_inc(later_in, 16)
                pool.wait_ge(later_in, 48)

            @block.sync
            def _(sync):
                for s in range(2):
                    sync.sem_inc(stored[s], 16)
                first = 0
                for name, at, turns, _, _ in DIRECT:
                    with sync.Fori(first, first + turns) as i:
                        for s in range(2):
                            sync.wait_ge(acc_out[s], i + 2)
                            sync.dma_start(d[name][2 * (i - first) + s + at], out[s][:]).then_inc(stored[s], 16)
                    first += turns
                with sync.Fori(0, NC) as i:
                    for s in range(2):
                        sync.wait_ge(out_ready[s], i + 2)
                        sync.dma_start(d["xbcT"][2 * i + s], out[s][:]).then_inc(stored[s], 16)
                for s in range(2):
                    sync.wait_ge(stored[s], 16 * (1 + N))

            @block.tensor
            def _(pe):
                with pe.Fori(0, N) as i:
                    for s in range(2):
                        pe.wait_ge(w_lo[s], i + 1)
                        pe.wait_ge(acc_out[s], i + 1)
                        for c in range(2):
                            for k in range(KD):
                                for a, b in PARTS:
                                    mm = pe.matmul(acc[s][:, c * HALF:(c + 1) * HALF], w[s][a][:, k, :],
                                                   n1T[b][:, k, c * HALF:(c + 1) * HALF],
                                                   start=(k == 0 and a + b == 0), stop=(k == KD - 1 and a == 1))
                        mm.then_inc(acc_ready[s], 1)

            @block.scalar
            def _(act):
                def split(i, s):
                    if not (isinstance(i, int) and i == 0):
                        act.wait_ge(w_in[s], i * 16)
                    act.activation(w[s][0][:], w_raw[s][:], ACT.Copy).then_inc(w_hi[s], 1)

                for s in range(2):
                    act.sem_inc(acc_out[s], 1)
                    split(0, s)
                first = 0
                for _, _, turns, func, scale in DIRECT:
                    with act.Fori(first, first + turns) as i:
                        for s in range(2):
                            act.wait_ge(acc_ready[s], i + 1)
                            act.wait_ge(stored[s], i * 16 + 16)
                            act.activation(out[s][:], acc[s][:], func, scale=scale).then_inc(acc_out[s], 1)
                            split(i + 1, s)
                    first += turns
                act.wait_ge(padded, 2)
                for s in range(2):
                    act.wait_ge(acc_ready[s], NQ + 1)
                    act.activation(u[s][:, 3:S + 3], acc[s][:], ACT.Copy).then_inc(acc_out[s], 1)
                    split(NQ + 1, s)

                def conv_turn(i, last):
                    for s in range(2):
                        act.wait_ge(y_ready[s], i + 1)
                        act.wait_ge(acc_ready[s], i + NQ + 2)
                        act.activation(u[s][:, 3:S + 3], acc[s][:], ACT.Copy).then_inc(acc_out[s], 1)
                        if not last:
                            split(i + NQ + 2, s)
                        act.wait_ge(stored[s], i * 16 + NQ * 16 + 16)
                        act.activation(out[s][:], y[s][:], ACT.Silu).then_inc(out_ready[s], 1)

                with act.Fori(0, NC - 2) as i:
                    conv_turn(i, False)
                conv_turn(NC - 2, True)
                for s in range(2):
                    act.wait_ge(y_ready[s], NC)
                    act.wait_ge(stored[s], N * 16)
                    act.activation(out[s][:], y[s][:], ACT.Silu).then_inc(out_ready[s], 1)

            @block.vector
            def _(dve):
                def split(i, s):
                    dve.wait_ge(w_hi[s], i + 1)
                    dve.tensor_tensor(w[s][1][:], w_raw[s][:], w[s][0][:].bitcast(F32), ALU.subtract).then_inc(w_lo[s], 1)

                for s in range(2):
                    dve.sem_inc(out_ready[s], 1)
                    split(0, s)
                for s in range(2):
                    dve.memset(u[s][:, 0:3], 0.0).then_inc(padded, 1)
                dve.wait_ge(conv_in, 16)
                dve.wait_ge(padded, 2)
                with dve.Fori(0, NQ) as i:
                    for s in range(2):
                        split(i + 1, s)

                def conv_turn(i, last):
                    for s in range(2):
                        st = Steps(dve, dve_step, i * 6 + 3 * s)
                        cw = conv_w[:, bass.ds(2 * i + s, 1), :].rearrange("p a b -> p (a b)")
                        if not last:
                            split(i + NQ + 1, s)
                        dve.wait_ge(acc_out[s], i + NQ + 2)
                        dve.wait_ge(out_ready[s], i + 1)
                        st.of(dve.tensor_scalar(y[s][:], u[s][:, 3:S + 3], cw[:, 3:4], cw[:, 4:5], ALU.mult, ALU.add))
                        for j in range(3):
                            st.wait()
                            tap = dve.scalar_tensor_tensor(y[s][:], u[s][:, j:S + j], cw[:, j:j + 1], y[s][:], ALU.mult, ALU.add)
                            if j < 2:
                                st.of(tap)
                        tap.then_inc(y_ready[s], 1)

                with dve.Fori(0, NC - 1) as i:
                    conv_turn(i, False)
                conv_turn(NC - 1, True)


def project_token_major(nc, d, n1T, w_raw, w_dt_raw):
    with ExitStack() as stack:
        sp = Space(nc, stack, "pt")
        NBUF = 4
        w = [[sp.sb(f"w{s}_{part}", [P, KD, HALF], F32R) for part in ("hi", "lo")] for s in range(2)]
        w_dt = [sp.sb(f"w_dt_{part}", [P, KD, SH], F32R) for part in ("hi", "lo")]
        dt_bias = sp.sb("dt_bias", [P, SH])
        out = [sp.sb(f"out{s}", [P, HALF]) for s in range(NBUF)]
        raw = sp.sb("raw", [P, TT, SH])
        mag = sp.sb("mag", [P, TT, SH])
        dt = sp.sb("dt", [P, TT, SH])
        acc = [sp.ps(f"acc{s}", [P, HALF]) for s in range(NBUF)]
        acc_dt = sp.ps("acc_dt", [P, TT, SH])
        small_in = sp.sem("small_in")
        w_in = [sp.sem(f"w_in{s}") for s in range(2)]
        w_hi = [sp.sem(f"w_hi{s}") for s in range(2)]
        w_lo = [sp.sem(f"w_lo{s}") for s in range(2)]
        dt_hi = sp.sem("dt_hi")
        dt_lo = sp.sem("dt_lo")
        acc_ready = [sp.sem(f"acc_ready{s}") for s in range(NBUF)]
        out_ready = [sp.sem(f"out_ready{s}") for s in range(NBUF)]
        stored = [sp.sem(f"stored{s}") for s in range(NBUF)]
        dt_ready = sp.sem("dt_ready")
        dt_step = sp.sem("dt_step")
        mag_step = sp.sem("mag_step")
        dt_stored = sp.sem("dt_stored")
        OUTS = [("z", 2, ACT.Silu), ("v", 1, ACT.Copy)]
        TURNS = sum(n for _, n, _ in OUTS)
        USES = 2 * TT // NBUF
        with nc.Block() as block:
            @block.gpsimd
            def _(pool):
                w_tok = d["w_tok"].rearrange("(k p) n -> p k n", p=P)
                pool.dma_start(dt_bias[:], d["dt_bias"].partition_broadcast(P)).then_inc(small_in, 16)
                with pool.Fori(1, TURNS) as i:
                    for s in range(2):
                        pool.wait_ge(w_lo[s], i)
                        pool.dma_start(w_raw[s][:], w_tok[:, :, bass.ds((2 * i + s) * HALF, HALF)]).then_inc(w_in[s], 16)
                pool.wait_ge(dt_step, 3)
                pool.dma_start(d["dt"].rearrange("t p n -> p t n"), dt[:]).then_inc(dt_stored, 16)
                pool.wait_ge(dt_stored, 16)

            @block.tensor
            def _(pe):
                pe.wait_ge(dt_lo, 1)
                for t in range(TT):
                    for k in range(KD):
                        for a, b in PARTS:
                            mm = pe.matmul(acc_dt[:, t, :], n1T[a][:, k, t * P:(t + 1) * P], w_dt[b][:, k, :],
                                           start=(k == 0 and a + b == 0), stop=(k == KD - 1 and a == 1))
                mm.then_inc(dt_ready, 1)
                with pe.Fori(0, TURNS) as i:
                    for s in range(2):
                        pe.wait_ge(w_lo[s], i + 1)
                        for t in range(TT):
                            n = s * TT + t
                            buf = n % NBUF
                            pe.wait_ge(out_ready[buf], i * USES + n // NBUF + 1)
                            for k in range(KD):
                                for a, b in PARTS:
                                    mm = pe.matmul(acc[buf][:], n1T[a][:, k, t * P:(t + 1) * P], w[s][b][:, k, :],
                                                   start=(k == 0 and a + b == 0), stop=(k == KD - 1 and a == 1))
                            mm.then_inc(acc_ready[buf], 1)

            @block.scalar
            def _(act):
                def split(i, s):
                    if not (isinstance(i, int) and i == 0):
                        act.wait_ge(w_in[s], i * 16)
                    act.activation(w[s][0][:], w_raw[s][:], ACT.Copy).then_inc(w_hi[s], 1)

                act.activation(w_dt[0][:], w_dt_raw[:], ACT.Copy).then_inc(dt_hi, 1)
                for b in range(NBUF):
                    act.sem_inc(out_ready[b], 1)
                for s in range(2):
                    split(0, s)

                def turn(i, func, last):
                    for n in range(2 * TT):
                        b = n % NBUF
                        act.wait_ge(acc_ready[b], i * USES + n // NBUF + 1)
                        act.wait_ge(stored[b], (i * USES + n // NBUF + 1) * 16)
                        act.activation(out[b][:], acc[b][:], func).then_inc(out_ready[b], 1)
                        if (n + 1) % TT == 0 and not last:
                            split(i + 1, n // TT)

                first = 0
                for name, turns, func in OUTS:
                    ends = first + turns == TURNS
                    if turns - ends:
                        with act.Fori(first, first + turns - ends) as i:
                            turn(i, func, False)
                    if ends:
                        turn(TURNS - 1, func, True)
                    first += turns
                act.wait_ge(dt_step, 1)
                act.activation(mag[:], raw[:], ACT.Abs).then_inc(mag_step, 1)
                act.wait_ge(mag_step, 1)
                act.activation(mag[:], mag[:], ACT.Exp, scale=-1.0).then_inc(mag_step, 1)
                act.wait_ge(mag_step, 2)
                act.activation(mag[:], mag[:], ACT.Ln, bias=1.0).then_inc(mag_step, 1)

            @block.sync
            def _(sync):
                for b in range(NBUF):
                    sync.sem_inc(stored[b], 16)
                first = 0
                for name, turns, func in OUTS:
                    with sync.Fori(first, first + turns) as i:
                        for n in range(2 * TT):
                            b = n % NBUF
                            sync.wait_ge(out_ready[b], i * USES + n // NBUF + 2)
                            sync.dma_start(d[name][n % TT, :, bass.ds((2 * (i - first) + n // TT) * HALF, HALF)],
                                           out[b][:]).then_inc(stored[b], 16)
                    first += turns
                for b in range(NBUF):
                    sync.wait_ge(stored[b], (TURNS * USES + 1) * 16)

            @block.vector
            def _(dve):
                def split(i, s):
                    dve.wait_ge(w_hi[s], i + 1)
                    dve.tensor_tensor(w[s][1][:], w_raw[s][:], w[s][0][:].bitcast(F32), ALU.subtract).then_inc(w_lo[s], 1)

                dve.wait_ge(dt_hi, 1)
                dve.tensor_tensor(w_dt[1][:], w_dt_raw[:], w_dt[0][:].bitcast(F32), ALU.subtract).then_inc(dt_lo, 1)
                for s in range(2):
                    split(0, s)
                dve.wait_ge(dt_ready, 1)
                dve.wait_ge(small_in, 16)
                dve.tensor_tensor(raw[:], acc_dt[:], dt_bias[:].unsqueeze(1).to_broadcast([P, TT, SH]), ALU.add).then_inc(dt_step, 1)
                with dve.Fori(1, TURNS) as i:
                    for s in range(2):
                        split(i, s)
                dve.wait_ge(mag_step, 1)
                dve.tensor_scalar(raw[:], raw[:], 0.0, None, ALU.max).then_inc(dt_step, 1)
                dve.wait_ge(dt_step, 2)
                dve.wait_ge(mag_step, 3)
                dve.tensor_tensor(dt[:], raw[:], mag[:], ALU.add).then_inc(dt_step, 1)


def stage_attention(nc, d):
    ROOT, NORM, TURN = 3, 5, 5
    with ExitStack() as stack:
        sp = Space(nc, stack, "at")
        ident = sp.sb("ident", [P, P])
        causal = sp.sb("causal", [P, P])
        ident_b = sp.sb("ident_b", [P, P], BF16)
        causal_b = sp.sb("causal_b", [P, P], BF16)
        lam_in = sp.sb("lam_in", [P, 4, 64])
        lam_prod = sp.sb("lam_prod", [P, 64])
        lam_sum = sp.sb("lam_sum", [P, 2])
        neg_lam = sp.sb("neg_lam", [P, 1])
        norm_w = sp.sb("norm_w", [P, 1])
        q = [sp.sb(f"q{s}", [P, S]) for s in range(2)]
        k = [sp.sb(f"k{s}", [P, S]) for s in range(2)]
        v = [sp.sb(f"v{s}", [P, TT, P]) for s in range(2)]
        bias = [sp.sb(f"bias{b}", [P, S]) for b in range(2)]
        soft = [[sp.sb(f"soft{b}{i}", [P, S]) for i in range(2)] for b in range(2)]
        top = [sp.sb(f"top{b}", [P, 2]) for b in range(2)]
        neg_top = [sp.sb(f"neg_top{b}", [P, 2]) for b in range(2)]
        total = [sp.sb(f"total{b}", [P, 2]) for b in range(2)]
        share = [sp.sb(f"share{b}", [P, 2]) for b in range(2)]
        diff = [sp.sb(f"diff{b}", [P, S]) for b in range(2)]
        diffT = [sp.sb(f"diffT{b}", [P, S]) for b in range(2)]
        squares = sp.sb("squares", [P, P])
        eps = sp.sb("eps", [P, 1])
        wait_here = sp.sb("wait_here", [1, 4])
        ss = [sp.sb(f"ss{s}", [P, TT]) for s in range(2)]
        rstd = [sp.sb(f"rstd{s}", [P, TT]) for s in range(2)]
        heads_out = [sp.sb(f"heads_out{s}", [P, TT, P]) for s in range(2)]
        outT = [sp.sb(f"outT{s}", [P, S]) for s in range(2)]
        logit_ps = [sp.ps(f"logit_ps{i}", [P, S]) for i in range(2)]
        turn_ps = sp.ps("turn_ps", [P, S])
        av_ps = [sp.ps(f"av_ps{b}", [P, HALF]) for b in range(2)]
        const_in = sp.sem("const_in")
        prep = sp.sem("prep")
        lam_exp = sp.sem("lam_exp")
        qkv_in = [sp.sem(f"qkv_in{s}") for s in range(2)]
        bias_in = [sp.sem(f"bias_in{b}") for b in range(2)]
        logits_mm = [sp.sem(f"logits_mm{i}") for i in range(2)]
        logits_ready = [sp.sem(f"logits_ready{i}") for i in range(2)]
        top_ready = [sp.sem(f"top_ready{i}") for i in range(2)]
        exp_done = [sp.sem(f"exp_done{i}") for i in range(2)]
        dve_step = sp.sem("dve_step")
        diff_ready = sp.sem("diff_ready")
        turned = sp.sem("turned")
        diffT_ready = sp.sem("diffT_ready")
        av_ready = sp.sem("av_ready")
        ss_ready = sp.sem("ss_ready")
        root_ready = sp.sem("root_ready")
        rstd_ready = sp.sem("rstd_ready")
        av_taken = sp.sem("av_taken")
        normed_ready = sp.sem("normed_ready")
        outT_mm = sp.sem("outT_mm")
        outT_ready = sp.sem("outT_ready")
        stored = [sp.sem(f"stored{s}") for s in range(2)]
        TURNS = AH // 2
        PAR = TT // 2

        def pipeline(eng, step):
            for s in range(2):
                for n in range(TT):
                    step(s, s, n, s > 0)
            with eng.Fori(1, TURNS) as i:
                for s in range(2):
                    for n in range(TT):
                        step(2 * i + s, s, n, True)
            for n in range(TURN + 1):
                step(AH, 0, n, True)

        def behind(h, s, n, lag, begun, stage):
            if n >= lag and not (isinstance(h, int) and h == AH):
                stage(h, s, n - lag)
            elif n < lag and begun:
                stage(h - 1, 1 - s, n - lag + TT)

        with nc.Block() as block:
            @block.sync
            def _(sync):
                sync.dma_start(ident[:], d["ident"]).then_inc(const_in, 16)
                sync.dma_start(causal[:], d["causal"]).then_inc(const_in, 16)
                sync.dma_start(norm_w[:], d["attn_norm_w"].rearrange("(p a) -> p a", a=1)).then_inc(const_in, 16)
                sync.dma_start(eps[:], d["eps"][2].rearrange("(p a) -> p a", a=1)).then_inc(const_in, 16)
                for n in range(4):
                    sync.dma_start(lam_in[:, n, :], d["lambdas"][n].partition_broadcast(P)).then_inc(const_in, 16)
                with sync.Fori(0, TURNS) as i:
                    for s in range(2):
                        h = 2 * i + s
                        for qt in range(TT):
                            b, ext = qt % 2, (qt + 1) * P
                            sync.wait_ge(logits_ready[1], h * TT + qt + 1)
                            sync.dma_start(bias[b][:, 0:ext], d["bias"][qt * P:(qt + 1) * P, bass.ds(h, 1), 0:ext].rearrange(
                                "q a k -> q (a k)")).then_inc(bias_in[b], 16)

            @block.gpsimd
            def _(pool):
                def load_head(h, s):
                    pool.dma_start(q[s][:], d["qkT"][h]).then_inc(qkv_in[s], 16)
                    pool.dma_start(k[s][:], d["qkT"][h + AH]).then_inc(qkv_in[s], 16)
                    pool.dma_start(v[s][:], d["v"][:, :, bass.ds(h * P, P)].rearrange("t p n -> p t n")).then_inc(qkv_in[s], 16)

                for s in range(2):
                    load_head(s, s)
                with pool.Fori(0, TURNS - 1) as i:
                    for s in range(2):
                        pool.wait_ge(av_ready, (2 * i + s) * TT + TT + 2)
                        load_head(2 * i + s + 2, s)

            @block.tensor
            def _(pe):
                pe.wait_ge(prep, 3)
                pe.sem_inc(turned, 2)
                pe.sem_inc(av_ready, 2)

                def logits(h, s, n):
                    if n == 0:
                        pe.wait_ge(qkv_in[s], (h - s) * 24 + 48)
                    for half in range(2):
                        pe.wait_ge(logits_ready[half], h * TT + n + 2)
                        rows = slice(half * 64, half * 64 + 64)
                        ext = (n + 1) * P
                        for c in range(0, ext, HALF):
                            e = min(c + HALF, ext)
                            last = e == ext
                            mm = pe.matmul(logit_ps[half][:, c:e], q[s][rows, n * P:ext], k[s][rows, c:e],
                                           start=True, stop=not last)
                        mm = pe.matmul(logit_ps[half][:, ext - P:ext], ident_b[:], causal_b[:], start=False, stop=True)
                        mm.then_inc(logits_mm[half], 1)

                def turn(h, s, n):
                    pe.wait_ge(diff_ready, h * TT + n + 3)
                    pe.wait_ge(diffT_ready, h * TT + n + 1)
                    if n == (TURN + 1) - 2:
                        pe.wait_ge(outT_ready, h + 2)
                    for t in range(n + 1):
                        mm = pe.transpose(turn_ps[:, t * P:(t + 1) * P], diff[n % 2][:, t * P:(t + 1) * P], ident[:])
                    mm.then_inc(turned, 1)

                def times_v(h, s, n):
                    pe.wait_ge(diffT_ready, h * TT + n + 2)
                    pe.wait_ge(av_taken, h * TT + n + 1)
                    for t in range(n + 1):
                        mm = pe.matmul(av_ps[n % 2][:, 0:P], diffT[n % 2][:, t * P:(t + 1) * P], v[s][:, t, :],
                                       start=(t == 0), stop=(t == n))
                    mm.then_inc(av_ready, 1)

                def step(h, s, n, begun):
                    behind(h, s, n, 0, begun, logits)
                    behind(h, s, n, 2, begun, turn)
                    behind(h, s, n, 3, begun, times_v)
                    if n == TURN and begun:
                        over = isinstance(h, int) and h == AH
                        pe.wait_ge(normed_ready, h)
                        pe.wait_ge(diffT_ready, h * TT + 1 if over else h * TT + TURN)
                        for t in range(TT):
                            mm = pe.transpose(turn_ps[:, t * P:(t + 1) * P], heads_out[1 - s][:, t, :], ident[:])
                        mm.then_inc(outT_mm, 1)

                pipeline(pe, step)

            @block.vector
            def _(dve):
                dve.wait_ge(const_in, 16 * 8)
                st = Steps(dve, dve_step)
                dve.tensor_copy(ident_b[:], ident[:]).then_inc(prep, 1)
                dve.tensor_copy(causal_b[:], causal[:]).then_inc(prep, 1)
                for n in range(2):
                    st.of(dve.tensor_tensor(lam_prod[:], lam_in[:, 2 * n, :], lam_in[:, 2 * n + 1, :], ALU.mult))
                    st.wait()
                    st.of(dve.reduce_sum(lam_sum[:, n:n + 1], lam_prod[:], AX.X))
                    st.wait()
                st.of(dve.tensor_scalar(norm_w[:], norm_w[:], (1.0 - LAMBDA_INIT) * math.sqrt(P), None, ALU.mult))
                dve.wait_ge(lam_exp, 1)
                st.of(dve.tensor_tensor(neg_lam[:], lam_sum[:, 1:2], lam_sum[:, 0:1], ALU.subtract))
                st.wait()
                dve.tensor_scalar(neg_lam[:], neg_lam[:], LAMBDA_INIT, None, ALU.subtract).then_inc(prep, 1)
                dve.wait_ge(prep, 3)
                for half in range(2):
                    dve.sem_inc(logits_ready[half], 2)
                dve.sem_inc(av_taken, 2)
                dve.sem_inc(diff_ready, 2)
                base = st.n

                def logits(h, s, n):
                    b, ext = n % 2, (n + 1) * P
                    dve.wait_ge(bias_in[b], h * PAR * 16 + (n // 2 + 1) * 16)
                    for half in range(2):
                        dve.wait_ge(logits_mm[half], h * TT + n + 1)
                        dve.wait_ge(diff_ready, h * TT + n + 1)
                        dve.memset(wait_here[:, 2 * b + half:2 * b + half + 1], 0.0)
                        dve.tensor_tensor_reduce(soft[b][half][:, 0:ext], logit_ps[half][:, 0:ext], bias[b][:, 0:ext],
                                                 1.0, FINFO_MIN, ALU.add, ALU.max, top[b][:, half:half + 1]
                                                 ).then_inc(logits_ready[half], 1)
                    for half in range(2):
                        dve.wait_ge(logits_ready[half], h * TT + n + 3)
                        dve.tensor_scalar(neg_top[b][:, half:half + 1], top[b][:, half:half + 1], -1.0, None,
                                          ALU.mult).then_inc(top_ready[half], 1)

                def difference(h, s, n):
                    b, ext = n % 2, (n + 1) * P
                    own = Steps(dve, dve_step, h * 3 * TT + 3 * n + base)
                    for half in range(2):
                        dve.wait_ge(exp_done[half], h * TT + n + 1)
                    own.of(dve.reciprocal(share[b][:], total[b][:]))
                    own.wait()
                    own.of(dve.tensor_scalar(share[b][:, 1:2], share[b][:, 1:2], neg_lam[:], None, ALU.mult))
                    own.wait()
                    dve.wait_ge(turned, h * TT + n + 1)
                    own.of(dve.tensor_scalar(diff[b][:, 0:ext], soft[b][1][:, 0:ext], share[b][:, 1:2], None, ALU.mult))
                    own.wait()
                    dve.scalar_tensor_tensor(diff[b][:, 0:ext], soft[b][0][:, 0:ext], share[b][:, 0:1],
                                             diff[b][:, 0:ext], ALU.mult, ALU.add).then_inc(diff_ready, 1)

                def take_av(h, s, n):
                    dve.wait_ge(ss_ready, h * TT + n + 1)
                    if n == 0:
                        dve.wait_ge(outT_ready, h + 1)
                    dve.tensor_copy(heads_out[s][:, n, :], av_ps[n % 2][:, 0:P]).then_inc(av_taken, 1)

                def step(h, s, n, begun):
                    behind(h, s, n, 4, begun, take_av)
                    if n == NORM and begun:
                        o = 1 - s
                        dve.wait_ge(root_ready, h)
                        dve.reciprocal(rstd[o][:], ss[o][:]).then_inc(rstd_ready, 1)
                        dve.wait_ge(rstd_ready, h)
                        dve.wait_ge(av_taken, h * TT + 2)
                        dve.tensor_tensor(heads_out[o][:], heads_out[o][:], rstd[o][:].unsqueeze(2).to_broadcast([P, TT, P]),
                                          ALU.mult).then_inc(normed_ready, 1)
                    behind(h, s, n, 0, begun, logits)
                    behind(h, s, n, 1, begun, difference)

                pipeline(dve, step)

            @block.scalar
            def _(act):
                act.wait_ge(dve_step, 4)
                act.activation(lam_sum[:], lam_sum[:], ACT.Exp).then_inc(lam_exp, 1)
                act.wait_ge(prep, 3)
                act.sem_inc(diffT_ready, 1)
                act.sem_inc(outT_ready, 2)

                def sum_squares(h, s, n):
                    act.wait_ge(av_ready, h * TT + n + 3)
                    if not (isinstance(h, int) and h + n == 0):
                        act.wait_ge(ss_ready, h * TT + n)
                    act.activation(squares[:], av_ps[n % 2][:, 0:P], ACT.Square, accum_out=ss[s][:, n:n + 1]).then_inc(ss_ready, 1)

                def exponentials(h, s, n):
                    b, ext = n % 2, (n + 1) * P
                    for half in range(2):
                        act.wait_ge(top_ready[half], h * TT + n + 1)
                        act.activation(soft[b][half][:, 0:ext], soft[b][half][:, 0:ext], ACT.Exp,
                                       bias=neg_top[b][:, half:half + 1],
                                       accum_out=total[b][:, half:half + 1]).then_inc(exp_done[half], 1)

                def take_turned(h, s, n):
                    act.wait_ge(turned, h * TT + n + 3)
                    act.wait_ge(av_ready, h * TT + n + 1)
                    act.activation(diffT[n % 2][:, 0:(n + 1) * P], turn_ps[:, 0:(n + 1) * P], ACT.Copy).then_inc(diffT_ready, 1)

                def step(h, s, n, begun):
                    behind(h, s, n, 4, begun, sum_squares)
                    behind(h, s, n, 0, begun, exponentials)
                    behind(h, s, n, 2, begun, take_turned)
                    o = 1 - s
                    if n == ROOT and begun:
                        act.wait_ge(ss_ready, h * TT)
                        act.activation(ss[o][:], ss[o][:], ACT.Sqrt, bias=eps[:]).then_inc(root_ready, 1)
                    if n == TURN and begun:
                        act.wait_ge(stored[o], (h - 1 - o) * 8 + 16)
                        act.wait_ge(outT_mm, h)
                        act.activation(outT[o][:], turn_ps[:], ACT.Copy, scale=norm_w[:]).then_inc(outT_ready, 1)
                        act.wait_ge(outT_ready, h + 2)
                        act.dma_start(d["attT"][h - 1], outT[o][:]).then_inc(stored[o], 16)

                for s in range(2):
                    act.sem_inc(stored[s], 16)
                pipeline(act, step)
                for s in range(2):
                    act.wait_ge(stored[s], (TURNS + 1) * 16)


def stage_ssd(nc, d):
    OUTS = 4
    ROOT, NORM, OUT = 1, 2, 3
    with ExitStack() as stack:
        sp = Space(nc, stack, "ssd")
        ident = sp.sb("ident", [P, P])
        upto = sp.sb("upto", [P, P])
        after = sp.sb("after", [P, P])
        ones = sp.sb("ones", [P, P])
        eps = sp.sb("eps", [P, 1])
        norm_w = sp.sb("norm_w", [P, DI // P])
        skip = sp.sb("skip", [P, SH])
        a_row = sp.sb("a_row", [P, SH])
        dt = sp.sb("dt", [P, TT, SH])
        da = sp.sb("da", [P, TT, SH])
        from_start = sp.sb("from_start", [P, TT, SH])
        to_end = sp.sb("to_end", [P, TT, SH])
        whole = sp.sb("whole", [P, TT, SH])
        bT = [sp.sb(f"bT{s}", [P, S]) for s in range(2)]
        cT = [sp.sb(f"cT{s}", [P, S]) for s in range(2)]
        xT = [sp.sb(f"xT{s}", [P, 2, S]) for s in range(2)]
        z = [sp.sb(f"z{s}", [P, TT, GW]) for s in range(2)]
        rows = [sp.sb(f"rows{b}", [P, HALF]) for b in range(2)]
        spread = [sp.sb(f"spread{b}", [P, HPG, P]) for b in range(2)]
        x_dt = [sp.sb(f"x_dt{b}", [P, HPG, HD]) for b in range(2)]
        x_end = [sp.sb(f"x_end{b}", [P, HPG, HD]) for b in range(2)]
        x_skip = [sp.sb(f"x_skip{b}", [P, HPG, HD]) for b in range(2)]
        decay = [sp.sb(f"decay{b}", [P, HPG, P]) for b in range(2)]
        cb = sp.sb("cb", [P, P])
        weights = [sp.sb(f"weights{b}", [P, HPG, P]) for b in range(2)]
        state = sp.sb("state", [P, HPG, HD])
        scaled = sp.sb("scaled", [P, HPG, HD])
        y = sp.sb("y", [P, HPG, HD])
        yz = [sp.sb(f"yz{s}", [P, TT, GW]) for s in range(2)]
        squares = sp.sb("squares", [P, GW])
        ss = [sp.sb(f"ss{s}", [P, TT]) for s in range(2)]
        rstd = [sp.sb(f"rstd{s}", [P, TT]) for s in range(2)]
        ynT = [sp.sb(f"ynT{s}", [P, 2, S]) for s in range(2)]
        turn_ps = [sp.ps(f"turn_ps{b}", [P, HALF]) for b in range(2)]
        seg_ps = [sp.ps(f"seg_ps{b}", [P, HPG, P]) for b in range(2)]
        y_ps = [sp.ps(f"y_ps{b}", [P, 2, HPG, HD]) for b in range(2)]
        st_ps = sp.ps("st_ps", [P, HPG, HD])
        out_ps = sp.ps("out_ps", [P, HALF])

        const_in = sp.sem("const_in")
        prep = sp.sem("prep")
        a_exp = sp.sem("a_exp")
        sums_mm = sp.sem("sums_mm")
        sums_exp = sp.sem("sums_exp")
        group_in = [sp.sem(f"group_in{s}") for s in range(2)]
        turn_mm = sp.sem("turn_mm")
        turn_taken = sp.sem("turn_taken")
        spread_ready = sp.sem("spread_ready")
        seg_mm = sp.sem("seg_mm")
        decay_ready = sp.sem("decay_ready")
        x_ready = sp.sem("x_ready")
        weights_ready = sp.sem("weights_ready")
        y_mm = sp.sem("y_mm")
        state_ready = sp.sem("state_ready")
        y_taken = sp.sem("y_taken")
        dve_step = sp.sem("dve_step")
        ss_ready = sp.sem("ss_ready")
        root_ready = sp.sem("root_ready")
        normed_ready = sp.sem("normed_ready")
        rstd_ready = sp.sem("rstd_ready")
        cb_ready = sp.sem("cb_ready")
        out_mm = sp.sem("out_mm")
        out_taken = sp.sem("out_taken")
        stored = [sp.sem(f"stored{s}") for s in range(2)]
        TURNS = G // 2
        CONSTS = 8

        def heads(t, c, g):
            return t[:, c, bass.ds(g * HPG, HPG)]

        sums_ps = out_ps[:, 0:TT * SH].rearrange("p (t n) -> p t n", t=TT)

        def pipeline(eng, step):
            for s in range(2):
                for n in range(TT):
                    step(s, s, n, s > 0)
            with eng.Fori(1, TURNS) as i:
                for s in range(2):
                    for n in range(TT):
                        step(2 * i + s, s, n, True)
            for n in range(TT):
                step(G, 0, n, True)

        def behind(g, s, n, lag, begun, stage):
            if n >= lag and not (isinstance(g, int) and g == G):
                stage(g, s, n - lag)
            elif n < lag and begun:
                stage(g - 1, 1 - s, n - lag + TT)

        with nc.Block() as block:
            @block.sync
            def _(sync):
                sync.dma_start(ident[:], d["ident"]).then_inc(const_in, 16)
                sync.dma_start(upto[:], d["upto"]).then_inc(const_in, 16)
                sync.dma_start(after[:], d["after"]).then_inc(const_in, 16)
                sync.dma_start(eps[:], d["eps"][1].rearrange("(p a) -> p a", a=1)).then_inc(const_in, 16)
                sync.dma_start(norm_w[:], d["ssd_norm_w"]).then_inc(const_in, 16)
                sync.dma_start(skip[:], d["d_skip"].partition_broadcast(P)).then_inc(const_in, 16)
                sync.dma_start(a_row[:], d["a_log"].partition_broadcast(P)).then_inc(const_in, 16)
                sync.dma_start(dt[:], d["dt"].rearrange("t p n -> p t n")).then_inc(const_in, 16)

                def load_group(g, s):
                    sync.dma_start(bT[s][:], d["xbcT"][DI // P + g]).then_inc(group_in[s], 16)
                    sync.dma_start(cT[s][:], d["xbcT"][DI // P + G + g]).then_inc(group_in[s], 16)
                    sync.dma_start(xT[s][:], d["xbcT"][bass.ds(2 * g, 2)].rearrange("a p n -> p a n")).then_inc(group_in[s], 16)
                    sync.dma_start(z[s][:], d["z"][:, :, bass.ds(g * GW, GW)].rearrange("t p n -> p t n")).then_inc(group_in[s], 16)

                for s in range(2):
                    load_group(s, s)
                with sync.Fori(0, TURNS - 1) as i:
                    for s in range(2):
                        sync.wait_ge(y_taken, (2 * i + s) * TT + TT + 2)
                        load_group(2 * i + s + 2, s)

            @block.gpsimd
            def _(pool):
                pool.wait_ge(prep, 5)

                def spread_da(g, s, c):
                    u = g * TT + c
                    pool.wait_ge(seg_mm, u + 1)
                    pool.tensor_tensor(spread[c % 2][:], after[:].unsqueeze(1).to_broadcast([P, HPG, P]),
                                       heads(da, c, g).unsqueeze(2).to_broadcast([P, HPG, P]), ALU.mult).then_inc(spread_ready, 1)

                def scale_x(g, s, c):
                    u, b = g * TT + c, c % 2
                    pool.wait_ge(turn_taken, u + 3)
                    pool.wait_ge(y_taken, u + 1)
                    x = rows[b][:, 0:GW].rearrange("p (r e) -> p r e", r=HPG)
                    for out, factor in ((x_dt[b], heads(dt, c, g)), (x_end[b], heads(to_end, c, g)),
                                        (x_skip[b], skip[:, bass.ds(g * HPG, HPG)])):
                        pool.tensor_tensor(out[:], x, factor.unsqueeze(2).to_broadcast([P, HPG, HD]),
                                           ALU.mult).then_inc(x_ready, 1)

                def step(g, s, n, begun):
                    behind(g, s, n, 0, begun, spread_da)
                    behind(g, s, n, 1, begun, scale_x)

                pipeline(pool, step)

            @block.tensor
            def _(pe):
                pe.wait_ge(const_in, 16 * CONSTS)
                pe.wait_ge(prep, 3)
                for n, left in enumerate((upto, after, ones)):
                    if n:
                        pe.wait_ge(sums_exp, n)
                    pe.matmul(sums_ps[:], left[:], da[:], start=True, stop=True).then_inc(sums_mm, 1)
                pe.sem_inc(seg_mm, 2)
                pe.wait_ge(sums_exp, 3)
                pe.sem_inc(out_mm, 2 * OUTS)

                def turn_and_segments(g, s, c):
                    u, b = g * TT + c, c % 2
                    cols = slice(c * P, (c + 1) * P)
                    if c == 0:
                        pe.wait_ge(group_in[s], (g - s) * 32 + 64)
                    pe.wait_ge(turn_taken, u + 1)
                    pe.transpose(turn_ps[b][:, 0:P], xT[s][:, 0, cols], ident[:])
                    pe.transpose(turn_ps[b][:, P:2 * P], xT[s][:, 1, cols], ident[:])
                    pe.transpose(turn_ps[b][:, 2 * P:3 * P], bT[s][:, cols], ident[:])
                    pe.matmul(turn_ps[b][:, 3 * P:4 * P], bT[s][:, cols], cT[s][:, cols],
                              start=True, stop=True).then_inc(turn_mm, 1)
                    pe.wait_ge(spread_ready, u + 1)
                    pe.wait_ge(decay_ready, u + 1)
                    for r in range(HPG):
                        mm = pe.matmul(seg_ps[b][:, r, :], spread[b][:, r, :], upto[:], start=True, stop=True)
                    mm.then_inc(seg_mm, 1)

                def outputs(g, s, c):
                    u, b = g * TT + c, c % 2
                    pe.wait_ge(weights_ready, u + 3)
                    pe.wait_ge(x_ready, 3 * u + 3)
                    pe.wait_ge(y_taken, u + 1)
                    pe.matmul(y_ps[b][:, 0, :, :], ident[:], x_skip[b][:], start=True, stop=False)
                    for r in range(HPG):
                        mm = pe.matmul(y_ps[b][:, 0, r, :], weights[b][:, r, :], x_dt[b][:, r, :], start=False, stop=(r == HPG - 1))
                    if c > 0:
                        pe.wait_ge(state_ready, g * (TT - 1) + c)
                        mm = pe.matmul(y_ps[b][:, 1, :, :], cT[s][:, c * P:(c + 1) * P], state[:], start=True, stop=True)
                    if c < TT - 1:
                        mm = pe.matmul(st_ps[:], rows[b][:, 2 * P:3 * P], x_end[b][:], start=True, stop=True)
                    mm.then_inc(y_mm, 1)

                def turn_output(g, s, o):
                    pe.wait_ge(normed_ready, g + 1)
                    pe.wait_ge(out_taken, g * OUTS + o + 1)
                    for t in range(4):
                        tok = 4 * (o % 2) + t
                        mm = pe.transpose(out_ps[:, t * P:(t + 1) * P], yz[s][:, tok, (o // 2) * P:(o // 2 + 1) * P], ident[:])
                    mm.then_inc(out_mm, 1)

                def step(g, s, n, begun):
                    behind(g, s, n, 0, begun, turn_and_segments)
                    behind(g, s, n, 1, begun, outputs)
                    if begun and 0 <= n - OUT < OUTS:
                        turn_output(g - 1, 1 - s, n - OUT)

                pipeline(pe, step)

            @block.vector
            def _(dve):
                dve.memset(ones[:], 1.0).then_inc(prep, 1)
                dve.wait_ge(const_in, 16 * CONSTS)
                dve.wait_ge(a_exp, 1)
                dve.tensor_scalar(a_row[:], a_row[:], -1.0, None, ALU.mult).then_inc(prep, 1)
                dve.wait_ge(prep, 2)
                dve.tensor_tensor(da[:], dt[:], a_row[:].unsqueeze(1).to_broadcast([P, TT, SH]), ALU.mult).then_inc(prep, 1)
                dve.wait_ge(sums_exp, 2)
                dve.tensor_tensor(to_end[:], to_end[:], dt[:], ALU.mult).then_inc(prep, 1)
                dve.wait_ge(sums_exp, 3)
                dve.tensor_scalar(norm_w[:], norm_w[:], math.sqrt(GW), None, ALU.mult).then_inc(prep, 1)
                dve.sem_inc(weights_ready, 2)
                dve.sem_inc(y_taken, 2)
                dve.sem_inc(out_taken, 1)

                def mask(g, s, c):
                    u, b = g * TT + c, c % 2
                    if c == 0:
                        dve.wait_ge(group_in[s], (g - s) * 32 + 64)
                    dve.wait_ge(turn_taken, u + 3)
                    dve.wait_ge(weights_ready, u + 2)
                    dve.tensor_tensor(cb[:], rows[b][:, 3 * P:4 * P], upto[:], ALU.mult).then_inc(cb_ready, 1)

                def weigh(g, s, c):
                    u, b = g * TT + c, c % 2
                    dve.wait_ge(cb_ready, u + 1)
                    dve.wait_ge(decay_ready, u + 3)
                    dve.tensor_tensor(weights[b][:], decay[b][:], cb[:].unsqueeze(1).to_broadcast([P, HPG, P]),
                                      ALU.mult).then_inc(weights_ready, 1)

                def finish_steps(g, c):
                    return Steps(dve, dve_step, g * (3 * TT - 4) + max(3 * c - 3, 0))

                def scale_state(g, s, c):
                    u, b = g * TT + c, c % 2
                    own = finish_steps(g, c)
                    dve.wait_ge(y_mm, u + 1)
                    dve.wait_ge(y_taken, u + 2)
                    if 0 < c < TT - 1:
                        own.of(dve.tensor_tensor(state[:], state[:], heads(whole, c, g).unsqueeze(2).to_broadcast(
                            [P, HPG, HD]), ALU.mult))
                    if c > 0:
                        own.of(dve.tensor_tensor(scaled[:], y_ps[b][:, 1, :, :], heads(from_start, c, g).unsqueeze(2).to_broadcast(
                            [P, HPG, HD]), ALU.mult))

                def finish(g, s, c):
                    u, b = g * TT + c, c % 2
                    own = finish_steps(g, c)
                    own.n = (c > 0) + (0 < c < TT - 1)
                    if c > 0:
                        own.wait()
                    if c == 0:
                        dve.tensor_copy(state[:], st_ps[:]).then_inc(state_ready, 1)
                        dve.wait_ge(out_mm, g * OUTS + OUTS)
                    elif c < TT - 1:
                        dve.tensor_tensor(state[:], state[:], st_ps[:], ALU.add).then_inc(state_ready, 1)
                    if c > 0:
                        own.of(dve.tensor_tensor(y[:], y_ps[b][:, 0, :, :], scaled[:], ALU.add))
                        own.wait()
                        dve.tensor_tensor(yz[s][:, c, :], y[:].rearrange("p r e -> p (r e)"), z[s][:, c, :], ALU.mult).then_inc(y_taken, 1)
                    else:
                        dve.tensor_tensor(yz[s][:, c, :], y_ps[b][:, 0, :, :].rearrange("p r e -> p (r e)"), z[s][:, c, :], ALU.mult).then_inc(y_taken, 1)

                def norm(g, s):
                    dve.wait_ge(root_ready, g + 1)
                    dve.reciprocal(rstd[s][:], ss[s][:]).then_inc(rstd_ready, 1)
                    dve.wait_ge(rstd_ready, g + 1)
                    dve.tensor_tensor(yz[s][:], yz[s][:], rstd[s][:].unsqueeze(2).to_broadcast([P, TT, GW]), ALU.mult).then_inc(normed_ready, 1)

                def take_output(g, s, o):
                    if o == 0:
                        dve.wait_ge(stored[s], (g - s) * 8 + 16)
                    dve.wait_ge(out_mm, (g + 2) * OUTS + o + 1)
                    dve.tensor_scalar(ynT[s][:, o // 2, (o % 2) * HALF:(o % 2 + 1) * HALF], out_ps[:],
                                      norm_w[:, bass.ds(2 * g + o // 2, 1)], None, ALU.mult).then_inc(out_taken, 1)

                def step(g, s, n, begun):
                    behind(g, s, n, 0, begun, mask)
                    behind(g, s, n, 1, begun, scale_state)
                    behind(g, s, n, 0, begun, weigh)
                    behind(g, s, n, 1, begun, finish)
                    if begun and n == NORM:
                        norm(g - 1, 1 - s)
                    if begun and 0 <= n - OUT < OUTS:
                        take_output(g - 1, 1 - s, n - OUT)

                pipeline(dve, step)

            @block.scalar
            def _(act):
                act.wait_ge(const_in, 16 * CONSTS)
                act.activation(a_row[:], a_row[:], ACT.Exp).then_inc(a_exp, 1)
                for n, out in enumerate((from_start, to_end, whole)):
                    act.wait_ge(sums_mm, n + 1)
                    act.activation(out[:], sums_ps[:], ACT.Exp).then_inc(sums_exp, 1)
                act.wait_ge(prep, 5)
                act.sem_inc(turn_taken, 2)
                act.sem_inc(decay_ready, 2)
                for s in range(2):
                    act.sem_inc(stored[s], 16)

                def take_and_decay(g, s, c):
                    u, b = g * TT + c, c % 2
                    act.wait_ge(turn_mm, u + 1)
                    act.wait_ge(y_taken, u + 1)
                    act.activation(rows[b][:], turn_ps[b][:], ACT.Copy).then_inc(turn_taken, 1)
                    act.wait_ge(seg_mm, u + 3)
                    act.wait_ge(weights_ready, u + 1)
                    act.activation(decay[b][:], seg_ps[b][:], ACT.Exp).then_inc(decay_ready, 1)

                def sum_squares(g, s, c):
                    act.wait_ge(y_taken, g * TT + c + 3)
                    act.activation(squares[:], yz[s][:, c, :], ACT.Square, accum_out=ss[s][:, c:c + 1]).then_inc(ss_ready, 1)
                    act.wait_ge(ss_ready, g * TT + c + 1)

                def step(g, s, n, begun):
                    o = 1 - s
                    behind(g, s, n, 0, begun, take_and_decay)
                    behind(g, s, n, 2, begun, sum_squares)
                    if begun and n == ROOT:
                        act.activation(ss[o][:], ss[o][:], ACT.Sqrt, bias=eps[:]).then_inc(root_ready, 1)
                    if begun and n == OUT + OUTS:
                        act.wait_ge(out_taken, g * OUTS + 1)
                        act.dma_start(d["ynT"][bass.ds(2 * g - 2, 2)].rearrange("a p n -> p a n"), ynT[o][:]).then_inc(stored[o], 16)

                pipeline(act, step)
                for s in range(2):
                    act.wait_ge(stored[s], (TURNS + 1) * 16)


def stage_merge(nc, d, held):
    with ExitStack() as stack:
        sp = Space(nc, stack, "mg")
        raw = [sp.sb(f"raw{s}", [P, KD, HALF]) for s in range(2)]
        merge_branches(nc, d, held, raw)
        merge_out(nc, d, held, raw)


def merge_branches(nc, d, mixT, raw):
    CH = 3
    with ExitStack() as stack:
        sp = Space(nc, stack, "mb")
        branch = [[sp.sb(f"branch{c}_{part}", [P, KD, HALF], F32R) for part in ("hi", "lo")] for c in range(CH)]
        w_raw = [sp.sb(f"w_raw{c}", [P, KD, P]) for c in range(CH)]
        w = [[sp.sb(f"w{c}_{part}", [P, KD, P], F32R) for part in ("hi", "lo")] for c in range(CH)]
        gate = [sp.sb(f"gate{s}", [P, 2, HALF]) for s in range(2)]
        ssd_ps = [sp.ps(f"ssd_ps{s}", [P, HALF]) for s in range(2)]
        att_ps = [sp.ps(f"att_ps{s}", [P, HALF]) for s in range(2)]
        raw_in = [sp.sem(f"raw_in{s}") for s in range(2)]
        branch_hi = sp.sem("branch_hi")
        branch_lo = sp.sem("branch_lo")
        w_in = [sp.sem(f"w_in{c}") for c in range(CH)]
        w_hi = [sp.sem(f"w_hi{c}") for c in range(CH)]
        w_lo = [sp.sem(f"w_lo{c}") for c in range(CH)]
        w_used = [sp.sem(f"w_used{c}") for c in range(CH)]
        gate_in = [sp.sem(f"gate_in{s}") for s in range(2)]
        merged = [sp.sem(f"merged{s}") for s in range(2)]
        dve_step = sp.sem("dve_step")
        HT = KD // 2
        with nc.Block() as block:
            @block.sync
            def _(sync):
                for n in range(2 * CH + 2):
                    if n >= 2:
                        sync.wait_ge(branch_lo, n - 1)
                    half, c = divmod(n, CH)
                    if half == 2:
                        src = d["w_out"].rearrange("(k p) n -> p k n", p=P)[:, :, c * HALF:(c + 1) * HALF]
                    else:
                        src = d["attT"] if c == 2 else d["ynT"][c * KD:(c + 1) * KD]
                        src = src[:, :, half * HALF:(half + 1) * HALF].rearrange("k p n -> p k n")
                    sync.dma_start(raw[n % 2][:], src).then_inc(raw_in[n % 2], 16)
                for s in range(2):
                    sync.wait_ge(raw_in[s], 16 * (CH + 1))

            @block.gpsimd
            def _(pool):
                gates = d["gateT"].rearrange("(b k) p n -> p b k n", b=2)

                def turn(m, half, first):
                    for s in range(2):
                        i = 2 * m + s + half * KD
                        for c in range(CH):
                            if not (first and i == 0):
                                pool.wait_ge(w_lo[c], i)
                            pool.dma_start(w_raw[c][:], d["w_branch"][2 * m + s][:, c * KD:(c + 1) * KD, :] if first else
                                           d["w_branch"][bass.ds(2 * m + s, 1), :, c * KD:(c + 1) * KD, :].rearrange("a p k n -> p (a k) n")
                                           ).then_inc(w_in[c], 16)
                        if not (first and half == 0):
                            pool.wait_ge(merged[s], m + half * HT)
                        pool.dma_start(gate[s][:], gates[:, :, bass.ds(2 * m + s, 1), half * HALF:(half + 1) * HALF]
                                       .rearrange("p b a n -> p b (a n)")).then_inc(gate_in[s], 16)

                for half in range(2):
                    turn(0, half, True)
                    with pool.Fori(1, HT) as m:
                        turn(m, half, False)

            @block.scalar
            def _(act):
                def turn(m, half, first):
                    for s in range(2):
                        i = 2 * m + s + half * KD
                        for c in range(CH):
                            if first and s == 0:
                                n = half * CH + c
                                act.wait_ge(raw_in[n % 2], n // 2 * 16 + 16)
                                if half:
                                    act.wait_ge(w_used[c], KD)
                                act.activation(branch[c][0][:], raw[n % 2][:], ACT.Copy).then_inc(branch_hi, 1)
                            act.wait_ge(w_in[c], i * 16 + 16)
                            if not (first and i == 0):
                                act.wait_ge(w_used[c], i)
                            act.activation(w[c][0][:], w_raw[c][:], ACT.Copy).then_inc(w_hi[c], 1)

                for half in range(2):
                    turn(0, half, True)
                    with act.Fori(1, HT) as m:
                        turn(m, half, False)

            @block.tensor
            def _(pe):
                def turn(m, half, first):
                    for s in range(2):
                        i = 2 * m + s + half * KD
                        if not (first and half == 0):
                            pe.wait_ge(merged[s], m + half * HT)
                        for c in range(CH):
                            ps = att_ps[s] if c == 2 else ssd_ps[s]
                            if first and s == 0:
                                pe.wait_ge(branch_lo, half * CH + c + 1)
                            pe.wait_ge(w_lo[c], i + 1)
                            for k in range(KD):
                                for a, b in PARTS:
                                    mm = pe.matmul(ps[:], w[c][a][:, k, :], branch[c][b][:, k, :],
                                                   start=(c != 1 and k == 0 and a + b == 0), stop=(c != 0 and k == KD - 1 and a == 1))
                            mm.then_inc(w_used[c], 1)

                for half in range(2):
                    turn(0, half, True)
                    with pe.Fori(1, HT) as m:
                        turn(m, half, False)

            @block.vector
            def _(dve):
                def merge(m, s, half):
                    i = 2 * m + s + half * KD
                    own = Steps(dve, dve_step, i * 2)
                    dve.wait_ge(w_used[CH - 1], i + 1)
                    dve.wait_ge(w_used[1], i + 1)
                    dve.wait_ge(gate_in[s], m * 16 + half * HT * 16 + 16)
                    own.of(dve.tensor_tensor(gate[s][:, 0, :], ssd_ps[s][:], gate[s][:, 0, :], ALU.mult))
                    own.of(dve.tensor_tensor(gate[s][:, 1, :], att_ps[s][:], gate[s][:, 1, :], ALU.mult))
                    own.wait()
                    dve.tensor_tensor(mixT[:, bass.ds(2 * m + s, 1), half * HALF:(half + 1) * HALF].rearrange("p a n -> p (a n)"),
                                      gate[s][:, 0, :], gate[s][:, 1, :], ALU.add).then_inc(merged[s], 1)

                def turn(m, half, first):
                    for s in range(2):
                        i = 2 * m + s + half * KD
                        for c in range(CH):
                            if first and s == 0:
                                n = half * CH + c
                                dve.wait_ge(branch_hi, n + 1)
                                dve.tensor_tensor(branch[c][1][:], raw[n % 2][:], branch[c][0][:].bitcast(F32), ALU.subtract).then_inc(branch_lo, 1)
                            dve.wait_ge(w_hi[c], i + 1)
                            dve.tensor_tensor(w[c][1][:], w_raw[c][:], w[c][0][:].bitcast(F32), ALU.subtract).then_inc(w_lo[c], 1)
                        if s == 1:
                            merge(m, 0, half)
                        elif not first:
                            merge(m - 1, 1, half)
                        elif half:
                            merge(HT - 1, 1, 0)

                for half in range(2):
                    turn(0, half, True)
                    with dve.Fori(1, HT) as m:
                        turn(m, half, False)
                merge(HT - 1, 1, 1)


def merge_out(nc, d, held, raw):
    with ExitStack() as stack:
        sp = Space(nc, stack, "mo")
        ident = sp.sb("ident", [P, P])
        eps = sp.sb("eps", [P, 1])
        g1 = sp.sb("g1", [P, D])
        scale2 = sp.sb("scale2", [P, D])
        shift2 = sp.sb("shift2", [P, D])
        w_out = [sp.sb(f"w_out_{part}", [P, KD, D], F32R) for part in ("hi", "lo")]
        mix = [[sp.sb(f"mix{s}_{part}", [P, KD, P], F32R) for part in ("hi", "lo")] for s in range(2)]
        x = [sp.sb(f"x{s}", [P, D]) for s in range(2)]
        n2 = [sp.sb(f"n2{s}", [P, D]) for s in range(2)]
        squares = sp.sb("squares", [P, D])
        ss = [sp.sb(f"ss{s}", [P, 1]) for s in range(2)]
        rstd = [sp.sb(f"rstd{s}", [P, 1]) for s in range(2)]
        out_ps = [sp.ps(f"out_ps{s}", [P, D]) for s in range(2)]
        turn_ps = [sp.ps(f"turn_ps{s}", [P, KD, P]) for s in range(2)]
        const_in = sp.sem("const_in")
        w_hi = sp.sem("w_hi")
        w_lo = sp.sem("w_lo")
        mix_hi = [sp.sem(f"mix_hi{s}") for s in range(2)]
        mix_lo = [sp.sem(f"mix_lo{s}") for s in range(2)]
        x_in = [sp.sem(f"x_in{s}") for s in range(2)]
        out_mm = [sp.sem(f"out_mm{s}") for s in range(2)]
        h_ready = [sp.sem(f"h_ready{s}") for s in range(2)]
        ss_step = [sp.sem(f"ss_step{s}") for s in range(2)]
        dve_step = sp.sem("dve_step")
        n2_ready = [sp.sem(f"n2_ready{s}") for s in range(2)]
        turned = [sp.sem(f"turned{s}") for s in range(2)]
        turned_out = [sp.sem(f"turned_out{s}") for s in range(2)]
        h_stored = [sp.sem(f"h_stored{s}") for s in range(2)]
        NT = TT // 2

        with nc.Block() as block:
            @block.gpsimd
            def _(pool):
                for s in range(2):
                    pool.dma_start(x[s][:], d["x"][s * P:(s + 1) * P, :]).then_inc(x_in[s], 16)
                with pool.Fori(1, NT) as m:
                    for s in range(2):
                        pool.wait_ge(n2_ready[s], m)
                        pool.wait_ge(h_stored[s], m * 16)
                        pool.dma_start(x[s][:], d["x"][bass.ds(2 * m * P + s * P, P), :]).then_inc(x_in[s], 16)

            @block.sync
            def _(sync):
                sync.dma_start(ident[:], d["ident"]).then_inc(const_in, 16)
                sync.dma_start(eps[:], d["eps"][0].rearrange("(p a) -> p a", a=1)).then_inc(const_in, 16)
                for row, n in ((g1, 2), (scale2, 4), (shift2, 3)):
                    sync.dma_start(row[:], d["rows"][n].partition_broadcast(P)).then_inc(const_in, 16)
                with sync.Fori(0, NT) as m:
                    for s in range(2):
                        sync.wait_ge(h_ready[s], m + 1)
                        sync.dma_start(d["h"][2 * m + s], x[s][:]).then_inc(h_stored[s], 16)
                for s in range(2):
                    sync.wait_ge(h_stored[s], 16 * NT)

            @block.tensor
            def _(pe):
                def transposes(m, s, very_first):
                    pe.wait_ge(n2_ready[s], m + 1)
                    if not very_first:
                        pe.wait_ge(turned_out[s], m)
                    for k in range(KD):
                        mm = pe.transpose(turn_ps[s][:, k, :], n2[s][:, k * P:(k + 1) * P], ident[:])
                    mm.then_inc(turned[s], 1)

                def turn(m, first, last):
                    for s in range(2):
                        pe.wait_ge(mix_lo[s], m + 1)
                        if not first:
                            pe.wait_ge(h_ready[s], m)
                        for c in range(2):
                            if first and s == 0:
                                pe.wait_ge(w_lo, c + 1)
                            for k in range(KD):
                                for a, b in PARTS:
                                    mm = pe.matmul(out_ps[s][:, c * HALF:(c + 1) * HALF], mix[s][a][:, k, :],
                                                   w_out[b][:, k, c * HALF:(c + 1) * HALF],
                                                   start=(k == 0 and a + b == 0), stop=(k == KD - 1 and a == 1))
                        mm.then_inc(out_mm[s], 1)
                        if s == 1:
                            transposes(m, 0, first)
                        elif not first:
                            transposes(m - 1, 1, isinstance(m, int) and m == 1)

                pe.wait_ge(const_in, 5 * 16)
                turn(0, True, False)
                turn(1, False, False)
                with pe.Fori(2, NT) as m:
                    turn(m, False, False)
                transposes(NT - 1, 1, False)

            @block.scalar
            def _(act):
                def high(m, s, first):
                    if not first:
                        act.wait_ge(out_mm[s], m)
                    act.activation(mix[s][0][:], held[:, :, bass.ds((2 * m + s) * P, P)], ACT.Copy).then_inc(mix_hi[s], 1)

                def norm(m, s):
                    act.wait_ge(h_ready[s], m + 1)
                    act.activation(squares[:], x[s][:], ACT.Square, accum_out=ss[s][:]).then_inc(ss_step[s], 1)
                    act.wait_ge(ss_step[s], 2 * m + 1)
                    act.activation(ss[s][:], ss[s][:], ACT.Sqrt, bias=eps[:]).then_inc(ss_step[s], 1)
                    act.wait_ge(turned[s], m + 1)
                    act.wait_ge(mix_lo[s], m + 1)
                    act.activation(held[:, :, bass.ds((2 * m + s) * P, P)], turn_ps[s][:], ACT.Copy).then_inc(turned_out[s], 1)

                def turn(m, first, last):
                    high(m, 1, first)
                    if not first:
                        norm(m - 1, 1)
                    if not last:
                        high(m + 1, 0, False)
                    norm(m, 0)

                high(0, 0, True)
                for c in range(2):
                    act.activation(w_out[0][:, :, c * HALF:(c + 1) * HALF], raw[c][:], ACT.Copy).then_inc(w_hi, 1)
                act.wait_ge(const_in, 5 * 16)
                turn(0, True, False)
                turn(1, False, False)
                with act.Fori(2, NT - 1) as m:
                    turn(m, False, False)
                turn(NT - 1, False, True)
                norm(NT - 1, 1)

            @block.vector
            def _(dve):
                def low(m, s):
                    dve.wait_ge(mix_hi[s], m + 1)
                    dve.tensor_tensor(mix[s][1][:], held[:, :, bass.ds((2 * m + s) * P, P)], mix[s][0][:].bitcast(F32), ALU.subtract).then_inc(mix_lo[s], 1)

                def norm(m, s, very_first):
                    own = Steps(dve, dve_step, (2 * m + s) * 3)
                    dve.wait_ge(out_mm[s], m + 1)
                    dve.wait_ge(x_in[s], m * 16 + 16)
                    if not very_first:
                        dve.wait_ge(turned[s], m)
                    own.of(dve.tensor_tensor(n2[s][:], out_ps[s][:], g1[:], ALU.mult))
                    own.wait()
                    dve.tensor_tensor(x[s][:], x[s][:], n2[s][:], ALU.add).then_inc(h_ready[s], 1)
                    dve.wait_ge(ss_step[s], 2 * m + 2)
                    own.of(dve.reciprocal(rstd[s][:], ss[s][:]))
                    own.wait()
                    own.of(dve.scalar_tensor_tensor(n2[s][:], x[s][:], rstd[s][:], scale2[:], ALU.mult, ALU.mult))
                    own.wait()
                    dve.tensor_tensor(n2[s][:], n2[s][:], shift2[:], ALU.add).then_inc(n2_ready[s], 1)

                def turn(m, first, last):
                    low(m, 1)
                    if not first:
                        norm(m - 1, 1, isinstance(m, int) and m == 1)
                    if not last:
                        low(m + 1, 0)
                    norm(m, 0, first)

                low(0, 0)
                for c in range(2):
                    dve.wait_ge(w_hi, c + 1)
                    dve.tensor_tensor(w_out[1][:, :, c * HALF:(c + 1) * HALF], raw[c][:], w_out[0][:, :, c * HALF:(c + 1) * HALF].bitcast(F32),
                                      ALU.subtract).then_inc(w_lo, 1)
                dve.wait_ge(const_in, 5 * 16)
                turn(0, True, False)
                turn(1, False, False)
                with dve.Fori(2, NT - 1) as m:
                    turn(m, False, False)
                turn(NT - 1, False, True)
                norm(NT - 1, 1, False)


PAIR_ROWS = [(0, 1, 16), (1, 2, 8), (2, 3, 5), (3, 4, 4), (4, 5, 3), (5, 8, 2), (8, 16, 1)]
PAIRS = sum((a1 - a0) * nb for a0, a1, nb in PAIR_ROWS)


def stage_peer_topk(nc, d, n2T):
    with ExitStack() as stack:
        sp = Space(nc, stack, "tk")
        ident = sp.sb("ident", [P, P])
        pair_iota = sp.sb("pair_iota", [P, PAIRS])
        wq = [sp.sb(f"wq{s}", [P, KD, P]) for s in range(2)]
        keys = [sp.sb(f"keys{s}", [P, 2 * NK]) for s in range(2)]
        qT = [sp.sb(f"qT{s}", [P, S]) for s in range(2)]
        score = [sp.sb(f"score{s}", [P, TT, 2, NK]) for s in range(2)]
        top = [sp.sb(f"top{s}", [P, TT, 2, TOPK]) for s in range(2)]
        index = [sp.sb(f"index{s}", [P, TT, 2, TOPK], U32) for s in range(2)]
        indexf = [sp.sb(f"indexf{s}", [P, TT, 2, TOPK]) for s in range(2)]
        pair = [sp.sb(f"pair{s}", [P, TT, PAIRS]) for s in range(2)]
        pair_id = [sp.sb(f"pair_id{s}", [P, TT, PAIRS]) for s in range(2)]
        best = [sp.sb(f"best{s}", [P, TT, TOPK]) for s in range(2)]
        place = [sp.sb(f"place{s}", [P, TT, TOPK], U32) for s in range(2)]
        placef = [sp.sb(f"placef{s}", [P, TT, TOPK]) for s in range(2)]
        waits = sp.sb("waits", [1, 10])
        hot = [sp.sb(f"hot{s}", [P, TT * TOPK, PAIRS]) for s in range(2)]
        expert = [sp.sb(f"expert{s}", [P, TT, TOPK], I32) for s in range(2)]
        total = [sp.sb(f"total{s}", [P, TT]) for s in range(2)]
        chosen = sp.sb("chosen", [P, 3, TT, PH, TOPK])
        chosenT = sp.sb("chosenT", [P, 3, S])
        split = [sp.sb(f"split{s}", [P, TT, TOPK], I32) for s in range(2)]
        one = sp.sb("one", [P, 1])
        q_ps = sp.ps("q_ps", [P, S])
        score_ps = sp.ps("score_ps", [P, TT, 2 * NK])
        turn_ps = [sp.ps(f"turn_ps{b}", [P, HALF]) for b in range(2)]
        const_in = sp.sem("const_in")
        keys_zero = sp.sem("keys_zero")
        one_set = sp.sem("one_set")
        keys_in = [sp.sem(f"keys_in{s}") for s in range(2)]
        w_in = [sp.sem(f"w_in{s}") for s in range(2)]
        q_mm = sp.sem("q_mm")
        q_ready = sp.sem("q_ready")
        score_mm = sp.sem("score_mm")
        score_ready = sp.sem("score_ready")
        dve_step = sp.sem("dve_step")
        place_ready = sp.sem("place_ready")
        offset_ready = sp.sem("offset_ready")
        offset_mag = sp.sem("offset_mag")
        hot_made = sp.sem("hot_made")
        hot_ready = sp.sem("hot_ready")
        gate_exp = sp.sem("gate_exp")
        head_done = sp.sem("head_done")
        turn_mm = sp.sem("turn_mm")
        turned = sp.sem("turned")
        stored = sp.sem("stored")
        TURNS = PH // 2
        HOT = TT * TOPK // 2

        def hot_part(s, part):
            return hot[s][:, part * HOT:(part + 1) * HOT, :]

        with nc.Block() as block:
            @block.sync
            def _(sync):
                def load_wq(h, s):
                    sync.dma_start(wq[s][:], d["w_pq"][h]).then_inc(w_in[s], 16)

                def load_keys(h, s):
                    sync.dma_start(keys[s][0:64, 0:NK], d["key1T"][h]).then_inc(keys_in[s], 16)
                    sync.dma_start(keys[s][64:P, NK:2 * NK], d["key2T"][h]).then_inc(keys_in[s], 16)

                for s in range(2):
                    load_wq(s, s)
                sync.wait_ge(keys_zero, 2)
                for s in range(2):
                    load_keys(s, s)
                sync.dma_start(ident[:], d["ident"]).then_inc(const_in, 16)
                sync.dma_start(pair_iota[:], d["iota"][0:PAIRS].partition_broadcast(P)).then_inc(const_in, 16)
                with sync.Fori(0, TURNS - 1) as i:
                    for s in range(2):
                        sync.wait_ge(score_mm, 2 * i + s + 1)
                        load_wq(2 * i + s + 2, s)
                        load_keys(2 * i + s + 2, s)
                sync.wait_ge(turned, 6)
                sync.dma_start(d["chosenT"].rearrange("a p n -> p a n"), chosenT[:]).then_inc(stored, 16)
                sync.wait_ge(stored, 16)

            @block.tensor
            def _(pe):
                with pe.Fori(0, TURNS) as i:
                    for s in range(2):
                        h = 2 * i + s
                        pe.wait_ge(w_in[s], i * 16 + 16)
                        pe.wait_ge(q_ready, h + 1)
                        for c in range(2):
                            for k in range(KD):
                                mm = pe.matmul(q_ps[:, c * HALF:(c + 1) * HALF], wq[s][:, k, :], n2T[:, k, c * HALF:(c + 1) * HALF],
                                               start=(k == 0), stop=(k == KD - 1))
                        mm.then_inc(q_mm, 1)
                        pe.wait_ge(q_ready, h + 2)
                        pe.wait_ge(score_ready, h + 1)
                        pe.wait_ge(keys_in[s], i * 32 + 32)
                        for t in range(TT):
                            mm = pe.matmul(score_ps[:, t, :], qT[s][:, t * P:(t + 1) * P], keys[s][:], start=True, stop=True)
                        mm.then_inc(score_mm, 1)
                pe.wait_ge(const_in, 32)
                pe.wait_ge(head_done, PH)
                for n in range(6):
                    if n >= 2:
                        pe.wait_ge(turned, n - 1)
                    for t in range(4):
                        tt = 4 * (n % 2) + t
                        mm = pe.transpose(turn_ps[n % 2][:, t * P:(t + 1) * P],
                                          chosen[:, n // 2, tt, :, :].rearrange("p h k -> p (h k)"), ident[:])
                    mm.then_inc(turn_mm, 1)

            @block.scalar
            def _(act):
                act.sem_inc(q_ready, 1)
                act.sem_inc(score_ready, 1)
                act.wait_ge(one_set, 1)

                def take_scores(h, s):
                    act.wait_ge(q_mm, h + 1)
                    act.activation(qT[s][:], q_ps[:], ACT.Copy).then_inc(q_ready, 1)
                    act.wait_ge(score_mm, h + 1)
                    act.wait_ge(place_ready, h + 1)
                    act.activation(score[s][:], score_ps[:].rearrange("p t (a n) -> p t a n", a=2), ACT.Copy).then_inc(score_ready, 1)

                def exponentials(h, s):
                    act.wait_ge(place_ready, h + 3)
                    act.activation(best[s][:], best[s][:], ACT.Exp).then_inc(gate_exp, 1)
                    for part in range(2):
                        act.wait_ge(offset_ready, 2 * h + part + 1)
                        act.activation(hot_part(s, part), hot_part(s, part), ACT.Abs).then_inc(offset_mag, 1)
                        act.wait_ge(offset_mag, 2 * h + part + 1)
                        act.activation(hot_part(s, part), hot_part(s, part), ACT.Relu, bias=one[:], scale=-1.0).then_inc(hot_made, 1)

                take_scores(0, 0)
                with act.Fori(0, TURNS - 1) as i:
                    for s in range(2):
                        take_scores(2 * i + s + 1, 1 - s)
                        exponentials(2 * i + s, s)
                take_scores(PH - 1, 1)
                exponentials(PH - 2, 0)
                exponentials(PH - 1, 1)
                for n in range(6):
                    act.wait_ge(turn_mm, n + 1)
                    act.activation(chosenT[:, n // 2, (n % 2) * HALF:(n % 2 + 1) * HALF], turn_ps[n % 2][:], ACT.Copy).then_inc(turned, 1)

            @block.gpsimd
            def _(pool):
                pool.wait_ge(const_in, 32)
                with pool.Fori(0, TURNS) as i:
                    for s in range(2):
                        h = 2 * i + s
                        pool.wait_ge(place_ready, h + 3)
                        for part in range(2):
                            pool.tensor_tensor(hot_part(s, part), placef[s][:].rearrange("p t k -> p (t k)")[
                                :, part * HOT:(part + 1) * HOT].unsqueeze(2).to_broadcast([P, HOT, PAIRS]),
                                pair_iota[:].unsqueeze(1).to_broadcast([P, HOT, PAIRS]), ALU.subtract).then_inc(offset_ready, 1)
                        for part in range(2):
                            pool.wait_ge(hot_made, 2 * h + part + 1)
                            hot4 = hot_part(s, part).rearrange("p (t k) n -> p t k n", t=TT // 2)
                            pool.tensor_tensor(hot4, hot4, pair_id[s][:, part * TT // 2:(part + 1) * TT // 2].unsqueeze(2).to_broadcast(
                                [P, TT // 2, TOPK, PAIRS]), ALU.mult).then_inc(hot_ready, 1)

            @block.vector
            def _(dve):
                for s in range(2):
                    dve.memset(keys[s][:], 0.0).then_inc(keys_zero, 1)
                dve.memset(one[:], 1.0).then_inc(one_set, 1)
                dve.sem_inc(place_ready, 2)

                def two_rounds(own, lists, cell):
                    def passes(make):
                        nonlocal cell
                        own.of(dve.memset(waits[:, cell:cell + 1], 0.0))
                        cell += 1
                        for values, out, place in lists:
                            own.of(make(values, out, place))
                        own.wait()

                    for lo in (0, 8):
                        if lo:
                            passes(lambda values, out, place: dve.match_replace(values, out[:, 0:8], values, FINFO_MIN))
                        passes(lambda values, out, place: dve.max(out[:, lo:lo + 8], values))
                        passes(lambda values, out, place: dve.max_index(place[:, lo:lo + 8], out[:, lo:lo + 8], values))

                def select(h, s, own):
                    dve.wait_ge(score_ready, h + 2)
                    two_rounds(own, [(score[s][:, t, a, :], top[s][:, t, a, :], index[s][:, t, a, :])
                                     for t in range(TT) for a in range(2)], 0)
                    own.of(dve.tensor_copy(indexf[s][:], index[s][:]))
                    own.wait()
                    own.of(dve.tensor_scalar(indexf[s][:, :, 0, :], indexf[s][:, :, 0, :], float(NK), None, ALU.mult))
                    own.wait()
                    for out, src in ((pair[s], top[s]), (pair_id[s], indexf[s])):
                        at = 0
                        for a0, a1, nb in PAIR_ROWS:
                            na = a1 - a0
                            own.of(dve.tensor_tensor(out[:, :, at:at + na * nb].rearrange("p t (a b) -> p t a b", a=na),
                                                     src[:, :, 0, a0:a1].unsqueeze(3).to_broadcast([P, TT, na, nb]),
                                                     src[:, :, 1, 0:nb].unsqueeze(2).to_broadcast([P, TT, na, nb]), ALU.add))
                            at += na * nb
                    own.wait()
                    two_rounds(own, [(pair[s][:, t, :], best[s][:, t, :], place[s][:, t, :]) for t in range(TT)], 5)
                    own.of(dve.tensor_copy(placef[s][:], place[s][:]))
                    own.of(dve.tensor_copy(total[s][:], best[s][:, :, 0:1].rearrange("p t a -> p (t a)")))
                    own.wait()
                    dve.tensor_tensor(best[s][:], best[s][:], total[s][:].unsqueeze(2).to_broadcast([P, TT, TOPK]),
                                      ALU.subtract).then_inc(place_ready, 1)

                def collect(h, s, own):
                    dve.wait_ge(gate_exp, h + 1)
                    own.of(dve.reduce_sum(total[s][:], best[s][:], AX.X))
                    own.wait()
                    own.of(dve.reciprocal(total[s][:], total[s][:]))
                    own.wait()
                    own.of(dve.tensor_tensor(chosen[:, 2, :, bass.ds(h, 1), :].rearrange("p t a k -> p t (a k)"), best[s][:],
                                             total[s][:].unsqueeze(2).to_broadcast([P, TT, TOPK]), ALU.mult))
                    dve.wait_ge(hot_ready, 2 * h + 2)
                    own.of(dve.reduce_sum(placef[s][:].rearrange("p t k -> p (t k)"), hot[s][:], AX.X))
                    own.wait()
                    own.of(dve.tensor_copy(expert[s][:], placef[s][:]))
                    own.wait()
                    own.of(dve.tensor_scalar(split[s][:], expert[s][:], 7, None, ALU.arith_shift_right))
                    own.of(dve.tensor_scalar(expert[s][:], expert[s][:], NK - 1, None, ALU.bitwise_and))
                    own.wait()
                    own.of(dve.tensor_copy(chosen[:, 0, :, bass.ds(h, 1), :].rearrange("p t a k -> p t (a k)"), split[s][:]))
                    own.of(dve.tensor_copy(chosen[:, 1, :, bass.ds(h, 1), :].rearrange("p t a k -> p t (a k)"), expert[s][:]))
                    own.wait()
                    dve.sem_inc(head_done, 1)

                SELECT, COLLECT = 5 * 2 * TT + 5 + 2 + 2 * len(PAIR_ROWS) + 5 * TT + 5 + 2, 9

                def step(h, s):
                    own = Steps(dve, dve_step, h * SELECT + (h - 1) * COLLECT)
                    select(h, s, own)
                    assert own.n == SELECT, own.n
                    collect(h - 1, 1 - s, own)
                    assert own.n == SELECT + COLLECT, own.n - SELECT

                select(0, 0, Steps(dve, dve_step))
                with dve.Fori(0, TURNS - 1) as i:
                    for s in range(2):
                        step(2 * i + s + 1, 1 - s)
                step(PH - 1, 1)
                collect(PH - 1, 1, Steps(dve, dve_step, PH * SELECT + (PH - 1) * COLLECT))


def stage_peer_gates(nc, d):
    TOK = 4
    UN = 2
    NBANK = 4
    SHARED = (1, 3)
    INNER = P // (TOK * NBANK)
    with ExitStack() as stack:
        sp = Space(nc, stack, "gt")
        chosenT = sp.sb("chosenT", [P, 3, S])
        iota = sp.sb("iota", [P, NK])
        row_hot = [sp.sb(f"row_hot{b}", [P, TOK, NK]) for b in range(NBANK)]
        distance = {b: sp.sb(f"distance{b}", [P, TOK, NK]) for b in SHARED}
        square = {b: sp.sb(f"square{b}", [P, TOK, NK]) for b in SHARED}
        one = sp.sb("one", [P, 1])
        col_hot = [sp.sb(f"col_hot{b}", [P, TOK, NK]) for b in range(NBANK)]
        gates = [sp.sb(f"gates{s}", [P, NK, P]) for s in range(2)]
        gate_ps = [sp.ps(f"gate_ps{b}", [P, TOK, NK]) for b in range(NBANK)]
        const_in = sp.sem("const_in")
        one_set = sp.sem("one_set")
        distance_ready = sp.sem("distance_ready")
        square_ready = {b: sp.sem(f"square_ready{b}") for b in SHARED}
        row_ready = {b: sp.sem(f"row_ready{b}") for b in SHARED}
        hot_ready = [sp.sem(f"hot_ready{b}") for b in range(NBANK)]
        gates_mm = [sp.sem(f"gates_mm{b}") for b in range(NBANK)]
        gates_taken = [sp.sem(f"gates_taken{b}") for b in range(NBANK)]
        stored = [sp.sem(f"stored{s}") for s in range(2)]
        TURNS = TT // 2
        with nc.Block() as block:
            @block.sync
            def _(sync):
                sync.dma_start(chosenT[:], d["chosenT"].rearrange("a p n -> p a n")).then_inc(const_in, 16)
                sync.dma_start(iota[:], d["iota"].partition_broadcast(P)).then_inc(const_in, 16)
                for s in range(2):
                    sync.sem_inc(stored[s], 16)
                with sync.Fori(0, TURNS) as i:
                    for s in range(2):
                        for b in range(NBANK):
                            sync.wait_ge(gates_taken[b], (2 * i + s) * INNER + INNER + 1)
                        sync.dma_start(d["gates"][:, :, bass.ds((2 * i + s) * P, P)], gates[s][:]).then_inc(stored[s], 16)
                for s in range(2):
                    sync.wait_ge(stored[s], (TURNS + 1) * 16)

            @block.vector
            def _(dve):
                dve.memset(one[:], 1.0).then_inc(one_set, 1)
                dve.wait_ge(const_in, 32)
                for b in range(NBANK):
                    dve.sem_inc(gates_mm[b], 1)
                with dve.Fori(0, TT * INNER) as j:
                    for b in range(NBANK):
                        dve.wait_ge(gates_mm[b], j + 1)
                        if b not in SHARED:
                            dve.tensor_tensor(row_hot[b][:], iota[:].unsqueeze(1).to_broadcast([P, TOK, NK]),
                                              chosenT[:, 0, bass.ds(j * TOK * NBANK + b * TOK, TOK)].unsqueeze(2).to_broadcast([P, TOK, NK]), ALU.is_equal)
                        for t in range(TOK):
                            tok = bass.ds(j * TOK * NBANK + b * TOK + t, 1)
                            ins = dve.tensor_scalar(col_hot[b][:, t, :], iota[:], chosenT[:, 1, tok], chosenT[:, 2, tok],
                                                    ALU.is_equal, ALU.mult)
                        ins.then_inc(hot_ready[b], 1)

            @block.gpsimd
            def _(pool):
                pool.wait_ge(const_in, 32)
                for b in SHARED:
                    pool.sem_inc(square_ready[b], 1)
                with pool.Fori(0, TT * INNER) as j:
                    for n, b in enumerate(SHARED):
                        pool.wait_ge(square_ready[b], j + 1)
                        pool.tensor_tensor(distance[b][:], iota[:].unsqueeze(1).to_broadcast([P, TOK, NK]),
                                           chosenT[:, 0, bass.ds(j * TOK * NBANK + b * TOK, TOK)].unsqueeze(2).to_broadcast([P, TOK, NK]),
                                           ALU.subtract).then_inc(distance_ready, 1)
                        pool.wait_ge(distance_ready, j * len(SHARED) + n + 1)
                        pool.wait_ge(row_ready[b], j + 1)
                        pool.tensor_tensor(square[b][:], distance[b][:], distance[b][:], ALU.mult).then_inc(square_ready[b], 1)

            @block.tensor
            def _(pe):
                with pe.Fori(0, TT * INNER) as j:
                    for b in range(NBANK):
                        pe.wait_ge(hot_ready[b], j + 1)
                        if b in SHARED:
                            pe.wait_ge(row_ready[b], j + 2)
                        pe.wait_ge(gates_taken[b], j + 1)
                        for t in range(TOK):
                            mm = pe.matmul(gate_ps[b][:, t, :], row_hot[b][:, t, :], col_hot[b][:, t, :], start=True, stop=True)
                        mm.then_inc(gates_mm[b], 1)

            @block.scalar
            def _(act):
                for b in range(NBANK):
                    act.sem_inc(gates_taken[b], 1)
                for b in SHARED:
                    act.sem_inc(row_ready[b], 1)
                act.wait_ge(one_set, 1)
                with act.Fori(0, TURNS) as i:
                    for s in range(2):
                        act.wait_ge(stored[s], i * 16 + 16)
                        with act.Fori(0, INNER) as j:
                            for b in SHARED:
                                act.wait_ge(square_ready[b], (2 * i + s) * INNER + j + 2)
                                act.wait_ge(gates_mm[b], (2 * i + s) * INNER + j + 1)
                                act.activation(row_hot[b][:], square[b][:], ACT.Relu, bias=one[:], scale=-1.0).then_inc(row_ready[b], 1)
                            for b in range(NBANK):
                                act.wait_ge(gates_mm[b], (2 * i + s) * INNER + j + 2)
                                act.activation(gates[s][:, :, bass.ds(j * TOK * NBANK + b * TOK, TOK)],
                                               gate_ps[b][:].rearrange("p t n -> p n t"), ACT.Copy).then_inc(gates_taken[b], 1)


def stage_peer_mix(nc, d, acc):
    NJ = 4
    TURNS = NK // NJ
    with ExitStack() as stack:
        sp = Space(nc, stack, "px")
        u_raw = [sp.sb(f"u_raw{r}", [P, KD, P]) for r in range(2)]
        u = [[sp.sb(f"u{r}_{p}", [P, KD, P], F32R) for p in ("hi", "lo")] for r in range(2)]
        v_raw = sp.sb("v_raw", [P, D])
        v = [[sp.sb(f"v{j}_{p}", [P, D], F32R) for p in ("hi", "lo")] for j in range(NJ)]
        gate = [sp.sb(f"gate{r}", [P, S]) for r in range(2)]
        hidden = [sp.sb(f"hidden{r}", [P, S]) for r in range(2)]
        weight = [[sp.sb(f"weight{j}_{p}", [P, S], F32R) for p in ("hi", "lo")] for j in range(NJ)]
        hid_ps = [sp.ps(f"hid_ps{r}", [P, S]) for r in range(2)]
        NOUT = 4
        out_ps = [sp.ps(f"out_ps{b}", [P, HALF]) for b in range(NOUT)]
        n2_hi = sp.sem("n2_hi")
        n2_lo = sp.sem("n2_lo")
        zeroed = sp.sem("zeroed")
        u_in = [sp.sem(f"u_in{r}") for r in range(2)]
        u_hi = [sp.sem(f"u_hi{r}") for r in range(2)]
        u_lo = [sp.sem(f"u_lo{r}") for r in range(2)]
        gate_in = [sp.sem(f"gate_in{r}") for r in range(2)]
        hid_mm = [sp.sem(f"hid_mm{r}") for r in range(2)]
        gelu_done = [sp.sem(f"gelu_done{r}") for r in range(2)]
        gated = [sp.sem(f"gated{r}") for r in range(2)]
        weight_hi = sp.sem("weight_hi")
        weight_lo = sp.sem("weight_lo")
        v_in = sp.sem("v_in")
        v_hi = sp.sem("v_hi")
        v_lo = sp.sem("v_lo")
        out_mm = [sp.sem(f"out_mm{b}") for b in range(NOUT)]
        out_taken = [sp.sem(f"out_taken{b}") for b in range(NOUT)]
        eps = sp.sb("eps", [P, 1])
        ss = sp.sb("ss", [P, TT])
        rstd = sp.sb("rstd", [P, TT])
        with ExitStack() as first:
            n2 = [first.enter_context(nc.sbuf_tensor(f"px_n2_{part}", [P, KD, S], F32R)) for part in ("hi", "lo")]
        h = sp.sb("h", [P, TT, D])
        g2, norm_w, squares = (sp.sb(name, [P, D])[:] for name in ("g2", "norm_w", "squares"))
        eps_in = sp.sem("eps_in")
        rows_in = sp.sem("rows_in")
        h_in = sp.sem("h_in")
        norm_step = sp.sem("norm_step")
        h_ready = sp.sem("h_ready")
        ss_step = sp.sem("ss_step")
        out_ready = sp.sem("out_ready")
        stored = sp.sem("stored")
        TILES = 2 * TT
        USES = TILES // NOUT
        LAST = (TILES - 1) % NOUT
        PER = NJ // 2

        with nc.Block() as block:
            @block.sync
            def _(sync):
                def load(e, r, before):
                    if before is not None:
                        sync.wait_ge(u_lo[r], before)
                    sync.dma_start(u_raw[r][:], d["uT"][e]).then_inc(u_in[r], 16)
                    if before is not None:
                        sync.wait_ge(gated[r], before)
                    sync.dma_start(gate[r][:], d["gates"][:, bass.ds(e, 1), :].rearrange("p a n -> p (a n)")).then_inc(gate_in[r], 16)

                def load_v(e):
                    if not (isinstance(e, int) and e == 0):
                        sync.wait_ge(v_lo, e)
                    sync.dma_start(v_raw[:], d["v_experts"][:, bass.ds(e, 1), :].rearrange("p a n -> p (a n)")).then_inc(v_in, 16)

                load(0, 0, None)
                load(1, 1, None)
                load_v(0)
                with sync.Fori(1, NK // 2) as m:
                    for r in range(2):
                        load(2 * m + r, r, m)
                        load_v(2 * m - 1 + r)
                load_v(NK - 1)
                sync.dma_start(eps[:], d["eps"][0].rearrange("(p a) -> p a", a=1)).then_inc(eps_in, 16)
                for r in range(2):
                    sync.wait_ge(hid_mm[r], TURNS * PER)
                sync.dma_start(g2, d["rows"][5].partition_broadcast(P)).then_inc(rows_in, 16)
                sync.dma_start(norm_w, d["final_norm_w"].partition_broadcast(P)).then_inc(rows_in, 16)
                sync.dma_start(h[:], d["h"].rearrange("t p n -> p t n")).then_inc(h_in, 16)
                for t in range(TT):
                    sync.wait_ge(out_ready, t + 1)
                    sync.dma_start(d["out"][t * P:(t + 1) * P, :], h[:, t, :]).then_inc(stored, 16)
                sync.wait_ge(stored, 16 * TT)

            @block.tensor
            def _(pe):
                with pe.Fori(0, TURNS) as i:
                    for j in range(NJ):
                        r, m = j % 2, i * PER + j // 2
                        pe.wait_ge(u_lo[r], m + 1)
                        pe.wait_ge(gelu_done[r], m + 1)
                        for c in range(2):
                            for k in range(KD):
                                if j == 0 and c == 0:
                                    pe.wait_ge(n2_lo, k + 1)
                                for a, b in PARTS:
                                    mm = pe.matmul(hid_ps[r][:, c * HALF:(c + 1) * HALF], u[r][a][:, k, :],
                                                   n2[b][:, k, c * HALF:(c + 1) * HALF],
                                                   start=(k == 0 and a + b == 0), stop=(k == KD - 1 and a == 1))
                        mm.then_inc(hid_mm[r], 1)
                    for b0 in range(0, TILES, NOUT):
                        for js in (range(NJ - 1), range(NJ - 1, NJ)):
                            for b in range(NOUT):
                                t, c = divmod(b0 + b, 2)
                                if js[0] == 0:
                                    pe.wait_ge(out_taken[b], i * USES + b0 // NOUT + 1)
                                for j in js:
                                    if b0 == 0 and b == 0:
                                        pe.wait_ge(weight_lo, i * NJ + j + 1)
                                        pe.wait_ge(v_lo, i * NJ + j + 1)
                                    for wp, vp in PARTS:
                                        mm = pe.matmul(out_ps[b][:], weight[j][wp][:, t * P:(t + 1) * P], v[j][vp][:, c * HALF:(c + 1) * HALF],
                                                       start=(j == 0 and wp + vp == 0), stop=(j == NJ - 1 and wp == 1))
                                if js[-1] == NJ - 1:
                                    mm.then_inc(out_mm[b], 1)

            @block.scalar
            def _(act):
                for k in range(KD):
                    act.activation(n2[0][:, k, :], acc[:, k, :], ACT.Copy).then_inc(n2_hi, 1)
                    if k in (2, 4):
                        r = k // 2 - 1
                        act.wait_ge(u_in[r], 16)
                        act.activation(u[r][0][:], u_raw[r][:], ACT.Copy).then_inc(u_hi[r], 1)
                        act.sem_inc(gelu_done[r], 1)

                def turn(i, last):
                    for j in range(NJ):
                        r, m = j % 2, i * PER + j // 2
                        act.wait_ge(hid_mm[r], m + 1)
                        act.wait_ge(weight_lo, i * NJ + j) if j >= 2 else act.wait_ge(zeroed, 1)
                        act.activation(hidden[r][:], hid_ps[r][:], ACT.Gelu).then_inc(gelu_done[r], 1)
                        if not (last and j >= NJ - 2):
                            act.wait_ge(u_in[r], m * 16 + 32)
                            act.activation(u[r][0][:], u_raw[r][:], ACT.Copy).then_inc(u_hi[r], 1)
                        act.wait_ge(gated[r], m + 1)
                        act.activation(weight[j][0][:], hidden[r][:], ACT.Copy).then_inc(weight_hi, 1)
                        act.wait_ge(v_in, (i * NJ + j) * 16 + 16)
                        act.activation(v[j][0][:], v_raw[:], ACT.Copy).then_inc(v_hi, 1)

                with act.Fori(0, TURNS - 1) as i:
                    turn(i, False)
                turn(TURNS - 1, True)
                act.wait_ge(eps_in, 16)
                for t in range(TT):
                    act.wait_ge(h_ready, t + 1)
                    act.activation(squares, h[:, t, :], ACT.Square, accum_out=ss[:, t:t + 1]).then_inc(ss_step, 1)
                    act.wait_ge(ss_step, 2 * t + 1)
                    act.activation(ss[:, t:t + 1], ss[:, t:t + 1], ACT.Sqrt, bias=eps[:]).then_inc(ss_step, 1)

            @block.vector
            def _(dve):
                for k in range(KD):
                    dve.wait_ge(n2_hi, k + 1)
                    dve.tensor_tensor(n2[1][:, k, :], acc[:, k, :], n2[0][:, k, :].bitcast(F32), ALU.subtract).then_inc(n2_lo, 1)
                    if k in (2, 4):
                        r = k // 2 - 1
                        dve.wait_ge(u_hi[r], 1)
                        dve.tensor_tensor(u[r][1][:], u_raw[r][:], u[r][0][:].bitcast(F32), ALU.subtract).then_inc(u_lo[r], 1)
                dve.wait_ge(n2_lo, KD)
                dve.memset(acc[:], 0.0).then_inc(zeroed, 1)
                dve.wait_ge(zeroed, 1)
                for b in range(NOUT):
                    dve.sem_inc(out_taken[b], 1)

                def turn(i, last):
                    for j in range(NJ):
                        r, m = j % 2, i * PER + j // 2
                        dve.wait_ge(gelu_done[r], m + 2)
                        dve.wait_ge(gate_in[r], m * 16 + 16)
                        dve.tensor_tensor(hidden[r][:], hidden[r][:], gate[r][:], ALU.mult).then_inc(gated[r], 1)
                        if not (last and j >= NJ - 2):
                            dve.wait_ge(u_hi[r], m + 2)
                            dve.tensor_tensor(u[r][1][:], u_raw[r][:], u[r][0][:].bitcast(F32), ALU.subtract).then_inc(u_lo[r], 1)
                        dve.wait_ge(weight_hi, i * NJ + j + 1)
                        dve.tensor_tensor(weight[j][1][:], hidden[r][:], weight[j][0][:].bitcast(F32), ALU.subtract).then_inc(weight_lo, 1)
                        dve.wait_ge(v_hi, i * NJ + j + 1)
                        dve.tensor_tensor(v[j][1][:], v_raw[:], v[j][0][:].bitcast(F32), ALU.subtract).then_inc(v_lo, 1)
                    for n in range(TILES):
                        t, c = divmod(n, 2)
                        b = n % NOUT
                        dve.wait_ge(out_mm[b], i * USES + n // NOUT + 1)
                        part = acc[:, t, c * HALF:(c + 1) * HALF]
                        dve.tensor_tensor(part, part, out_ps[b][:], ALU.add).then_inc(out_taken[b], 1)
                        if last and c == 1:
                            if t == 0:
                                scale_norm_w()
                            residual(t)
                            if t >= 1:
                                normalise(t - 1)
                    if last:
                        normalise(TT - 1)

                own = Steps(dve, norm_step)

                def scale_norm_w():
                    dve.wait_ge(rows_in, 32)
                    own.of(dve.tensor_scalar(norm_w, norm_w, math.sqrt(D), None, ALU.mult))
                    dve.wait_ge(h_in, 16)

                def residual(t):
                    for c in range(2):
                        dve.wait_ge(out_taken[(2 * t + c) % NOUT], TURNS * USES - USES + (2 * t + c) // NOUT + 2)
                    own.of(dve.tensor_tensor(acc[:, t, :], acc[:, t, :], g2, ALU.mult))
                    own.wait()
                    dve.tensor_tensor(h[:, t, :], h[:, t, :], acc[:, t, :], ALU.add).then_inc(h_ready, 1)

                def normalise(t):
                    dve.wait_ge(ss_step, 2 * t + 2)
                    own.of(dve.reciprocal(rstd[:, t:t + 1], ss[:, t:t + 1]))
                    own.wait()
                    dve.scalar_tensor_tensor(h[:, t, :], h[:, t, :], rstd[:, t:t + 1], norm_w, ALU.mult, ALU.mult).then_inc(out_ready, 1)

                with dve.Fori(0, TURNS - 1) as i:
                    turn(i, False)
                turn(TURNS - 1, True)


OFF_XBC, OFF_DT = DI, DI + CONV_TILES * P
OFF_Q = OFF_DT + SH
OFF_V = OFF_Q + 2 * D
OFF_END = OFF_V + D + 2 * D


def layouts(a):
    c = np.ascontiguousarray
    w_in = a["w_in"][0]
    ch = np.concatenate([w_in[:, OFF_Q:OFF_V], w_in[:, OFF_V + D:OFF_END], w_in[:, OFF_XBC:OFF_DT]], axis=1)
    conv = np.concatenate([a["conv_w"][0], a["conv_b"]], axis=0)
    out = {
        "x": a["x"][0], "cT": c(a["c"].reshape(KD, P).T), "ada_w": a["ada_w"][0], "ada_b": a["ada_b"],
        "norm1_w": a["norm1_w"], "norm2_w": a["norm2_w"],
        "w_ch": c(ch.reshape(KD, P, -1, P).transpose(2, 1, 0, 3)),
        "conv_w": c(conv.reshape(5, CONV_TILES, P).transpose(2, 1, 0)),
        "w_tok": c(np.concatenate([w_in[:, :DI], w_in[:, OFF_V:OFF_V + D]], axis=1)),
        "w_dt": c(w_in[:, OFF_DT:OFF_Q]), "dt_bias": a["dt_bias"][0],
        "ident": np.eye(P, dtype=np.float32),
        "eps": np.tile(np.array([[D], [GW], [P]], np.float32) * np.float32(EPS), (1, P)),
    }
    b, n = np.arange(NB), np.arange(P)
    out |= {
        "pos": a["positions"][0], "pos_q": c(a["positions"][0].reshape(-1, 4).T), "rel_bias": a["rel_bias"],
        "first": np.tile(np.where(b == 0, -2.0 ** 30, bucket_starts()).astype(np.float32), 4),
        "causal": np.where(n[None, :] <= n[:, None], 0, -1e30).astype(np.float32),
        "attn_norm_w": a["attn_norm_w"][0],
        "w_pq": c(a["peer_wq"][0].reshape(KD, P, PH, P).transpose(2, 1, 0, 3)),
        "key1T": c(a["peer_key1"][0].transpose(0, 2, 1)), "key2T": c(a["peer_key2"][0].transpose(0, 2, 1)),
        "iota": np.arange(NK, dtype=np.float32),
        "uT": c(a["peer_u"][0].reshape(NK, NK, KD, P).transpose(1, 3, 2, 0)),
        "v_experts": a["peer_v"][0].reshape(NK, NK, D), "final_norm_w": a["final_norm_w"],
        "w_branch": c(np.concatenate([a["w_ssd_o"][0], a["w_attn_o"][0]]).reshape(-1, P, KD, P).transpose(2, 1, 0, 3)), "w_out": a["w_out"][0],
        "upto": (n[:, None] <= n[None, :]).astype(np.float32), "after": (n[:, None] > n[None, :]).astype(np.float32),
        "ssd_norm_w": c(a["ssd_norm_w"][0].reshape(-1, P).T), "d_skip": a["d_skip"][0], "a_log": a["a_log"][0],
        "lambdas": np.stack([a["lambda_q1"][0], a["lambda_k1"][0], a["lambda_q2"][0], a["lambda_k2"][0]]),
    }
    return out


_SCRATCH = {
    "rows": (6, D), "qkT": (2 * AH, P, S), "xbcT": (CONV_TILES, P, S), "z": (TT, P, DI), "v": (TT, P, D),
    "gateT": (2 * KD, P, S), "dt": (TT, P, SH), "bias": (S, AH, S), "ynT": (DI // P, P, S), "attT": (KD, P, S),
    "h": (TT, P, D), "chosenT": (3, P, S), "gates": (NK, NK, S),
}


def hybrid_block(nc, d):
    stage_modulation_and_bias(nc, d)
    stage_project(nc, d)
    stage_ssd(nc, d)
    stage_attention(nc, d)
    with ExitStack() as stack:
        held = Space(nc, stack, "held").sb("tiles", [P, KD, S])
        stage_merge(nc, d, held)
        stage_peer_topk(nc, d, held)
        stage_peer_gates(nc, d)
        stage_peer_mix(nc, d, held)


def kernel(**inputs):
    import concourse.bacc as _bacc
    from concourse.bass_utils import run_bass_kernel_spmd as _run

    nc = _bacc.Bacc("TRN2", target_bir_lowering=False, num_devices=1)
    arrays, d = {}, {}
    for name, a in layouts({k: np.asarray(v) for k, v in inputs.items()}).items():
        a = np.ascontiguousarray(a)
        arrays[f"in_{name}"] = a
        d[name] = nc.dram_tensor(f"in_{name}", a.shape, mybir.dt.from_np(a.dtype), kind="ExternalInput").ap()
    for name, shape in _SCRATCH.items():
        d[name] = nc.dram_tensor(f"scratch_{name}", shape, F32, kind="Internal").ap()
    out = nc.dram_tensor("out_0", (S, D), F32, kind="ExternalOutput").ap()
    d["out"] = out
    hybrid_block(nc, d)
    r = _run(nc, [arrays], core_ids=[0])
    return r.results[0]["out_0"].reshape(1, S, D)
```
